# Optimizing a Trainium2 kernel written in Bass

```python
import math
import jax, jax.numpy as jnp
from jax import lax
import numpy as np

D_MODEL = 1024
BATCH = 1
SEQ = 256
DEPTH = 2
DEC_BATCH = 1
DEC_SEQ = 512
PAST_LEN = 128

GRID_W = 64
N_MIXERS = 2
N_RET_LAYERS = (DEPTH + 1) // 2
N_NA_LAYERS = DEPTH // 2
RET_HEADS = 4
RET_QK_DIM = D_MODEL // RET_HEADS
RET_V_DIM = 2 * D_MODEL // RET_HEADS
RET_CHUNK = 128
ROPE_THETA = 10000.0
NA_HEADS = 16
NA_HEAD_DIM = D_MODEL // NA_HEADS
NA_MAX_ROWS = 8
NA_WIN_COLS = 16
NA_Q_COLS = 16
NA_BAND_COLS = 32
N_EXPERTS = 16
EC_CAPACITY = 2
D_FF_EXPERT = D_MODEL
PLE_DIM = 256
NORM_EPS = 1e-6

kernel_name = "hybrid_retention_natten_ec_encoder"

F32 = jnp.float32

def rms_norm(x, g):
    xf = x.astype(F32)
    y = xf * lax.rsqrt(jnp.mean(xf * xf, axis=-1, keepdims=True) + NORM_EPS)
    return (y * g.astype(F32)).astype(x.dtype)

def rope(x):
    S, d = x.shape[-2], x.shape[-1]
    inv = ROPE_THETA ** (-jnp.arange(0, d, 2, dtype=F32) / d)
    ang = jnp.arange(S, dtype=F32)[:, None] * inv[None, :]
    cos, sin = jnp.cos(ang), jnp.sin(ang)
    xf = x.astype(F32)
    x1, x2 = xf[..., : d // 2], xf[..., d // 2:]
    return jnp.concatenate([x1 * cos - x2 * sin, x1 * sin + x2 * cos], axis=-1).astype(x.dtype)

def causal_retention_chunks(q, k, v, log_g, strict):
    B, H, S, dk = q.shape
    dv = v.shape[-1]
    C = RET_CHUNK
    NC = S // C

    def chunks(t):
        return jnp.moveaxis(t.reshape(B, H, NC, C, t.shape[-1]), 2, 0)

    pos = jnp.arange(C, dtype=F32)
    diff = pos[:, None] - pos[None, :]
    mask = (diff > 0) if strict else (diff >= 0)
    decay = jnp.where(mask, jnp.exp(jnp.where(mask, diff, 0.0)[None] * log_g[:, None, None]), 0.0)
    q_decay = jnp.exp((pos + 1.0)[None, :] * log_g[:, None])[:, :, None]
    k_decay = jnp.exp((C - 1.0 - pos)[None, :] * log_g[:, None])[:, :, None]
    chunk_decay = jnp.exp(C * log_g)[:, None, None]

    def step(state, qkv):
        qc, kc, vc = qkv
        scores = jnp.einsum('bhid,bhjd->bhij', qc, kc) * decay
        inner = jnp.einsum('bhij,bhjv->bhiv', scores, vc)
        cross = jnp.einsum('bhid,bhdv->bhiv', qc * q_decay, state)
        new_state = state * chunk_decay + jnp.einsum('bhjd,bhjv->bhdv', kc * k_decay, vc)
        return new_state, inner + cross

    state0 = jnp.zeros((B, H, dk, dv), F32)
    _, out = lax.scan(step, state0, (chunks(q), chunks(k), chunks(v)))
    return jnp.moveaxis(out, 0, 2).reshape(B, H, S, dv)

def retention_mixer(h, w_in, decay_logit, gn_w, w_out):
    B, S, _ = h.shape
    proj = h @ w_in
    q, k, v, g = jnp.split(proj, [D_MODEL, 2 * D_MODEL, 4 * D_MODEL], axis=-1)

    def heads(t, d):
        return t.reshape(B, S, RET_HEADS, d).transpose(0, 2, 1, 3)

    q = rope(heads(q, RET_QK_DIM)).astype(F32)
    k = rope(heads(k, RET_QK_DIM)).astype(F32) * (RET_QK_DIM ** -0.5)
    v = heads(v, RET_V_DIM).astype(F32)
    log_g = jax.nn.log_sigmoid(decay_logit.astype(F32))
    fwd = causal_retention_chunks(q, k, v, log_g[0], False)

    def flip(t):
        return jnp.flip(t, axis=2)

    bwd = flip(causal_retention_chunks(flip(q), flip(k), flip(v), log_g[1], True))
    o = fwd + bwd
    mu = jnp.mean(o, axis=-1, keepdims=True)
    var = jnp.mean(jnp.square(o - mu), axis=-1, keepdims=True)
    o = (o - mu) * lax.rsqrt(var + NORM_EPS)
    o = o.transpose(0, 2, 1, 3).reshape(B, S, 2 * D_MODEL) * gn_w.astype(F32)
    out = (jax.nn.silu(g.astype(F32)) * o).astype(h.dtype)
    return out @ w_out

def neighbourhood_attention(h, w_in, rpb, w_out):
    B, S, _ = h.shape
    rows = S // GRID_W
    kr = min(NA_MAX_ROWS, rows)
    qkv = (h @ w_in).reshape(B, rows, GRID_W, 3, NA_HEADS, NA_HEAD_DIM).transpose(3, 0, 4, 1, 2, 5)
    q = qkv[0] * (NA_HEAD_DIM ** -0.5)
    k, v = qkv[1], qkv[2]

    n_cb = GRID_W // NA_Q_COLS
    c0 = np.arange(n_cb) * NA_Q_COLS
    band_start = np.clip(c0 - NA_WIN_COLS // 2, 0, GRID_W - NA_BAND_COLS)
    band_cols = band_start[:, None] + np.arange(NA_BAND_COLS)
    q_cols = c0[:, None] + np.arange(NA_Q_COLS)
    win_start = np.clip(q_cols - NA_WIN_COLS // 2, 0, GRID_W - NA_WIN_COLS)
    kcol = band_cols[:, None, :]
    col_valid = (kcol >= win_start[..., None]) & (kcol < win_start[..., None] + NA_WIN_COLS)
    dc_idx = np.clip(kcol - q_cols[..., None] + NA_WIN_COLS - 1, 0, 2 * NA_WIN_COLS - 2)
    mask_add = jnp.where(jnp.asarray(col_valid), 0.0, -1e30).astype(F32)[:, :, None, :]
    rpb_cols = rpb[:, :, dc_idx]

    def row_block(r):
        rs = jnp.clip(r - kr // 2, 0, rows - kr)
        k_rows = lax.dynamic_slice_in_dim(k, rs, kr, axis=2)[:, :, :, band_cols]
        v_rows = lax.dynamic_slice_in_dim(v, rs, kr, axis=2)[:, :, :, band_cols]
        q_r = lax.dynamic_index_in_dim(q, r, axis=2, keepdims=False).reshape(B, NA_HEADS, n_cb, NA_Q_COLS, NA_HEAD_DIM)
        dr_idx = rs + jnp.arange(kr) - r + NA_MAX_ROWS - 1
        bias = jnp.take(rpb_cols, dr_idx, axis=1).transpose(0, 2, 3, 1, 4).astype(F32) + mask_add
        s = jnp.einsum('bhnid,bhanjd->bhniaj', q_r, k_rows).astype(F32) + bias
        p = jax.nn.softmax(s.reshape(B, NA_HEADS, n_cb, NA_Q_COLS, kr * NA_BAND_COLS), axis=-1)
        p = p.reshape(s.shape).astype(v.dtype)
        o = jnp.einsum('bhniaj,bhanjd->bhnid', p, v_rows)
        return o.reshape(B, NA_HEADS, GRID_W, NA_HEAD_DIM)

    out = lax.map(row_block, jnp.arange(rows))
    out = out.transpose(1, 0, 3, 2, 4).reshape(B, S, D_MODEL)
    return out @ w_out

def expert_choice_moe(h, router_w, w_gate, w_up, w_down):
    B, S, D = h.shape
    n_tok = B * S
    cap = EC_CAPACITY * n_tok // N_EXPERTS
    xt = h.reshape(n_tok, D)
    aff = jax.nn.softmax((xt @ router_w).astype(F32), axis=-1)
    gates, idx = lax.top_k(aff.T, cap)
    xe = xt[idx]
    hid = jax.nn.silu(jnp.einsum('ecd,edf->ecf', xe, w_gate)) * jnp.einsum('ecd,edf->ecf', xe, w_up)
    ye = jnp.einsum('ecf,efd->ecd', hid, w_down) * gates[..., None].astype(h.dtype)
    y = jnp.zeros((n_tok, D), h.dtype).at[idx.reshape(-1)].add(ye.reshape(-1, D))
    return y.reshape(B, S, D)

def per_layer_embedding(h, p_i, norm_g, w_up, w_gate):
    gate = jax.nn.sigmoid((rms_norm(h, norm_g) @ w_gate).astype(F32))
    return ((p_i @ w_up).astype(F32) * gate).astype(h.dtype)

def trunk(x, p, ret_w_in, ret_decay_logit, ret_gn_w, ret_w_out, na_w_in, na_rpb, na_w_out,
          mix_norm, ffn_norm, ple_norm, router_w, exp_w_gate, exp_w_up, exp_w_down,
          ple_w_up, ple_w_gate, final_norm):
    h = x
    for i in range(DEPTH):
        hn = rms_norm(h, mix_norm[i])
        j = i // N_MIXERS
        if i % N_MIXERS == 0:
            h = h + retention_mixer(hn, ret_w_in[j], ret_decay_logit[j], ret_gn_w[j], ret_w_out[j])
        else:
            h = h + neighbourhood_attention(hn, na_w_in[j], na_rpb[j], na_w_out[j])
        h = h + expert_choice_moe(rms_norm(h, ffn_norm[i]), router_w[i], exp_w_gate[i], exp_w_up[i], exp_w_down[i])
        h = h + per_layer_embedding(h, p[i], ple_norm[i], ple_w_up[i], ple_w_gate[i])
    return rms_norm(h, final_norm)

def setup_inputs(seed: int = 0) -> dict:
    key = jax.random.key(seed)
    ks = jax.random.split(key, 24)

    def nrm(k, shape, scale):
        return jax.random.normal(k, shape, F32) * scale

    def gain(k, shape):
        return 1.0 + 0.05 * jax.random.normal(k, shape, F32)

    D = D_MODEL
    base_logit = jnp.asarray(np.log(2.0 ** (5 + np.arange(RET_HEADS)) - 1.0), F32)
    return {
        "x_prompt": nrm(ks[0], (BATCH, SEQ, D), 1.0),
        "x_sample": nrm(ks[1], (DEC_BATCH, DEC_SEQ, D), 1.0),
        "p_prompt": nrm(ks[2], (DEPTH, BATCH, SEQ, PLE_DIM), 1.0),
        "p_sample": nrm(ks[3], (DEPTH, DEC_BATCH, DEC_SEQ, PLE_DIM), 1.0),
        "ret_w_in": nrm(ks[4], (N_RET_LAYERS, D, 6 * D), D ** -0.5),
        "ret_decay_logit": base_logit[None, None, :] + nrm(ks[5], (N_RET_LAYERS, 2, RET_HEADS), 0.1),
        "ret_gn_w": gain(ks[6], (N_RET_LAYERS, 2 * D)),
        "ret_w_out": nrm(ks[7], (N_RET_LAYERS, 2 * D, D), (2 * D) ** -0.5),
        "na_w_in": nrm(ks[8], (N_NA_LAYERS, D, 3 * D), D ** -0.5),
        "na_rpb": nrm(ks[9], (N_NA_LAYERS, NA_HEADS, 2 * NA_MAX_ROWS - 1, 2 * NA_WIN_COLS - 1), 0.1),
        "na_w_out": nrm(ks[10], (N_NA_LAYERS, D, D), D ** -0.5),
        "mix_norm": gain(ks[11], (DEPTH, D)),
        "ffn_norm": gain(ks[12], (DEPTH, D)),
        "ple_norm": gain(ks[13], (DEPTH, D)),
        "router_w": nrm(ks[14], (DEPTH, D, N_EXPERTS), D ** -0.5),
        "exp_w_gate": nrm(ks[15], (DEPTH, N_EXPERTS, D, D_FF_EXPERT), D ** -0.5),
        "exp_w_up": nrm(ks[16], (DEPTH, N_EXPERTS, D, D_FF_EXPERT), D ** -0.5),
        "exp_w_down": nrm(ks[17], (DEPTH, N_EXPERTS, D_FF_EXPERT, D), D_FF_EXPERT ** -0.5),
        "ple_w_up": nrm(ks[18], (DEPTH, PLE_DIM, D), PLE_DIM ** -0.5),
        "ple_w_gate": nrm(ks[19], (DEPTH, D, D), D ** -0.5),
        "final_norm": gain(ks[20], (D,)),
    }

def reference(x_prompt, x_sample, p_prompt, p_sample, ret_w_in, ret_decay_logit, ret_gn_w, ret_w_out,
              na_w_in, na_rpb, na_w_out, mix_norm, ffn_norm, ple_norm, router_w, exp_w_gate, exp_w_up,
              exp_w_down, ple_w_up, ple_w_gate, final_norm):
    y_prompt = trunk(x_prompt, p_prompt, ret_w_in, ret_decay_logit, ret_gn_w, ret_w_out, na_w_in, na_rpb,
                     na_w_out, mix_norm, ffn_norm, ple_norm, router_w, exp_w_gate, exp_w_up, exp_w_down,
                     ple_w_up, ple_w_gate, final_norm)
    y_sample = trunk(x_sample, p_sample, ret_w_in, ret_decay_logit, ret_gn_w, ret_w_out, na_w_in, na_rpb,
                     na_w_out, mix_norm, ffn_norm, ple_norm, router_w, exp_w_gate, exp_w_up, exp_w_down,
                     ple_w_up, ple_w_gate, final_norm)
    return (y_prompt, y_sample)


_drawn_inputs = setup_inputs


def setup_inputs(seed=0):
    import zlib

    import numpy as np

    out = dict(_drawn_inputs(seed))
    spreads = {}
    factors = {'na_rpb': 3.38, 'ple_norm': 3.877}
    for name, (base, spread) in spreads.items():
        noise = np.random.default_rng([zlib.crc32(name.encode()), seed]).standard_normal(out[name].shape)
        drawn = base * np.exp(spread * noise) if base else spread * noise
        out[name] = __import__('jax').numpy.asarray(drawn.astype(out[name].dtype))
    for name, factor in factors.items():
        out[name] = (out[name] * factor).astype(out[name].dtype)
    return out
```

```python
from contextlib import ExitStack

import numpy as np
import concourse.bass as bass
from concourse import mybir

ALU = mybir.AluOpType
ACT = mybir.ActivationFunctionType
AX_X = mybir.AxisListType.X
F32 = mybir.dt.float32
BF16 = mybir.dt.bfloat16
U32 = mybir.dt.uint32

P = 128
D = 1024
DT = D // P
SEQ_P, SEQ_S = 256, 512
TOK = SEQ_P + SEQ_S
TT = TOK // P
GROUPS = [(0, SEQ_P), (SEQ_P, SEQ_S)]
HALF = 512
EPS = 1e-6

RET_HEADS, RET_DK, RET_DV = 4, 256, 512
STRIP = SEQ_S + SEQ_S - P
STRIP0 = SEQ_S - P

GRID_W = 64
NA_HEADS, NA_DH = 16, 64
QUAD = 4
ROWS_P, ROWS_S = SEQ_P // GRID_W, SEQ_S // GRID_W
COLS_P, COLS_S = P // ROWS_P, P // ROWS_S
NA_WIN = 16
RPB_A, RPB_B = 15, 31
RPB_PAD = 64
WIDE_S, WIDE_P = 3 * COLS_S, 3 * COLS_P
A_P = 2 * ROWS_P - 1
A0_P = RPB_A // 2 - (ROWS_P - 1)

EXPERTS = 16
CAP_P, CAP_S = 2 * SEQ_P // EXPERTS, 2 * SEQ_S // EXPERTS
CAP = CAP_P + CAP_S
PLE = 256
MASKED = -1e30

NA_KEYS = [(0, 2, 0), (0, 2, 256), (2, 2, 512), (2, 3, 768), (3, 3, 768), (4, 2, 1152)]
MASK_W = 1408


def at(base, per, i):
    return base + i * per if per else base


class Plan:

    def __init__(self, n):
        self.count = [0] * n
        self.where = {}

    def add(self, phase, keys, passes=1):
        places = [place for _, place in keys]
        local = {}
        for key, place in keys:
            local[place] = local.get(place, 0) + 1
            per = places.count(place) if passes > 1 else 0
            self.where[phase, key] = (place, self.count[place] + local[place], per)
        for place, n in local.items():
            self.count[place] += n * passes

    def get(self, phase, key, i):
        place, first, per = self.where[phase, key]
        return place, first, per, at(first, per, i)


class Chain:

    def __init__(self, eng, sem):
        self.eng, self.sem, self.base, self.local, self.i, self.per = eng, sem, 0, 0, 0, 0

    def link(self, ins):
        ins.then_inc(self.sem, 1)
        self.local += 1
        self.eng.wait_ge(self.sem, at(self.base + self.local, self.per, self.i))

    def enter(self, i, per):
        self.base += self.local
        self.local, self.i, self.per = 0, i, per

    def leave(self, passes):
        assert self.local == self.per, (self.local, self.per)
        self.base += self.per * passes
        self.local, self.i, self.per = 0, 0, 0


def psum_keys(keys):
    return [(k, n % 8) for n, k in enumerate(keys)]


def ret_keys():
    keys = []
    for g, (_, n) in enumerate(GROUPS):
        nt = n // P
        keys += [("qk", g, f) for f in range(4)] + [("v", g, t) for t in range(nt)]
        keys += [("s", g, t) for t in range(nt)]
        for t in range(nt):
            keys += [("g", g, t), ("o", g, t)]
            if t:
                keys.append(("tr", g, t - 1))
        keys.append(("tr", g, nt - 1))
        keys += [("out", g, t, h) for t in range(nt) for h in range(2)]
    return keys


def na_units():
    return [(t, h) for t in range(TT) for h in range(QUAD)]


def na_keys():
    keys = [("qk", f, n) for f in range(4) for n in range(2)] + [("v", t) for t in range(TT)]
    units = na_units()
    for u in range(len(units) + 2):
        if u < len(units):
            keys.append(("s", u))
        if 1 <= u <= len(units):
            keys.append(("pt", u - 1))
        if u >= 2:
            if units[u - 2][1] == 0:
                keys.append(("o", units[u - 2][0]))
            if units[u - 2][1] == QUAD - 1:
                keys.append(("tr", units[u - 2][0]))
    place = {"qk": [0, 1, 2, 3, 4, 5, 6, 7], "v": [0, 1, 2, 3, 4, 5], "s": [0, 1, 2], "pt": [3, 4],
             "o": [5, 6], "tr": [7]}
    seen = {}
    out = []
    for k in keys:
        n = seen.get(k[0], 0)
        seen[k[0]] = n + 1
        out.append((k, place[k[0]][n % len(place[k[0]])]))
    return out


def build(nc, x_prompt, x_sample, p_prompt, p_sample, ret_w_in, ret_decay_logit, ret_gn_w, ret_w_out,
          na_w_in, na_rpb_padded, na_w_out, mix_norm, ffn_norm, ple_norm, router_w, exp_w_gate, exp_w_up,
          exp_w_down, ple_w_up, ple_w_gate, final_norm, rope_cos, rope_sin, row_minus_col, col_mask,
          y_prompt, y_sample):
    ctx = ExitStack()
    with ctx:
        def sb(name, shape, dt=F32):
            return ctx.enter_context(nc.sbuf_tensor(name, shape, dt))

        def sem(name):
            return ctx.enter_context(nc.semaphore(name))

        rows_normed = [nc.dram_tensor(f"rows_normed{l}", [TOK, D], F32, kind="Internal").ap() for l in range(2)]
        rows_summed = [nc.dram_tensor(f"rows_summed{l}", [TOK, D], F32, kind="Internal").ap() for l in range(2)]
        bias_s = nc.dram_tensor("bias_s", [COLS_S, NA_HEADS, RPB_A, WIDE_S], F32, kind="Internal").ap()
        bias_p = nc.dram_tensor("bias_p", [COLS_P, NA_HEADS, A_P, WIDE_P], F32, kind="Internal").ap()

        wt = sb("wt", [P, 6, 4096])
        resid = sb("resid", [P, TT, D])
        xt = sb("xt", [P, DT, TOK])
        work = sb("work", [P, 6144])
        xn = sb("xn", [P, 2, D])
        gain = sb("gain", [P, 2, D])
        ident = sb("ident", [P, P])
        ident16 = sb("ident16", [P, P], BF16)
        cos_t = sb("cos_t", [P, SEQ_S])
        sin_t = sb("sin_t", [P, SEQ_S])
        mask = sb("mask", [P, MASK_W], BF16)
        bias = sb("bias", [P, QUAD, 8 * WIDE_S + 4 * WIDE_P])
        rw = sb("rw", [P, 2, DT, EXPERTS])
        sumsq = sb("sumsq", [P, 8])
        meansq = sb("meansq", [P, 8])
        rstd = sb("rstd", [P, 8])
        minus_half = sb("minus_half", [P, 8])
        lg = sb("lg", [P, 2 * RET_HEADS])
        lgt = sb("lgt", [P, 8, 8])
        stats = sb("stats", [P, 6])
        mv = sb("mv", [P, 2, 2])
        mvr = sb("mvr", [P, 2])
        top_v = sb("top_v", [EXPERTS, CAP])
        top_i = sb("top_i", [EXPERTS, CAP], U32)
        top_f = sb("top_f", [EXPERTS, CAP])
        gate_t = sb("gate_t", [CAP, EXPERTS])
        idx_t = sb("idx_t", [CAP, EXPERTS], U32)
        idx_in = sb("idx_in", [CAP, 1], U32)
        idx_out = sb("idx_out", [CAP, 1], U32)
        rsm = sb("rsm", [P, 4, 8])
        mx = sb("mx", [P, 2])
        nmx = sb("nmx", [P, 2])
        den = sb("den", [P, 2, QUAD])
        rden = sb("rden", [P, QUAD])

        bank = [ctx.enter_context(nc.psum_tensor(f"bank{b}", [P, HALF], F32)) for b in range(8)]

        psum, slot = Plan(8), Plan(6)
        norm_uses = [(("t", t, c), (2 * t + c) % 8) for t in range(TT) for c in range(2)]
        moe_uses = [("g0", 0), ("u0", 1), ("g1", 2), ("u1", 3), ("x0", 4), ("x1", 5), ("h0", 6), ("h1", 7),
                    ("y0", 4), ("y1", 5)]

        def plan_moe(l):
            psum.add(f"route{l}", [("logit", 0), ("aff0", 1), ("aff1", 2), ("gate", 3), ("idx", 4)])
            psum.add(f"first{l}", [("x0", 4), ("x1", 5)])
            psum.add(f"moe{l}", moe_uses, EXPERTS - 1)
            psum.add(f"last{l}", [(k, b) for k, b in moe_uses if k[0] != "x"])

        def plan_ple(l):
            psum.add(f"ple{l}", psum_keys([("pt", t) for t in range(TT)]
                                          + [(k, t, h) for t in range(TT) for h in range(2) for k in "gu"]))

        psum.add("norm0", norm_uses)
        psum.add("ret", psum_keys(ret_keys()), RET_HEADS)
        psum.add("norm1", norm_uses)
        plan_moe(0)
        psum.add("norm2", norm_uses)
        plan_ple(0)
        psum.add("norm3", norm_uses)
        psum.add("na", na_keys(), NA_HEADS // QUAD)
        psum.add("naout", psum_keys([("out", t, h) for t in range(TT) for h in range(2)]))
        psum.add("norm4", norm_uses)
        plan_moe(1)
        psum.add("norm5", norm_uses)
        plan_ple(1)

        slot.add("ret", [("q", 0), ("k", 0), ("v", 1), ("g", 2), ("o", 3)], RET_HEADS)
        slot.add("moe0", [(s, s) for s in range(6)], EXPERTS)
        slot.add("ple0", [("g0", 0), ("g1", 1), ("u", 2)])
        slot.add("na", [("q", 0), ("k", 0), ("v", 1)], NA_HEADS // QUAD)
        slot.add("naout", [(0, 4), (1, 5)])
        slot.add("moe1", [(s, s) for s in range(6)], EXPERTS)
        slot.add("ple1", [("g0", 0), ("g1", 1), ("u", 2)])

        bank_full = [sem(f"bank_full{b}") for b in range(8)]
        bank_free = [sem(f"bank_free{b}") for b in range(8)]
        slot_full = [sem(f"slot_full{s}") for s in range(6)]
        dve_step, pool_step = sem("dve_step"), sem("pool_step")
        held = sem("held")
        x_in = [sem(f"x_in{g}") for g in range(2)]
        const_in, bias_table, gn_in, ident_set = sem("const_in"), sem("bias_table"), sem("gn_in"), sem("ident_set")
        gain_in = [sem(f"gain_in{b}") for b in range(2)]
        norm_sq = [sem(f"norm_sq{n}") for n in range(7)]
        norm_rs = [sem(f"norm_rs{n}") for n in range(7)]
        norm_rows = [sem(f"norm_rows{n}") for n in range(7)]
        rows_out = [[sem(f"rows_out{n}_{b}") for b in range(2)] for n in range(2)]
        final_out = [sem(f"final_out{b}") for b in range(2)]
        decay_abs, decay_exp = sem("decay_abs"), sem("decay_exp")
        strip_arg, strip_set = sem("strip_arg"), sem("strip_set")
        ret_rot = sem("ret_rot")
        ret_var, ret_rstd, ret_og = sem("ret_var"), sem("ret_rstd"), sem("ret_og")
        moe_exp = [sem(f"moe_exp{l}") for l in range(2)]
        moe_aff = [sem(f"moe_aff{l}") for l in range(2)]
        moe_top = [sem(f"moe_top{l}") for l in range(2)]
        moe_rows = [sem(f"moe_rows{l}") for l in range(2)]
        moe_added = [sem(f"moe_added{l}") for l in range(2)]
        moe_y_free = [sem(f"moe_y_free{l}") for l in range(2)]
        resid_saved = [sem(f"resid_saved{l}") for l in range(2)]
        resid_in = [sem(f"resid_in{l}") for l in range(2)]
        p_in = [sem(f"p_in{l}") for l in range(2)]
        ple_add = [sem(f"ple_add{l}") for l in range(2)]
        na_bias, na_max, na_exp = sem("na_bias"), sem("na_max"), sem("na_exp")

        def fill(pe, phase, key, i=0):
            b, first, per, _ = psum.get(phase, key, i)
            if first > 1 or per:
                pe.wait_ge(bank_free[b], at(first - 1, per, i))
            return bank[b], bank_full[b]

        def filled(eng, phase, key, i=0):
            b, _, _, n = psum.get(phase, key, i)
            eng.wait_ge(bank_full[b], n)
            return bank[b], bank_free[b]

        def matmuls_done(eng, phase, key, i=0):
            b, _, _, n = psum.get(phase, key, i)
            eng.wait_ge(bank_full[b], n)

        def drained(eng, phase, key, i=0):
            b, _, _, n = psum.get(phase, key, i)
            eng.wait_ge(bank_free[b], n)

        def hold(eng):
            eng.sem_inc(held, 1)

        def loaded(pe, phase, key, i=0):
            s, first, per, _ = slot.get(phase, key, i)
            pe.wait_ge(slot_full[s], at(16 * first, 16 * per, i))

        def w3(s, a, b):
            return wt[:, s, 0:a * b].rearrange("p (a b) -> p a b", a=a)

        big = wt[:, 4:6, :].rearrange("p s n -> p (s n)")
        r_qk = big[:, 0:2048].rearrange("p (f n) -> p f n", f=4)
        r_v = big[:, 2048:4096].rearrange("p (t n) -> p t n", t=4)
        r_s = big[:, 4096:6144].rearrange("p (t n) -> p t n", t=4)
        r_ot = big[:, 6144:8192].rearrange("p (f n) -> p f n", f=4)
        r_diff, r_strip = work[:, 0:STRIP], work[:, STRIP:2 * STRIP]
        o = 2 * STRIP
        r_tmp = work[:, o:o + 2048].rearrange("p (f n) -> p f n", f=4)
        r_og = work[:, o + 2048:o + 3072].rearrange("p (f n) -> p f n", f=2)
        r_silu = work[:, o + 3072:o + 4096].rearrange("p (f n) -> p f n", f=2)
        r_gn = xn[:, :, :].rearrange("p a n -> p (a n)")
        m_x = work[0:CAP, 0:1024]
        m_xt = work[:, 1024:1792].rearrange("p (f n) -> p f n", f=DT)
        m_silu = work[0:CAP, 1792:2816].rearrange("p (f n) -> p f n", f=2)
        m_hid = work[0:CAP, 2816:3840]
        m_hidt = work[:, 3840:4608].rearrange("p (f n) -> p f n", f=DT)
        m_y = work[0:CAP, 4608:5632]
        m_aff = work[0:EXPERTS, 4608:4608 + TOK]
        m_lg = work[:, 5632:5632 + TT * EXPERTS].rearrange("p (t e) -> p t e", t=TT)
        m_ex = work[:, 5760:5760 + TT * EXPERTS].rearrange("p (t e) -> p t e", t=TT)
        m_af = work[:, 5888:5888 + TT * EXPERTS].rearrange("p (t e) -> p t e", t=TT)
        e_p = work[:, 0:1536].rearrange("p (t n) -> p t n", t=TT)
        e_pt = work[:, 1536:3072].rearrange("p (f n) -> p f n", f=2)
        e_sig = work[:, 3072:4096].rearrange("p (f n) -> p f n", f=2)
        e_prod = work[:, 4096:5120].rearrange("p (f n) -> p f n", f=2)
        nbig = wt[:, 2:4, :].rearrange("p s n -> p (s n)")
        n_qk = nbig[:, 0:3072].rearrange("p (f n) -> p f n", f=4)
        n_v = nbig[:, 3072:4608].rearrange("p (t n) -> p t n", t=TT)
        n_s = nbig[:, 4608:5376].rearrange("p (t n) -> p t n", t=2)
        n_p = nbig[:, 5376:6144].rearrange("p (t n) -> p t n", t=2)
        n_pt = nbig[:, 6144:6912].rearrange("p (t n) -> p t n", t=2)
        n_o = nbig[:, 6912:7424].rearrange("p (t n) -> p t n", t=2)
        n_ot = work[:, :].rearrange("p (f n) -> p f n", f=DT)

        def natural_rows(src_p, src_s, tiles):
            return [(src_p.rearrange("(t p) d -> p t d", p=P), tiles[:, 0:2, :]),
                    (src_s.rearrange("(t p) d -> p t d", p=P), tiles[:, 2:TT, :])]

        def grid_rows(src_p, src_s, tiles):
            out = []
            for r in range(ROWS_P):
                out.append((src_p[r * GRID_W:(r + 1) * GRID_W, :].rearrange("(t c) d -> c t d", c=COLS_P),
                            tiles[r * COLS_P:(r + 1) * COLS_P, 0:2, :]))
            for r in range(ROWS_S):
                out.append((src_s[r * GRID_W:(r + 1) * GRID_W, :].rearrange("(t c) d -> c t d", c=COLS_S),
                            tiles[r * COLS_S:(r + 1) * COLS_S, 2:TT, :]))
            return out

        def tile_rows(dram, t, order):
            if order == 0:
                return [(dram[t * P:(t + 1) * P, :], 0, P)]
            out = []
            first, rows, cols, j = (0, ROWS_P, COLS_P, t) if t < 2 else (SEQ_P, ROWS_S, COLS_S, t - 2)
            for r in range(rows):
                a = first + r * GRID_W + j * cols
                out.append((dram[a:a + cols, :], r * cols, cols))
            return out

        def pieces(tiles, order, parity=None):
            return sum(len(tile_rows(rows_normed[0], t, order)) for t in range(tiles) if parity in (None, t % 2))

        block = ctx.enter_context(nc.Block())

        @block.sync
        def _(sp):
            sp.dma_start(resid[:, 0:2, :], x_prompt[0].rearrange("(t p) d -> p t d", p=P)).then_inc(x_in[0], 16)
            sp.dma_start(resid[:, 2:TT, :], x_sample[0].rearrange("(t p) d -> p t d", p=P)).then_inc(x_in[1], 16)

            def columns(w, first, n):
                return w.rearrange("(t p) f -> p t f", p=P)[:, :, bass.ds(first, n)]

            def halves(w):
                return [columns(w, f * HALF, HALF) for f in range(2)]

            def ret_loads(h, again):
                if again:
                    matmuls_done(sp, "ret", ("qk", 1, 3), h - 1)
                q_k = w3(0, DT, 512)
                sp.dma_start(q_k[:, :, 0:256], columns(ret_w_in[0], h * 256, 256)).then_inc(slot_full[0], 16)
                sp.dma_start(q_k[:, :, 256:512], columns(ret_w_in[0], h * 256 + D, 256)).then_inc(slot_full[0], 16)
                if again:
                    matmuls_done(sp, "ret", ("v", 1, 3), h - 1)
                sp.dma_start(w3(1, DT, 512), columns(ret_w_in[0], h * 512 + 2 * D, 512)).then_inc(slot_full[1], 16)
                if again:
                    matmuls_done(sp, "ret", ("g", 1, 3), h - 1)
                sp.dma_start(w3(2, DT, 512), columns(ret_w_in[0], h * 512 + 4 * D, 512)).then_inc(slot_full[2], 16)
                if again:
                    matmuls_done(sp, "ret", ("out", 1, 3, 1), h - 1)
                sp.dma_start(w3(3, 4, D), ret_w_out[0].rearrange("(t p) f -> p t f", p=P)[:, bass.ds(h * 4, 4), :])\
                    .then_inc(slot_full[3], 16)

            ret_loads(0, False)
            with sp.Fori(1, RET_HEADS) as h:
                ret_loads(h, True)

            def shifted(first, n_a, wide):
                v = na_rpb_padded[bass.ds(first, 64)]
                return bass.AP(tensor=v.tensor, offset=v.offset,
                               ap=[[RPB_A * RPB_B, NA_HEADS], [RPB_B, n_a], [1, wide]])

            with sp.Fori(0, COLS_S) as c:
                sp.dma_start(bias_s[c], shifted(RPB_PAD + NA_WIN - 1 - COLS_S - c, RPB_A, WIDE_S))\
                    .then_inc(bias_table, 16)
            with sp.Fori(0, COLS_P) as c:
                sp.dma_start(bias_p[c], shifted(RPB_PAD + A0_P * RPB_B + NA_WIN - 1 - COLS_P - c, A_P, WIDE_P))\
                    .then_inc(bias_table, 16)

            def moe_loads(l, before):
                order = [(2 * f + k, w, f) for f in range(2) for k, w in enumerate((exp_w_gate, exp_w_up))]
                order += [(4 + f, exp_w_down, f) for f in range(2)]
                users = ["g0", "u0", "g1", "u1", "y0", "y1"]
                for s, w, f in order:
                    matmuls_done(sp, *before[s])
                    sp.dma_start(w3(s, DT, HALF), halves(w[l, 0])[f]).then_inc(slot_full[s], 16)
                with sp.Fori(1, EXPERTS) as e:
                    for s, w, f in order:
                        matmuls_done(sp, f"moe{l}", users[s], e - 1)
                        sp.dma_start(w3(s, DT, HALF), halves(w[l, e])[f]).then_inc(slot_full[s], 16)

            def ple_loads(l):
                for s, w in enumerate(halves(ple_w_gate[l])):
                    matmuls_done(sp, f"last{l}", ("g0", "u0")[s])
                    sp.dma_start(w3(s, DT, HALF), w).then_inc(slot_full[s], 16)
                matmuls_done(sp, f"last{l}", "g1")
                sp.dma_start(w3(2, 2, D), ple_w_up[l].rearrange("(t p) f -> p t f", p=P)).then_inc(slot_full[2], 16)

            r = RET_HEADS - 1
            moe_loads(0, [("ret", ("qk", 1, 3), r), ("ret", ("v", 1, 3), r), ("ret", ("g", 1, 3), r)]
                      + [("ret", ("out", 1, 3, 1), r)] * 3)
            ple_loads(0)

            def na_loads(q, before):
                matmuls_done(sp, *before[0])
                q_k = w3(0, DT, 512)
                sp.dma_start(q_k[:, :, 0:256], columns(na_w_in[0], q * 256, 256)).then_inc(slot_full[0], 16)
                sp.dma_start(q_k[:, :, 256:512], columns(na_w_in[0], q * 256 + D, 256)).then_inc(slot_full[0], 16)
                matmuls_done(sp, *before[1])
                sp.dma_start(w3(1, DT, 256), columns(na_w_in[0], q * 256 + 2 * D, 256)).then_inc(slot_full[1], 16)

            na_loads(0, [("ple0", ("g", TT - 1, 0)), ("ple0", ("g", TT - 1, 1))])
            for f, w in enumerate(halves(na_w_out[0])):
                matmuls_done(sp, "last0", f"y{f}")
                sp.dma_start(w3(4 + f, DT, HALF), w).then_inc(slot_full[4 + f], 16)
            with sp.Fori(1, NA_HEADS // QUAD) as q:
                na_loads(q, [("na", ("qk", 3, 1), q - 1), ("na", ("v", TT - 1), q - 1)])
            r = NA_HEADS // QUAD - 1
            moe_loads(1, [("na", ("qk", 3, 1), r), ("na", ("v", TT - 1), r), ("na", ("tr", TT - 1), r),
                          ("na", ("tr", TT - 1), r), ("naout", ("out", TT - 1, 0)), ("naout", ("out", TT - 1, 1))])
            ple_loads(1)

        @block.gpsimd
        def _(pool):
            chain = Chain(pool, pool_step)
            gains = [mix_norm[0], ffn_norm[0], ple_norm[0], mix_norm[1], ffn_norm[1], ple_norm[1], final_norm]

            def load_gain(n):
                pool.dma_start(gain[:, n % 2, :], gains[n].rearrange("(a d) -> a d", a=1).broadcast_to([P, D]))\
                    .then_inc(gain_in[n % 2], 16)

            load_gain(0)
            for m in (ident, ident16):
                chain.link(nc.gpsimd.memset(m[:], 0.0))
                nc.gpsimd.affine_select(out=m[:], in_=m[:], compare_op=ALU.not_equal, fill=1.0, base=0,
                                        pattern=[[-1, P]], channel_multiplier=1).then_inc(ident_set, 1)
            chain.link(nc.gpsimd.memset(minus_half[:], -0.5))
            pool.dma_start(lgt[:, 0, :], ret_decay_logit.rearrange("a b h -> a (b h)").broadcast_to([P, 8]))\
                .then_inc(const_in, 16)
            pool.dma_start(r_diff, row_minus_col).then_inc(const_in, 16)
            pool.dma_start(cos_t[:], rope_cos).then_inc(const_in, 16)
            pool.dma_start(sin_t[:], rope_sin).then_inc(const_in, 16)
            load_gain(1)
            pool.dma_start(mask[:], col_mask.bitcast(BF16)).then_inc(const_in, 16)
            pool.dma_start(rw[:, :, :, :].rearrange("p l t e -> p (l t) e"),
                           router_w.rearrange("l (t p) e -> p (l t) e", p=P)).then_inc(const_in, 16)

            def rsqrt(src, scale, dst, t):
                chain.link(nc.gpsimd.tensor_scalar(meansq[:, t:t + 1], src, scale, EPS, ALU.mult, ALU.add))
                return nc.gpsimd.tensor_tensor(dst, meansq[:, t:t + 1], minus_half[:, 0:1], ALU.pow)

            def save_rows(n, l, t, order):
                pool.wait_ge(norm_rows[n], t + 1)
                for dram, p0, k in tile_rows(rows_normed[l], t, order):
                    pool.dma_start(dram, xn[p0:p0 + k, t % 2, :]).then_inc(rows_out[l][t % 2], 16)
                for dram, p0, k in tile_rows(rows_summed[l], t, order):
                    pool.dma_start(dram, resid[p0:p0 + k, t, :]).then_inc(resid_saved[l], 16)

            def norm(n, l=None, order=0):
                for t in range(TT):
                    pool.wait_ge(norm_sq[n], t + 1)
                    rsqrt(sumsq[:, t:t + 1], 1.0 / D, rstd[:, t:t + 1], t).then_inc(norm_rs[n], 1)
                    if l is not None and t:
                        save_rows(n, l, t - 1, order)
                if l is not None:
                    save_rows(n, l, TT - 1, order)
                if 1 <= n < 6:
                    load_gain(n + 1)

            def mixture(l, order):
                pool.wait_ge(resid_saved[l], 16 * pieces(TT, order))
                for b in range(2):
                    pool.wait_ge(rows_out[l][b], 16 * pieces(TT, order, b))
                drained(pool, f"route{l}", "idx")

                def gather(e):
                    chain.link(nc.gpsimd.tensor_copy(idx_in[:], idx_t[:, bass.ds(e, 1)]))
                    hold(pool)
                    nc.gpsimd.indirect_dma_start(
                        out=m_x, out_offset=None, in_=rows_normed[l],
                        in_offset=bass.IndirectOffsetOnAxis(ap=idx_in[:, :], axis=0)).then_inc(moe_rows[l], 16)

                def scatter(phase, e, n):
                    drained(pool, phase, "y1", e)
                    chain.link(nc.gpsimd.tensor_copy(idx_out[:], idx_t[:, bass.ds(n, 1)]))
                    hold(pool)
                    nc.gpsimd.indirect_dma_start(
                        out=rows_summed[l], out_offset=bass.IndirectOffsetOnAxis(ap=idx_out[:, :], axis=0),
                        in_=m_y, in_offset=None, compute_op=ALU.add).then_inc(moe_added[l], 16)
                    pool.wait_ge(moe_added[l], at(16, 16, n))
                    pool.sem_inc(moe_y_free[l], 1)

                pool.sem_inc(moe_y_free[l], 1)
                gather(0)
                matmuls_done(pool, f"first{l}", "x1")
                gather(1)
                with pool.Fori(0, EXPERTS - 2) as e:
                    chain.enter(e, 2)
                    matmuls_done(pool, f"moe{l}", "x1", e)
                    gather(e + 2)
                    scatter(f"moe{l}", e, e)
                    chain.leave(EXPERTS - 2)
                scatter(f"moe{l}", EXPERTS - 2, EXPERTS - 2)
                scatter(f"last{l}", 0, EXPERTS - 1)

            def after_mixture(l, order):
                rows = grid_rows if order else natural_rows
                src = rows_summed[l]
                for dram, tiles in rows(src[0:SEQ_P, :], src[SEQ_P:TOK, :], resid):
                    pool.dma_start(tiles, dram).then_inc(resid_in[l], 16)
                for dram, tiles in rows(p_prompt[l, 0], p_sample[l, 0], e_p):
                    pool.dma_start(tiles, dram).then_inc(p_in[l], 16)

            def load_bias(q):
                for rows, cols, table, w, lo in ((ROWS_S, COLS_S, bias_s, WIDE_S, 0),
                                                 (ROWS_P, COLS_P, bias_p, WIDE_P, 8 * WIDE_S)):
                    for r in range(rows):
                        a = rows - 1 - r
                        src = table[:, bass.ds(q * QUAD, QUAD), a:a + rows, :].rearrange("c h a w -> c h (a w)")
                        pool.dma_start(bias[r * cols:(r + 1) * cols, :, lo:lo + rows * w], src).then_inc(na_bias, 16)

            norm(0)
            matmuls_done(pool, "norm0", ("t", TT - 1, 1))
            pool.dma_start(r_gn, ret_gn_w.broadcast_to([P, 2 * D])).then_inc(gn_in, 16)
            with pool.Fori(0, RET_HEADS) as h:
                chain.enter(h, TT)
                for t in range(TT):
                    pool.wait_ge(ret_var, at(t + 1, TT, h))
                    hold(pool)
                    rsqrt(mv[:, t % 2, 1:2], 1.0, mvr[:, t % 2:t % 2 + 1], t).then_inc(ret_rstd, 1)
                chain.leave(RET_HEADS)
            norm(1, 0, 0)
            mixture(0, 0)
            after_mixture(0, 1)
            norm(2)
            pool.wait_ge(bias_table, 16 * (COLS_S + COLS_P))
            load_bias(0)
            norm(3)
            with pool.Fori(1, NA_HEADS // QUAD) as q:
                drained(pool, "na", ("s", len(na_units()) - 1), q - 1)
                load_bias(q)
            norm(4, 1, 1)
            mixture(1, 1)
            after_mixture(1, 0)
            norm(5)
            outs = [y_prompt[0, 0:P], y_prompt[0, P:SEQ_P]] + [y_sample[0, t * P:(t + 1) * P] for t in range(4)]
            for t in range(TT):
                pool.wait_ge(norm_sq[6], t + 1)
                rsqrt(sumsq[:, t:t + 1], 1.0 / D, rstd[:, t:t + 1], t).then_inc(norm_rs[6], 1)
                pool.wait_ge(norm_rows[6], t + 1)
                pool.dma_start(outs[t], xn[:, t % 2, :]).then_inc(final_out[t % 2], 16)
            for b in range(2):
                pool.wait_ge(final_out[b], 16 * TT // 2)

        @block.scalar
        def _(act):
            def resid_wait(n, t):
                if n == 0:
                    act.wait_ge(x_in[0 if t < 2 else 1], 16)
                elif n == 1:
                    drained(act, "ret", ("out", 1, 3, 1), RET_HEADS - 1)
                elif n in (2, 5):
                    act.wait_ge(resid_in[n // 3], 16 * (ROWS_P + ROWS_S if n == 2 else 2))
                elif n in (3, 6):
                    act.wait_ge(ple_add[n // 3 - 1], 2 * (t + 1))
                else:
                    drained(act, "naout", ("out", t, 1))

            def norm(n, l=None, order=0):
                for t in range(TT + 1):
                    if t < TT:
                        resid_wait(n, t)
                        if t >= 2 and n < 6:
                            matmuls_done(act, f"norm{n}", ("t", t - 2, 1))
                        if t >= 2 and l is not None:
                            act.wait_ge(rows_out[l][t % 2], 16 * pieces(t - 1, order, t % 2))
                        if t >= 2 and n == 6:
                            act.wait_ge(final_out[t % 2], 16 * (t // 2))
                        nc.scalar.activation(xn[:, t % 2, :], resid[:, t, :], ACT.Square,
                                             accum_out=sumsq[:, t:t + 1]).then_inc(norm_sq[n], 1)
                    if t and n < 6:
                        b, done = filled(act, f"norm{n}", ("t", t - 1, 0))
                        nc.scalar.copy(xt[:, 0:4, (t - 1) * P:t * P],
                                       b[:, :].rearrange("p (f n) -> p f n", f=4)).then_inc(done, 1)

            norm(0)
            act.wait_ge(decay_abs, 1)
            nc.scalar.activation(lgt[:, 2, :], lgt[:, 1, :], ACT.Exp, scale=-1.0).then_inc(decay_exp, 1)

            with act.Fori(0, RET_HEADS) as h:
                act.wait_ge(strip_arg, h + 1)
                nc.scalar.activation(r_strip, r_strip, ACT.Exp).then_inc(strip_set, 1)
                for g, (_, n) in enumerate(GROUPS):
                    nt = n // P
                    for t in range(nt):
                        b, done = filled(act, "ret", ("v", g, t), h)
                        nc.scalar.copy(r_v[:, t, :], b[:, :]).then_inc(done, 1)
                    for t in range(nt + 1):
                        if t < nt:
                            b, done = filled(act, "ret", ("g", g, t), h)
                            nc.scalar.activation(r_silu[:, t % 2, :], b[:, :], ACT.Silu).then_inc(done, 1)
                        if t:
                            b, done = filled(act, "ret", ("tr", g, t - 1), h)
                            nc.scalar.copy(r_ot[:, :, (t - 1) * P:t * P],
                                           b[:, :].rearrange("p (f n) -> p f n", f=4)).then_inc(done, 1)

            def mixture(l):
                drained(act, f"route{l}", "logit")
                nc.scalar.activation(m_ex, m_lg, ACT.Exp).then_inc(moe_exp[l], 1)

                def move(phase, key, i, dst):
                    b, done = filled(act, phase, key, i)
                    nc.scalar.copy(dst, b[:, 0:4 * CAP].rearrange("p (f n) -> p f n", f=4)).then_inc(done, 1)

                def expert(phase, e):
                    for f in range(2):
                        b, done = filled(act, phase, f"g{f}", e)
                        nc.scalar.activation(m_silu[:, f, :], b[0:CAP, :], ACT.Silu).then_inc(done, 1)
                    if phase[0] == "m":
                        for c in range(2):
                            move(phase, f"x{c}", e, m_xt[:, 4 * c:4 * c + 4, :])
                    for c in range(2):
                        move(phase, f"h{c}", e, m_hidt[:, 4 * c:4 * c + 4, :])

                for c in range(2):
                    move(f"first{l}", f"x{c}", 0, m_xt[:, 4 * c:4 * c + 4, :])
                with act.Fori(0, EXPERTS - 1) as e:
                    expert(f"moe{l}", e)
                expert(f"last{l}", 0)

            def embedding(l):
                for t in range(TT):
                    b, done = filled(act, f"ple{l}", ("pt", t))
                    nc.scalar.copy(e_pt[:, :, t * P:(t + 1) * P],
                                   b[:, 0:2 * P].rearrange("p (f n) -> p f n", f=2)).then_inc(done, 1)
                for t in range(TT):
                    for f in range(2):
                        if t:
                            drained(act, f"ple{l}", ("u", t - 1, f))
                        b, done = filled(act, f"ple{l}", ("g", t, f))
                        nc.scalar.activation(e_sig[:, f, :], b[:, :], ACT.Sigmoid).then_inc(done, 1)

            norm(1, 0, 0)
            mixture(0)
            norm(2)
            embedding(0)
            norm(3)

            units = na_units()
            with act.Fori(0, NA_HEADS // QUAD) as q:
                for f in range(2):
                    for c, (a, w) in enumerate(((0, 512), (512, 256))):
                        b, done = filled(act, "na", ("qk", f, c), q)
                        nc.scalar.mul(n_qk[:, f, a:a + w], b[:, 0:w], NA_DH ** -0.5).then_inc(done, 1)
                for t in range(0, TT, 2):
                    b, done = filled(act, "na", ("v", t), q)
                    nc.scalar.copy(n_v[:, t, :], b[:, 0:256]).then_inc(done, 1)
                for u in range(len(units) + 2):
                    if u < len(units):
                        t, h = units[u]
                        w = NA_KEYS[t][1] * P
                        act.wait_ge(na_max, at(u + 1, len(units), q))
                        if u >= 2:
                            matmuls_done(act, "na", ("pt", u - 2), q)
                        nc.scalar.activation(n_p[:, u % 2, 0:w], n_s[:, u % 2, 0:w], ACT.Exp, bias=nmx[:, u % 2:u % 2 + 1],
                                             accum_out=den[:, t % 2, h:h + 1]).then_inc(na_exp, 1)
                    if 1 <= u <= len(units) and (u - 1) % 2 == 0:
                        w = NA_KEYS[units[u - 1][0]][1] * P
                        b, done = filled(act, "na", ("pt", u - 1), q)
                        nc.scalar.copy(n_pt[:, 0, 0:w], b[:, 0:w]).then_inc(done, 1)
                    if u >= 2 and units[u - 2][1] == QUAD - 1:
                        t = units[u - 2][0]
                        b, done = filled(act, "na", ("tr", t), q)
                        nc.scalar.copy(n_ot[:, bass.ds(q * 2, 2), t * P:(t + 1) * P],
                                       b[:, 0:2 * P].rearrange("p (f n) -> p f n", f=2)).then_inc(done, 1)
            norm(4, 1, 1)
            mixture(1)
            norm(5)
            embedding(1)
            norm(6)

        @block.tensor
        def _(pe):
            def transposes(phase, key, srcs, i=0, w=P):
                b, full = fill(pe, phase, key, i)
                for c, src in enumerate(srcs):
                    k = src.shape[0]
                    last = nc.tensor.transpose(b[:, c * w:(c + 1) * w], src, ident[0:k, 0:k])
                last.then_inc(full, 1)

            def product(phase, key, lhs, rhs, i=0, m=P):
                b, full = fill(pe, phase, key, i)
                n = rhs[0].shape[-1]
                for c, (x, y) in enumerate(zip(lhs, rhs)):
                    last = nc.tensor.matmul(b[0:m, 0:n], x, y, start=(c == 0), stop=(c == len(lhs) - 1))
                last.then_inc(full, 1)

            def norm(n):
                for t in range(TT):
                    pe.wait_ge(norm_rows[n], t + 1)
                    for c in range(2):
                        transposes(f"norm{n}", ("t", t, c),
                                   [xn[:, t % 2, (4 * c + k) * P:(4 * c + k + 1) * P] for k in range(4)])
                for c in range(2):
                    drained(pe, f"norm{n}", ("t", TT - 1, c))

            def xt_tiles(a, w):
                return [xt[:, k, a:a + w] for k in range(DT)]

            pe.wait_ge(ident_set, 2)
            norm(0)
            with pe.Fori(0, RET_HEADS) as h:
                w_qk, w_v, w_g, w_o = w3(0, DT, 512), w3(1, DT, 512), w3(2, DT, 512), w3(3, 4, D)
                for g, (first, n) in enumerate(GROUPS):
                    nt = n // P
                    if g == 0:
                        loaded(pe, "ret", "k", h)
                    for f in range(4):
                        product("ret", ("qk", g, f), [w_qk[:, k, f * P:(f + 1) * P] for k in range(DT)],
                                xt_tiles(first, n), h)
                    if g == 0:
                        loaded(pe, "ret", "v", h)
                    for t in range(nt):
                        product("ret", ("v", g, t), xt_tiles(first + t * P, P), [w_v[:, k, :] for k in range(DT)], h)
                    pe.wait_ge(ret_rot, at(2 * g + 2, 4, h))
                    for t in range(nt):
                        product("ret", ("s", g, t), [r_qk[:, 2 + k, t * P:(t + 1) * P] for k in range(2)],
                                [r_qk[:, k, 0:n] for k in range(2)], h)
                    if g == 0:
                        loaded(pe, "ret", "g", h)
                    for t in range(nt + 1):
                        if t < nt:
                            product("ret", ("g", g, t), xt_tiles(first + t * P, P),
                                    [w_g[:, k, :] for k in range(DT)], h)
                            if t == 0:
                                for k in range(nt):
                                    drained(pe, "ret", ("v", g, k), h)
                                    drained(pe, "ret", ("s", g, k), h)
                            product("ret", ("o", g, t), [r_s[:, k, t * P:(t + 1) * P] for k in range(nt)],
                                    [r_v[:, k, :] for k in range(nt)], h)
                        if t:
                            pe.wait_ge(ret_og, at(first // P + t, TT, h))
                            transposes("ret", ("tr", g, t - 1),
                                       [r_og[:, (t - 1) % 2, k * P:(k + 1) * P] for k in range(4)], h)
                    if g == 0:
                        loaded(pe, "ret", "o", h)
                    for t in range(nt):
                        drained(pe, "ret", ("tr", g, t), h)
                        for f in range(2):
                            product("ret", ("out", g, t, f), [r_ot[:, k, t * P:(t + 1) * P] for k in range(4)],
                                    [w_o[:, k, f * HALF:(f + 1) * HALF] for k in range(4)], h)

            def mixture(l):
                if l == 0:
                    pe.wait_ge(const_in, 6 * 16)
                b, full = fill(pe, f"route{l}", "logit")
                for t in range(TT):
                    for k in range(DT):
                        last = nc.tensor.matmul(b[:, t * EXPERTS:(t + 1) * EXPERTS], xt[:, k, t * P:(t + 1) * P],
                                                rw[:, l, k, :], start=(k == 0), stop=(k == DT - 1))
                last.then_inc(full, 1)
                pe.wait_ge(moe_aff[l], 1)
                for g, (first, n) in enumerate(GROUPS):
                    b, full = fill(pe, f"route{l}", f"aff{g}")
                    for t in range(n // P):
                        last = nc.tensor.transpose(b[0:EXPERTS, t * P:(t + 1) * P], m_af[:, first // P + t, :], ident[:, :])
                    last.then_inc(full, 1)
                pe.wait_ge(moe_top[l], 1)
                for key, src in (("gate", top_v), ("idx", top_f)):
                    b, full = fill(pe, f"route{l}", key)
                    nc.tensor.transpose(b[0:CAP, 0:EXPERTS], src[:, :], ident[0:EXPERTS, 0:EXPERTS]).then_inc(full, 1)

                def rows(phase, e, n):
                    pe.wait_ge(moe_rows[l], at(16, 16, n))
                    for c in range(2):
                        transposes(phase, f"x{c}", [m_x[:, (4 * c + k) * P:(4 * c + k + 1) * P] for k in range(4)],
                                   e, CAP)

                def expert(phase, e, n):
                    m_tiles = [m_xt[:, k, :] for k in range(DT)]
                    for f in range(2):
                        for k, key in enumerate("gu"):
                            loaded(pe, f"moe{l}", 2 * f + k, n)
                            w = w3(2 * f + k, DT, HALF)
                            product(phase, f"{key}{f}", m_tiles, [w[:, j, :] for j in range(DT)], e, CAP)
                    if phase[0] == "m":
                        rows(phase, e, n + 1)
                    for f in range(2):
                        drained(pe, phase, f"u{f}", e)
                        transposes(phase, f"h{f}", [m_hid[:, (4 * f + k) * P:(4 * f + k + 1) * P] for k in range(4)],
                                   e, CAP)
                    for f in range(2):
                        drained(pe, phase, f"h{f}", e)
                    for f in range(2):
                        loaded(pe, f"moe{l}", 4 + f, n)
                        w = w3(4 + f, DT, HALF)
                        product(phase, f"y{f}", [m_hidt[:, j, :] for j in range(DT)], [w[:, j, :] for j in range(DT)],
                                e, CAP)

                rows(f"first{l}", 0, 0)
                for c in range(2):
                    drained(pe, f"first{l}", f"x{c}")
                with pe.Fori(0, EXPERTS - 1) as e:
                    expert(f"moe{l}", e, e)
                expert(f"last{l}", 0, EXPERTS - 1)

            def embedding(l):
                pe.wait_ge(p_in[l], 16 * (ROWS_P + ROWS_S if l == 0 else 2))
                for t in range(TT):
                    transposes(f"ple{l}", ("pt", t), [e_p[:, t, k * P:(k + 1) * P] for k in range(2)])
                for key in ("g0", "g1", "u"):
                    loaded(pe, f"ple{l}", key)
                w_g, w_u = [w3(0, DT, HALF), w3(1, DT, HALF)], w3(2, 2, D)
                for t in range(TT):
                    drained(pe, f"ple{l}", ("pt", t))
                    for f in range(2):
                        product(f"ple{l}", ("g", t, f), xt_tiles(t * P, P), [w_g[f][:, k, :] for k in range(DT)])
                        product(f"ple{l}", ("u", t, f), [e_pt[:, k, t * P:(t + 1) * P] for k in range(2)],
                                [w_u[:, k, f * HALF:(f + 1) * HALF] for k in range(2)])

            norm(1)
            mixture(0)
            norm(2)
            embedding(0)
            norm(3)

            units = na_units()
            with pe.Fori(0, NA_HEADS // QUAD) as q:
                w_qk, w_v = w3(0, DT, 512), w3(1, DT, 256)
                loaded(pe, "na", "k", q)
                for f in range(4):
                    for c, (a, w) in enumerate(((0, 512), (512, 256))):
                        product("na", ("qk", f, c), [w_qk[:, k, f * P:(f + 1) * P] for k in range(DT)], xt_tiles(a, w), q)
                loaded(pe, "na", "v", q)
                for t in range(TT):
                    product("na", ("v", t), xt_tiles(t * P, P), [w_v[:, k, :] for k in range(DT)], q)
                for f in range(4):
                    for c in range(2):
                        drained(pe, "na", ("qk", f, c), q)
                for t in range(TT):
                    drained(pe, "na", ("v", t), q)
                for u in range(len(units) + 2):
                    if u < len(units):
                        t, h = units[u]
                        k0, nk, m0 = NA_KEYS[t]
                        b, full = fill(pe, "na", ("s", u), q)
                        a = h % 2 * NA_DH
                        nc.tensor.matmul(b[:, 0:nk * P], ident16[:, :], mask[:, m0:m0 + nk * P], start=True, stop=False)
                        nc.tensor.matmul(b[:, 0:nk * P], n_qk[a:a + NA_DH, h // 2, t * P:(t + 1) * P],
                                         n_qk[a:a + NA_DH, 2 + h // 2, k0 * P:(k0 + nk) * P],
                                         start=False, stop=True).then_inc(full, 1)
                    if 1 <= u <= len(units):
                        v = u - 1
                        nk = NA_KEYS[units[v][0]][1]
                        pe.wait_ge(na_exp, at(v + 1, len(units), q))
                        transposes("na", ("pt", v), [n_p[:, v % 2, k * P:(k + 1) * P] for k in range(nk)], q)
                    if u >= 2:
                        v = u - 2
                        t, h = units[v]
                        k0, nk, _ = NA_KEYS[t]
                        if h == 0:
                            o_bank, o_full = fill(pe, "na", ("o", t), q)
                        drained(pe, "na", ("pt", v), q)
                        for k in range(nk):
                            last = nc.tensor.matmul(o_bank[:, h * NA_DH:(h + 1) * NA_DH], n_pt[:, v % 2, k * P:(k + 1) * P],
                                                    n_v[:, k0 + k, h * NA_DH:(h + 1) * NA_DH],
                                                    start=(k == 0), stop=(k == nk - 1))
                        if h == QUAD - 1:
                            last.then_inc(o_full, 1)
                            drained(pe, "na", ("o", t), q)
                            transposes("na", ("tr", t), [n_o[:, t % 2, k * P:(k + 1) * P] for k in range(2)], q)
            for f in range(2):
                loaded(pe, "naout", f)
            for t in range(TT):
                if t == 0:
                    drained(pe, "na", ("tr", TT - 1), NA_HEADS // QUAD - 1)
                for f in range(2):
                    product("naout", ("out", t, f), [n_ot[:, k, t * P:(t + 1) * P] for k in range(DT)],
                            [w3(4 + f, DT, HALF)[:, k, :] for k in range(DT)])
            norm(4)
            mixture(1)
            norm(5)
            embedding(1)

        @block.vector
        def _(dve):
            chain = Chain(dve, dve_step)
            v = nc.vector

            def norm(n):
                dve.wait_ge(gain_in[n % 2], 16 * (n // 2 + 1))
                for t in range(TT + 1):
                    if t < TT:
                        dve.wait_ge(norm_rs[n], t + 1)
                        v.scalar_tensor_tensor(out=xn[:, t % 2, :], in0=resid[:, t, :], scalar=rstd[:, t:t + 1],
                                               in1=gain[:, n % 2, :], op0=ALU.mult, op1=ALU.mult)\
                            .then_inc(norm_rows[n], 1)
                    if t and n < 6:
                        b, done = filled(dve, f"norm{n}", ("t", t - 1, 1))
                        v.tensor_copy(xt[:, 4:8, (t - 1) * P:t * P],
                                      b[:, :].rearrange("p (f n) -> p f n", f=4)).then_inc(done, 1)

            dve.wait_ge(const_in, 6 * 16)
            x, ax, y, s, s2, p = (lgt[:, k, :] for k in range(6))
            chain.link(v.tensor_scalar(ax, x, -1.0, None, ALU.mult))
            v.tensor_tensor(ax, ax, x, ALU.max).then_inc(decay_abs, 1)
            norm(0)
            dve.wait_ge(decay_exp, 1)
            chain.link(v.tensor_scalar(s2, y, 2.0, None, ALU.add))
            chain.link(v.reciprocal(p, s2))
            chain.link(v.tensor_tensor(s, p, y, ALU.mult))
            chain.link(v.tensor_tensor(s2, s, s, ALU.mult))
            chain.link(v.tensor_scalar(p, s2, 1.0 / 19, None, ALU.mult))
            for k in range(17, 1, -2):
                chain.link(v.scalar_tensor_tensor(out=p, in0=p, scalar=1.0 / k, in1=s2, op0=ALU.add, op1=ALU.mult))
            chain.link(v.scalar_tensor_tensor(out=p, in0=p, scalar=1.0, in1=s, op0=ALU.add, op1=ALU.mult))
            chain.link(v.tensor_scalar(s, x, 0.0, None, ALU.min))
            chain.link(v.scalar_tensor_tensor(out=lg[:], in0=p, scalar=-2.0, in1=s, op0=ALU.mult, op1=ALU.add))
            dve.wait_ge(gn_in, 16)

            with dve.Fori(0, RET_HEADS) as h:
                chain.enter(h, 2 + 2 * 6 + TT * 2)
                flat = r_tmp.rearrange("p f n -> p (f n)")
                a, b2 = flat[:, 0:STRIP], flat[:, STRIP:2 * STRIP]
                chain.link(v.tensor_scalar(a, r_diff, 0.0, lg[:, bass.ds(h, 1)], ALU.max, ALU.mult))
                chain.link(v.tensor_scalar(b2, r_diff, 0.0, lg[:, bass.ds(h + RET_HEADS, 1)], ALU.min, ALU.mult))
                v.tensor_tensor(r_strip, a, b2, ALU.subtract).then_inc(strip_arg, 1)
                dve.wait_ge(strip_arg, h + 1)
                for g, (first, n) in enumerate(GROUPS):
                    nt = n // P
                    for j in range(2):
                        t0, t1, t2, t3 = (r_tmp[:, k, 0:n] for k in range(4))
                        b, done = filled(dve, "ret", ("qk", g, 2 * j), h)
                        chain.link(v.tensor_tensor(t0, b[:, 0:n], cos_t[:, 0:n], ALU.mult))
                        v.tensor_tensor(t2, b[:, 0:n], sin_t[:, 0:n], ALU.mult).then_inc(done, 1)
                        b, done = filled(dve, "ret", ("qk", g, 2 * j + 1), h)
                        chain.link(v.tensor_tensor(t1, b[:, 0:n], sin_t[:, 0:n], ALU.mult))
                        v.tensor_tensor(t3, b[:, 0:n], cos_t[:, 0:n], ALU.mult).then_inc(done, 1)
                        chain.link(v.tensor_tensor(r_qk[:, 2 * j, 0:n], t0, t1, ALU.subtract))
                        drained(dve, "ret", ("qk", g, 2 * j + 1), h)
                        v.tensor_tensor(r_qk[:, 2 * j + 1, 0:n], t2, t3, ALU.add).then_inc(ret_rot, 1)
                        dve.wait_ge(ret_rot, at(2 * g + j + 1, 4, h))
                    if g == 0:
                        dve.wait_ge(strip_set, h + 1)
                    for t in range(nt):
                        b, done = filled(dve, "ret", ("s", g, t), h)
                        v.scalar_tensor_tensor(out=r_s[:, t, 0:n], in0=b[:, 0:n], scalar=RET_DK ** -0.5,
                                               in1=r_strip[:, STRIP0 - t * P:STRIP0 - t * P + n],
                                               op0=ALU.mult, op1=ALU.mult).then_inc(done, 1)
                    for t in range(nt):
                        k = first // P + t
                        b, done = filled(dve, "ret", ("o", g, t), h)
                        chain.link(v.bn_stats(stats[:], b[:, :]))
                        hold(dve)
                        v.bn_aggr(mv[:, k % 2, :], stats[:]).then_inc(ret_var, 1)
                        drained(dve, "ret", ("g", g, t), h)
                        chain.link(v.tensor_tensor(r_silu[:, t % 2, :], r_silu[:, t % 2, :],
                                                   r_gn[:, bass.ds(h * 512, 512)], ALU.mult))
                        dve.wait_ge(ret_rstd, at(k + 1, TT, h))
                        v.tensor_scalar(r_og[:, t % 2, :], b[:, :], mv[:, k % 2, 0:1], mvr[:, k % 2:k % 2 + 1],
                                        ALU.subtract, ALU.mult).then_inc(done, 1)
                        drained(dve, "ret", ("o", g, t), h)
                        v.tensor_tensor(r_og[:, t % 2, :], r_og[:, t % 2, :], r_silu[:, t % 2, :], ALU.mult)\
                            .then_inc(ret_og, 1)
                    for t in range(nt):
                        for f in range(2):
                            b, done = filled(dve, "ret", ("out", g, t, f), h)
                            k = first // P + t
                            r = resid[:, k, f * HALF:(f + 1) * HALF]
                            v.tensor_tensor(r, r, b[:, :], ALU.add).then_inc(done, 1)
                chain.leave(RET_HEADS)

            def mixture(l, order):
                smax, ssum, srec = rsm[:, 0, 0:TT], rsm[:, 1, 0:TT], rsm[:, 2, 0:TT]

                def wide(x):
                    return x.rearrange("p (t a) -> p t a", a=1).broadcast_to([P, TT, EXPERTS])

                b, done = filled(dve, f"route{l}", "logit")
                logits = b[:, 0:TT * EXPERTS].rearrange("p (t e) -> p t e", t=TT)
                chain.link(v.tensor_reduce(smax, logits, AX_X, ALU.max))
                v.tensor_tensor(m_lg, logits, wide(smax), ALU.subtract).then_inc(done, 1)
                dve.wait_ge(moe_exp[l], 1)
                chain.link(v.tensor_reduce(ssum, m_ex, AX_X, ALU.add))
                chain.link(v.reciprocal(srec, ssum))
                v.tensor_tensor(m_af, m_ex, wide(srec), ALU.mult).then_inc(moe_aff[l], 1)
                for g, (first, n) in enumerate(GROUPS):
                    b, done = filled(dve, f"route{l}", f"aff{g}")
                    dst, src = m_aff[:, first:first + n], b[0:EXPERTS, 0:n]
                    if order:
                        rows, cols = ((ROWS_P, COLS_P), (ROWS_S, COLS_S))[g]
                        dst = dst.rearrange("e (r t c) -> e t r c", r=rows, c=cols)
                        src = src.rearrange("e (t r c) -> e t r c", r=rows, c=cols)
                    for t in range(n // P if order else 1):
                        last = v.tensor_copy(dst[:, t] if order else dst, src[:, t] if order else src)
                    last.then_inc(done, 1)
                drained(dve, f"route{l}", "aff1")
                drained(dve, f"route{l}", "aff0")
                c0 = 0
                for (first, n), cap in zip(GROUPS, (CAP_P, CAP_S)):
                    a = m_aff[:, first:first + n]
                    for c in range(c0, c0 + cap, 8):
                        chain.link(v.max(out=top_v[:, c:c + 8], in_=a))
                        chain.link(v.max_index(out=top_i[:, c:c + 8], in_max=top_v[:, c:c + 8], in_values=a))
                        chain.link(v.match_replace(out=a, in_to_replace=top_v[:, c:c + 8], in_values=a, imm_value=-1.0))
                    c0 += cap
                chain.link(v.tensor_copy(top_f[:], top_i[:]))
                v.tensor_scalar(top_f[:, CAP_P:CAP], top_f[:, CAP_P:CAP], float(SEQ_P), None, ALU.add)\
                    .then_inc(moe_top[l], 1)
                for key, dst in (("gate", gate_t), ("idx", idx_t)):
                    b, done = filled(dve, f"route{l}", key)
                    v.tensor_copy(dst[:, :], b[0:CAP, 0:EXPERTS]).then_inc(done, 1)

                def expert(phase, e, n):
                    for f in range(2):
                        drained(dve, phase, f"g{f}", e)
                        b, done = filled(dve, phase, f"u{f}", e)
                        v.tensor_tensor(m_hid[:, f * HALF:(f + 1) * HALF], m_silu[:, f, :], b[0:CAP, :], ALU.mult)\
                            .then_inc(done, 1)
                    for f in range(2):
                        b, done = filled(dve, phase, f"y{f}", e)
                        if f == 0:
                            dve.wait_ge(moe_y_free[l], n + 1)
                        v.tensor_scalar(m_y[:, f * HALF:(f + 1) * HALF], b[0:CAP, :], gate_t[:, bass.ds(n, 1)], None,
                                        ALU.mult).then_inc(done, 1)

                with dve.Fori(0, EXPERTS - 1) as e:
                    expert(f"moe{l}", e, e)
                expert(f"last{l}", 0, EXPERTS - 1)

            def embedding(l):
                for t in range(TT):
                    for f in range(2):
                        drained(dve, f"ple{l}", ("g", t, f))
                        if t:
                            dve.wait_ge(ple_add[l], 2 * t - 1 + f)
                        b, done = filled(dve, f"ple{l}", ("u", t, f))
                        v.tensor_tensor(e_prod[:, f, :], e_sig[:, f, :], b[:, :], ALU.mult).then_inc(done, 1)
                        drained(dve, f"ple{l}", ("u", t, f))
                        r = resid[:, t, f * HALF:(f + 1) * HALF]
                        v.tensor_tensor(r, r, e_prod[:, f, :], ALU.add).then_inc(ple_add[l], 1)

            norm(1)
            mixture(0, 0)
            norm(2)
            embedding(0)
            norm(3)

            units = na_units()
            with dve.Fori(0, NA_HEADS // QUAD) as q:
                chain.enter(q, len(units) + TT)
                for f in range(2, 4):
                    for c, (a, w) in enumerate(((0, 512), (512, 256))):
                        b, done = filled(dve, "na", ("qk", f, c), q)
                        v.tensor_copy(n_qk[:, f, a:a + w], b[:, 0:w]).then_inc(done, 1)
                for t in range(1, TT, 2):
                    b, done = filled(dve, "na", ("v", t), q)
                    v.tensor_copy(n_v[:, t, :], b[:, 0:256]).then_inc(done, 1)
                dve.wait_ge(na_bias, at(16 * (ROWS_P + ROWS_S), 16 * (ROWS_P + ROWS_S), q))
                for u in range(len(units) + 2):
                    if u < len(units):
                        t, h = units[u]
                        k0, nk, _ = NA_KEYS[t]
                        rows, cols, wide_, lo = ((ROWS_P, COLS_P, WIDE_P, 8 * WIDE_S) if t < 2
                                                 else (ROWS_S, COLS_S, WIDE_S, 0))
                        bb = bias[:, h, lo:lo + rows * wide_].rearrange("p (r k c) -> p k r c", r=rows, c=cols)
                        rel = k0 - t + 1
                        b, done = filled(dve, "na", ("s", u), q)
                        if u >= 2:
                            dve.wait_ge(na_exp, at(u - 1, len(units), q))
                        scored = n_s[:, u % 2, 0:nk * P].rearrange("p (k r c) -> p k r c", k=nk, c=cols)
                        scores = b[:, 0:nk * P].rearrange("p (k r c) -> p k r c", k=nk, c=cols)
                        v.tensor_tensor(scored, scores, bb[:, rel:rel + nk], ALU.add).then_inc(done, 1)
                        drained(dve, "na", ("s", u), q)
                        chain.link(v.tensor_reduce(mx[:, u % 2:u % 2 + 1], n_s[:, u % 2, 0:nk * P], AX_X, ALU.max))
                        v.tensor_scalar(nmx[:, u % 2:u % 2 + 1], mx[:, u % 2:u % 2 + 1], -1.0, None, ALU.mult)\
                            .then_inc(na_max, 1)
                    if 1 <= u <= len(units) and (u - 1) % 2 == 1:
                        w = NA_KEYS[units[u - 1][0]][1] * P
                        b, done = filled(dve, "na", ("pt", u - 1), q)
                        v.tensor_copy(n_pt[:, 1, 0:w], b[:, 0:w]).then_inc(done, 1)
                    if u >= 2 and units[u - 2][1] == QUAD - 1:
                        t = units[u - 2][0]
                        b, done = filled(dve, "na", ("o", t), q)
                        chain.link(v.reciprocal(rden[:], den[:, t % 2, :]))
                        v.tensor_tensor(n_o[:, t % 2, :].rearrange("p (h d) -> p h d", h=QUAD),
                                        b[:, 0:256].rearrange("p (h d) -> p h d", h=QUAD),
                                        rden[:].rearrange("p (h a) -> p h a", a=1).broadcast_to([P, QUAD, NA_DH]),
                                        ALU.mult).then_inc(done, 1)
                chain.leave(NA_HEADS // QUAD)
            for t in range(TT):
                for f in range(2):
                    b, done = filled(dve, "naout", ("out", t, f))
                    r = resid[:, t, f * HALF:(f + 1) * HALF]
                    v.tensor_tensor(r, r, b[:, :], ALU.add).then_inc(done, 1)
            norm(4)
            mixture(1, 1)
            norm(5)
            embedding(1)
            norm(6)


def shape_constants():
    half = RET_DK // 2
    inv = np.float32(10000.0) ** (-np.arange(0, RET_DK, 2, dtype=np.float32) / np.float32(RET_DK))
    ang = inv.astype(np.float32)[:, None] * np.arange(SEQ_S, dtype=np.float32)[None, :]
    diff = np.arange(STRIP, dtype=np.float32)[None, :] - STRIP0 - np.arange(P, dtype=np.float32)[:, None]

    def window(rows, cols, tile, first, n):
        q = tile * cols + np.tile(np.arange(cols), rows)
        k = np.concatenate([(first + j) * cols + np.tile(np.arange(cols), rows) for j in range(n)])
        start = np.clip(q - NA_WIN // 2, 0, GRID_W - NA_WIN)
        ok = (k[None, :] >= start[:, None]) & (k[None, :] < start[:, None] + NA_WIN)
        return np.where(ok, 0.0, MASKED)

    mask = np.concatenate([window(ROWS_P, COLS_P, 0, 0, 2), window(ROWS_P, COLS_P, 1, 0, 2),
                           window(ROWS_S, COLS_S, 0, 0, 2), window(ROWS_S, COLS_S, 1, 0, 3),
                           window(ROWS_S, COLS_S, 3, 2, 2)], axis=1)
    assert mask.shape[1] == MASK_W and half == P
    mask_bits = (np.ascontiguousarray(mask, dtype=np.float32).view(np.uint32) >> 16).astype(np.uint16)
    return {"rope_cos": np.cos(ang).astype(np.float32), "rope_sin": np.sin(ang).astype(np.float32),
            "row_minus_col": diff.astype(np.float32), "col_mask": mask_bits}


_INS = ["x_prompt", "x_sample", "p_prompt", "p_sample", "ret_w_in", "ret_decay_logit", "ret_gn_w", "ret_w_out",
        "na_w_in", "na_rpb", "na_w_out", "mix_norm", "ffn_norm", "ple_norm", "router_w", "exp_w_gate", "exp_w_up",
        "exp_w_down", "ple_w_up", "ple_w_gate", "final_norm"]


def kernel(**inputs):
    import concourse.bacc as bacc
    from concourse.bass_utils import run_bass_kernel_spmd

    nc = bacc.Bacc("TRN2", target_bir_lowering=False, num_devices=1)
    arrays, args = {}, []
    given = {name: np.ascontiguousarray(inputs[name]) for name in _INS}
    given["na_rpb"] = np.pad(given["na_rpb"].reshape(-1), RPB_PAD)
    given.update(shape_constants())
    for name, a in given.items():
        arrays[f"in_{name}"] = a
        args.append(nc.dram_tensor(f"in_{name}", a.shape, mybir.dt.from_np(a.dtype), kind="ExternalInput").ap())
    for name, rows in (("y_prompt", SEQ_P), ("y_sample", SEQ_S)):
        args.append(nc.dram_tensor(name, (1, rows, D), F32, kind="ExternalOutput").ap())
    build(nc, *args)
    r = run_bass_kernel_spmd(nc, [arrays], core_ids=[0])
    return r.results[0]["y_prompt"], r.results[0]["y_sample"]
```

```python
from contextlib import ExitStack

import numpy as np
import concourse.bass as bass
from concourse import mybir

ALU = mybir.AluOpType
ACT = mybir.ActivationFunctionType
AX_X = mybir.AxisListType.X
F32 = mybir.dt.float32
F32R = mybir.dt.float32r
BF16 = mybir.dt.bfloat16
U32 = mybir.dt.uint32

P = 128
D = 1024
DT = D // P
SEQ_P, SEQ_S = 256, 512
TOK = SEQ_P + SEQ_S
TT = TOK // P
GROUPS = [(0, SEQ_P), (SEQ_P, SEQ_S)]
HALF = 512
EPS = 1e-6

RET_HEADS, RET_DK, RET_DV = 4, 256, 512
STRIP = SEQ_S + SEQ_S - P
STRIP0 = SEQ_S - P

GRID_W = 64
NA_HEADS, NA_DH = 16, 64
QUAD = 4
ROWS_P, ROWS_S = SEQ_P // GRID_W, SEQ_S // GRID_W
COLS_P, COLS_S = P // ROWS_P, P // ROWS_S
NA_WIN = 16
RPB_A, RPB_B = 15, 31
RPB_PAD = 64
WIDE_S, WIDE_P = 3 * COLS_S, 3 * COLS_P
A_P = 2 * ROWS_P - 1
A0_P = RPB_A // 2 - (ROWS_P - 1)

EXPERTS = 16
CAP_P, CAP_S = 2 * SEQ_P // EXPERTS, 2 * SEQ_S // EXPERTS
CAP = CAP_P + CAP_S
PLE = 256
MASKED = -1e30

MOE_USES = ["g0", "u0", "g1", "u1", "y0", "y1"]

NA_KEYS = [(0, 2, 0), (0, 2, 256), (2, 2, 512), (2, 3, 768), (3, 3, 768), (4, 2, 1152)]
MASK_W = 1408


def at(base, per, i):
    return base + i * per if per else base


class Plan:

    def __init__(self, n):
        self.count = [0] * n
        self.where = {}

    def add(self, phase, keys, passes=1):
        places = [place for _, place in keys]
        local = {}
        for key, place in keys:
            local[place] = local.get(place, 0) + 1
            per = places.count(place) if passes > 1 else 0
            self.where[phase, key] = (place, self.count[place] + local[place], per)
        for place, n in local.items():
            self.count[place] += n * passes

    def get(self, phase, key, i):
        place, first, per = self.where[phase, key]
        return place, first, per, at(first, per, i)


class Chain:

    def __init__(self, eng, sem):
        self.eng, self.sem, self.base, self.local, self.i, self.per = eng, sem, 0, 0, 0, 0

    def link(self, ins):
        ins.then_inc(self.sem, 1)
        self.local += 1
        self.eng.wait_ge(self.sem, at(self.base + self.local, self.per, self.i))

    def enter(self, i, per):
        self.base += self.local
        self.local, self.i, self.per = 0, i, per

    def leave(self, passes):
        assert self.local == self.per, (self.local, self.per)
        self.base += self.per * passes
        self.local, self.i, self.per = 0, 0, 0


def psum_keys(keys):
    return [(k, n % 8) for n, k in enumerate(keys)]


def ret_keys():
    keys = []
    for g, (_, n) in enumerate(GROUPS):
        nt = n // P
        keys += [("qk", g, f) for f in range(4)] + [("v", g, t) for t in range(nt)]
        keys += [("s", g, t) for t in range(nt)]
        for t in range(nt):
            keys += [("g", g, t), ("o", g, t)]
            if t:
                keys.append(("tr", g, t - 1))
        keys.append(("tr", g, nt - 1))
        keys += [("out", g, t, h) for t in range(nt) for h in range(2)]
    return keys


def na_units():
    return [(t, h) for t in range(TT) for h in range(QUAD)]


def na_keys():
    keys = [("qk", f, n) for f in range(4) for n in range(2)] + [("v", t) for t in range(TT)]
    units = na_units()
    for u in range(len(units) + 2):
        if u < len(units):
            keys.append(("s", u))
        if 1 <= u <= len(units):
            keys.append(("pt", u - 1))
        if u >= 2:
            if units[u - 2][1] == 0:
                keys.append(("o", units[u - 2][0]))
            if units[u - 2][1] == QUAD - 1:
                keys.append(("tr", units[u - 2][0]))
    place = {"qk": [0, 1, 2, 3, 4, 5, 6, 7], "v": [0, 1, 2, 3, 4, 5], "s": [0, 1, 2], "pt": [3, 4],
             "o": [5, 6], "tr": [7]}
    seen = {}
    out = []
    for k in keys:
        n = seen.get(k[0], 0)
        seen[k[0]] = n + 1
        out.append((k, place[k[0]][n % len(place[k[0]])]))
    return out


def build(nc, x_prompt, x_sample, p_prompt, p_sample, ret_w_in, ret_decay_logit, ret_gn_w, ret_w_out,
          na_w_in, na_rpb_padded, na_w_out, mix_norm, ffn_norm, ple_norm, router_w, exp_w_gate, exp_w_up,
          exp_w_down, ple_w_up, ple_w_gate, final_norm, rope_cos, rope_sin, row_minus_col, col_mask,
          y_prompt, y_sample):
    ctx = ExitStack()
    with ctx:
        def sb(name, shape, dt=F32):
            return ctx.enter_context(nc.sbuf_tensor(name, shape, dt))

        def sem(name):
            return ctx.enter_context(nc.semaphore(name))

        rows_normed = [nc.dram_tensor(f"rows_normed{l}", [TOK, D], F32, kind="Internal").ap() for l in range(2)]
        rows_summed = [nc.dram_tensor(f"rows_summed{l}", [TOK, D], F32, kind="Internal").ap() for l in range(2)]
        bias_s = nc.dram_tensor("bias_s", [COLS_S, NA_HEADS, RPB_A, WIDE_S], F32, kind="Internal").ap()
        bias_p = nc.dram_tensor("bias_p", [COLS_P, NA_HEADS, A_P, WIDE_P], F32, kind="Internal").ap()

        KB = 1024
        arena = nc.sbuf_base + (-nc.sbuf_base) % 64
        sb("arena", [P, (arena - nc.sbuf_base + 200 * KB) // 4])

        def put(name, shape, at_kb, dt=F32):
            return nc.alloc_sbuf_tensor_at(name, shape, dt, offset=arena + at_kb * KB)

        wt = put("wt", [P, 6, 4096], 0)
        xt = put("xt", [P, DT, TOK], 96)
        resid = put("resid", [P, TT, D], 120)
        w_parts = put("w_parts", [P, 3, 2, 2048], 96, F32R)
        work = put("work", [P, 6144], 144)
        xn = put("xn", [P, 2, D], 168)
        bias = put("bias", [P, QUAD, 8 * WIDE_S + 4 * WIDE_P], 176)
        cos_t = put("cos_t", [P, SEQ_S], 188)
        sin_t = put("sin_t", [P, SEQ_S], 190)
        xn_all = put("xn_all", [P, TT, D], 168)
        m_xt = [put(f"m_xt{k}", [P, DT, CAP], 176 + 3 * k, F32R) for k in range(2)]
        m_hidt = [put(f"m_hidt{k}", [P, DT, CAP], 182 + 3 * k, F32R) for k in range(2)]
        gain = put("gain", [P, 2, D], 192)
        ident = sb("ident", [P, P])
        ident16 = sb("ident16", [P, P], BF16)
        mask = sb("mask", [P, MASK_W], BF16)
        rw = sb("rw", [P, 2, DT, EXPERTS])
        sumsq = sb("sumsq", [P, 8])
        meansq = sb("meansq", [P, 8])
        rstd = sb("rstd", [P, 8])
        minus_half = sb("minus_half", [P, 8])
        lg = sb("lg", [P, 2 * RET_HEADS])
        lgt = sb("lgt", [P, 8, 8])
        stats = sb("stats", [P, 6])
        mv = sb("mv", [P, 2, 2])
        mvr = sb("mvr", [P, 2])
        top_v = sb("top_v", [EXPERTS, CAP])
        top_i = sb("top_i", [EXPERTS, CAP], U32)
        top_f = sb("top_f", [EXPERTS, CAP])
        gate_t = sb("gate_t", [CAP, EXPERTS])
        idx_t = sb("idx_t", [CAP, EXPERTS], U32)
        idx_in = sb("idx_in", [CAP, 1], U32)
        idx_out = sb("idx_out", [CAP, 1], U32)
        rsm = sb("rsm", [P, 4, 8])
        mx = sb("mx", [P, 2])
        nmx = sb("nmx", [P, 2])
        den = sb("den", [P, 2, QUAD])
        rden = sb("rden", [P, QUAD])

        bank = [ctx.enter_context(nc.psum_tensor(f"bank{b}", [P, HALF], F32)) for b in range(8)]

        psum, slot = Plan(8), Plan(6)
        norm_uses = [(("t", t, c), (2 * t + c) % 8) for t in range(TT) for c in range(2)]
        moe_uses = [("g0", 0), ("u0", 1), ("g1", 2), ("u1", 3), ("x0", 4), ("x1", 5), ("h0", 6), ("h1", 7),
                    ("y0", 4), ("y1", 5)]

        def plan_moe(l):
            psum.add(f"route{l}", [("logit", 0), ("aff0", 1), ("aff1", 2), ("gate", 3), ("idx", 4)])
            psum.add(f"first{l}", [("x0", 4), ("x1", 5)])
            psum.add(f"moe{l}", moe_uses, EXPERTS - 1)
            psum.add(f"last{l}", [(k, b) for k, b in moe_uses if k[0] != "x"])

        def plan_ple(l):
            psum.add(f"ple{l}", psum_keys([("pt", t) for t in range(TT)]
                                          + [(k, t, h) for t in range(TT) for h in range(2) for k in "gu"]))

        psum.add("norm0", norm_uses)
        psum.add("ret", psum_keys(ret_keys()), RET_HEADS)
        psum.add("norm1", norm_uses)
        plan_moe(0)
        psum.add("norm2", norm_uses)
        plan_ple(0)
        psum.add("norm3", norm_uses)
        psum.add("na", na_keys(), NA_HEADS // QUAD)
        psum.add("naout", psum_keys([("out", t, h) for t in range(TT) for h in range(2)]))
        psum.add("norm4", norm_uses)
        plan_moe(1)
        psum.add("norm5", norm_uses)
        plan_ple(1)

        slot.add("ret", [("q", 0), ("k", 0), ("v", 1), ("g", 2), ("o", 3)], RET_HEADS)
        slot.add("moe0", [(s, s) for s in range(6)], EXPERTS)
        slot.add("ple0", [("g0", 0), ("g1", 1), ("u", 2)])
        slot.add("na", [("q", 0), ("k", 0), ("v", 1)], NA_HEADS // QUAD)
        slot.add("naout", [(0, 4), (1, 5)])
        slot.add("moe1", [(s, s) for s in range(6)], EXPERTS)
        slot.add("ple1", [("g0", 0), ("g1", 1), ("u", 2)])

        bank_full = [sem(f"bank_full{b}") for b in range(8)]
        bank_free = [sem(f"bank_free{b}") for b in range(8)]
        slot_full = [sem(f"slot_full{s}") for s in range(6)]
        dve_step, pool_step = sem("dve_step"), sem("pool_step")
        held = sem("held")
        x_in = [sem(f"x_in{g}") for g in range(2)]
        const_in, bias_table, gn_in, ident_set = sem("const_in"), sem("bias_table"), sem("gn_in"), sem("ident_set")
        gain_in = [sem(f"gain_in{b}") for b in range(2)]
        norm_sq = [sem(f"norm_sq{n}") for n in range(7)]
        norm_rs = [sem(f"norm_rs{n}") for n in range(7)]
        norm_rows = [sem(f"norm_rows{n}") for n in range(7)]
        rows_out = [sem(f"rows_out{l}") for l in range(2)]
        final_out = [sem(f"final_out{b}") for b in range(2)]
        decay_abs, decay_exp = sem("decay_abs"), sem("decay_exp")
        strip_arg, strip_set = sem("strip_arg"), sem("strip_set")
        ret_rot = sem("ret_rot")
        ret_var, ret_rstd, ret_og = sem("ret_var"), sem("ret_rstd"), sem("ret_og")
        moe_exp = [sem(f"moe_exp{l}") for l in range(2)]
        moe_aff = [sem(f"moe_aff{l}") for l in range(2)]
        moe_top = [sem(f"moe_top{l}") for l in range(2)]
        moe_rows = [sem(f"moe_rows{l}") for l in range(2)]
        moe_wh = [sem(f"moe_wh{l}") for l in range(2)]
        moe_wl = [sem(f"moe_wl{l}") for l in range(2)]
        moe_wused = [sem(f"moe_wused{l}") for l in range(2)]
        moe_th = [sem(f"moe_th{l}") for l in range(2)]
        moe_added = [sem(f"moe_added{l}") for l in range(2)]
        moe_y_free = [sem(f"moe_y_free{l}") for l in range(2)]
        resid_saved = [sem(f"resid_saved{l}") for l in range(2)]
        resid_in = [sem(f"resid_in{l}") for l in range(2)]
        p_in = [sem(f"p_in{l}") for l in range(2)]
        ple_add = [sem(f"ple_add{l}") for l in range(2)]
        na_bias, na_max, na_exp = sem("na_bias"), sem("na_max"), sem("na_exp")

        def fill(pe, phase, key, i=0):
            b, first, per, _ = psum.get(phase, key, i)
            if first > 1 or per:
                pe.wait_ge(bank_free[b], at(first - 1, per, i))
            return bank[b], bank_full[b]

        def filled(eng, phase, key, i=0):
            b, _, _, n = psum.get(phase, key, i)
            eng.wait_ge(bank_full[b], n)
            return bank[b], bank_free[b]

        def matmuls_done(eng, phase, key, i=0):
            b, _, _, n = psum.get(phase, key, i)
            eng.wait_ge(bank_full[b], n)

        def drained(eng, phase, key, i=0):
            b, _, _, n = psum.get(phase, key, i)
            eng.wait_ge(bank_free[b], n)

        def split_done(eng, l, s, e):
            eng.wait_ge(moe_wl[l], at(2 * s + 2, 12, e))

        def parts_free(eng, l, c, phase, e):
            c = c - 3
            if c % 2 == 0:
                eng.wait_ge(moe_wused[l], at(c // 2 + 1, 6, e))
            else:
                matmuls_done(eng, phase, MOE_USES[c // 2], e if phase[0] == "m" else 0)

        def hold(eng):
            eng.sem_inc(held, 1)

        def loaded(pe, phase, key, i=0):
            s, first, per, _ = slot.get(phase, key, i)
            pe.wait_ge(slot_full[s], at(16 * first, 16 * per, i))

        def w3(s, a, b):
            return wt[:, s, 0:a * b].rearrange("p (a b) -> p a b", a=a)

        big = wt[:, 4:6, :].rearrange("p s n -> p (s n)")
        r_qk = big[:, 0:2048].rearrange("p (f n) -> p f n", f=4)
        r_v = big[:, 2048:4096].rearrange("p (t n) -> p t n", t=4)
        r_s = big[:, 4096:6144].rearrange("p (t n) -> p t n", t=4)
        r_ot = big[:, 6144:8192].rearrange("p (f n) -> p f n", f=4)
        r_diff, r_strip = work[:, 0:STRIP], work[:, STRIP:2 * STRIP]
        o = 2 * STRIP
        r_tmp = work[:, o:o + 2048].rearrange("p (f n) -> p f n", f=4)
        r_og = work[:, o + 2048:o + 3072].rearrange("p (f n) -> p f n", f=2)
        r_silu = work[:, o + 3072:o + 4096].rearrange("p (f n) -> p f n", f=2)
        r_gn = xn[:, :, :].rearrange("p a n -> p (a n)")
        m_x = work[0:CAP, 0:1024]
        m_silu = work[0:CAP, 1792:2816].rearrange("p (f n) -> p f n", f=2)
        m_hid = work[0:CAP, 2816:3840]
        m_y = work[0:CAP, 4608:5632]
        m_aff = work[0:EXPERTS, 4608:4608 + TOK]
        m_lg = work[:, 5632:5632 + TT * EXPERTS].rearrange("p (t e) -> p t e", t=TT)
        m_ex = work[:, 5760:5760 + TT * EXPERTS].rearrange("p (t e) -> p t e", t=TT)
        m_af = work[:, 5888:5888 + TT * EXPERTS].rearrange("p (t e) -> p t e", t=TT)
        e_p = work[:, 0:1536].rearrange("p (t n) -> p t n", t=TT)
        e_pt = work[:, 1536:3072].rearrange("p (f n) -> p f n", f=2)
        e_sig = work[:, 3072:4096].rearrange("p (f n) -> p f n", f=2)
        e_prod = work[:, 4096:5120].rearrange("p (f n) -> p f n", f=2)
        nbig = wt[:, 2:4, :].rearrange("p s n -> p (s n)")
        n_qk = nbig[:, 0:3072].rearrange("p (f n) -> p f n", f=4)
        n_v = nbig[:, 3072:4608].rearrange("p (t n) -> p t n", t=TT)
        n_s = nbig[:, 4608:5376].rearrange("p (t n) -> p t n", t=2)
        n_p = nbig[:, 5376:6144].rearrange("p (t n) -> p t n", t=2)
        n_pt = nbig[:, 6144:6912].rearrange("p (t n) -> p t n", t=2)
        n_o = nbig[:, 6912:7424].rearrange("p (t n) -> p t n", t=2)
        n_ot = work[:, :].rearrange("p (f n) -> p f n", f=DT)

        def natural_rows(src_p, src_s, tiles):
            return [(src_p.rearrange("(t p) d -> p t d", p=P), tiles[:, 0:2, :]),
                    (src_s.rearrange("(t p) d -> p t d", p=P), tiles[:, 2:TT, :])]

        def grid_rows(src_p, src_s, tiles):
            out = []
            for r in range(ROWS_P):
                out.append((src_p[r * GRID_W:(r + 1) * GRID_W, :].rearrange("(t c) d -> c t d", c=COLS_P),
                            tiles[r * COLS_P:(r + 1) * COLS_P, 0:2, :]))
            for r in range(ROWS_S):
                out.append((src_s[r * GRID_W:(r + 1) * GRID_W, :].rearrange("(t c) d -> c t d", c=COLS_S),
                            tiles[r * COLS_S:(r + 1) * COLS_S, 2:TT, :]))
            return out

        def normed(n, t):
            return xn_all[:, t, :] if n in (1, 4) else xn[:, t % 2, :]

        def row_dmas(order):
            return ROWS_P + ROWS_S if order else 2

        block = ctx.enter_context(nc.Block())

        @block.sync
        def _(sp):
            sp.dma_start(resid[:, 0:2, :], x_prompt[0].rearrange("(t p) d -> p t d", p=P)).then_inc(x_in[0], 16)
            sp.dma_start(resid[:, 2:TT, :], x_sample[0].rearrange("(t p) d -> p t d", p=P)).then_inc(x_in[1], 16)

            def columns(w, first, n):
                return w.rearrange("(t p) f -> p t f", p=P)[:, :, bass.ds(first, n)]

            def halves(w):
                return [columns(w, f * HALF, HALF) for f in range(2)]

            def ret_loads(h, again):
                if again:
                    matmuls_done(sp, "ret", ("qk", 1, 3), h - 1)
                q_k = w3(0, DT, 512)
                sp.dma_start(q_k[:, :, 0:256], columns(ret_w_in[0], h * 256, 256)).then_inc(slot_full[0], 16)
                sp.dma_start(q_k[:, :, 256:512], columns(ret_w_in[0], h * 256 + D, 256)).then_inc(slot_full[0], 16)
                if again:
                    matmuls_done(sp, "ret", ("v", 1, 3), h - 1)
                sp.dma_start(w3(1, DT, 512), columns(ret_w_in[0], h * 512 + 2 * D, 512)).then_inc(slot_full[1], 16)
                if again:
                    matmuls_done(sp, "ret", ("g", 1, 3), h - 1)
                sp.dma_start(w3(2, DT, 512), columns(ret_w_in[0], h * 512 + 4 * D, 512)).then_inc(slot_full[2], 16)
                if again:
                    matmuls_done(sp, "ret", ("out", 1, 3, 1), h - 1)
                sp.dma_start(w3(3, 4, D), ret_w_out[0].rearrange("(t p) f -> p t f", p=P)[:, bass.ds(h * 4, 4), :])\
                    .then_inc(slot_full[3], 16)

            ret_loads(0, False)
            with sp.Fori(1, RET_HEADS) as h:
                ret_loads(h, True)

            def shifted(first, n_a, wide):
                v = na_rpb_padded[bass.ds(first, 64)]
                return bass.AP(tensor=v.tensor, offset=v.offset,
                               ap=[[RPB_A * RPB_B, NA_HEADS], [RPB_B, n_a], [1, wide]])

            with sp.Fori(0, COLS_S) as c:
                sp.dma_start(bias_s[c], shifted(RPB_PAD + NA_WIN - 1 - COLS_S - c, RPB_A, WIDE_S))\
                    .then_inc(bias_table, 16)
            with sp.Fori(0, COLS_P) as c:
                sp.dma_start(bias_p[c], shifted(RPB_PAD + A0_P * RPB_B + NA_WIN - 1 - COLS_P - c, A_P, WIDE_P))\
                    .then_inc(bias_table, 16)

            def moe_loads(l, before):
                order = [(2 * f + k, w, f) for f in range(2) for k, w in enumerate((exp_w_gate, exp_w_up))]
                order += [(4 + f, exp_w_down, f) for f in range(2)]
                for s, w, f in order:
                    matmuls_done(sp, *before[s])
                    sp.dma_start(w3(s, DT, HALF), halves(w[l, 0])[f]).then_inc(slot_full[s], 16)
                with sp.Fori(1, EXPERTS) as e:
                    for s, w, f in order:
                        split_done(sp, l, s, e - 1)
                        sp.dma_start(w3(s, DT, HALF), halves(w[l, e])[f]).then_inc(slot_full[s], 16)

            def ple_loads(l):
                for s, w in enumerate(halves(ple_w_gate[l])):
                    split_done(sp, l, s, EXPERTS - 1)
                    sp.dma_start(w3(s, DT, HALF), w).then_inc(slot_full[s], 16)
                split_done(sp, l, 2, EXPERTS - 1)
                sp.dma_start(w3(2, 2, D), ple_w_up[l].rearrange("(t p) f -> p t f", p=P)).then_inc(slot_full[2], 16)

            r = RET_HEADS - 1
            moe_loads(0, [("ret", ("qk", 1, 3), r), ("ret", ("v", 1, 3), r), ("ret", ("g", 1, 3), r)]
                      + [("ret", ("out", 1, 3, 1), r)] * 3)
            ple_loads(0)

            def na_loads(q, before):
                matmuls_done(sp, *before[0])
                q_k = w3(0, DT, 512)
                sp.dma_start(q_k[:, :, 0:256], columns(na_w_in[0], q * 256, 256)).then_inc(slot_full[0], 16)
                sp.dma_start(q_k[:, :, 256:512], columns(na_w_in[0], q * 256 + D, 256)).then_inc(slot_full[0], 16)
                matmuls_done(sp, *before[1])
                sp.dma_start(w3(1, DT, 256), columns(na_w_in[0], q * 256 + 2 * D, 256)).then_inc(slot_full[1], 16)

            na_loads(0, [("ple0", ("g", TT - 1, 0)), ("ple0", ("g", TT - 1, 1))])
            for f, w in enumerate(halves(na_w_out[0])):
                split_done(sp, 0, 4 + f, EXPERTS - 1)
                sp.dma_start(w3(4 + f, DT, HALF), w).then_inc(slot_full[4 + f], 16)
            with sp.Fori(1, NA_HEADS // QUAD) as q:
                na_loads(q, [("na", ("qk", 3, 1), q - 1), ("na", ("v", TT - 1), q - 1)])
            r = NA_HEADS // QUAD - 1
            moe_loads(1, [("na", ("qk", 3, 1), r), ("na", ("v", TT - 1), r), ("na", ("tr", TT - 1), r),
                          ("na", ("tr", TT - 1), r), ("naout", ("out", TT - 1, 0)), ("naout", ("out", TT - 1, 1))])
            ple_loads(1)

        @block.gpsimd
        def _(pool):
            chain = Chain(pool, pool_step)
            gains = [mix_norm[0], ffn_norm[0], ple_norm[0], mix_norm[1], ffn_norm[1], ple_norm[1], final_norm]

            def load_gain(n):
                pool.dma_start(gain[:, n % 2, :], gains[n].rearrange("(a d) -> a d", a=1).broadcast_to([P, D]))\
                    .then_inc(gain_in[n % 2], 16)

            load_gain(0)
            for m in (ident, ident16):
                chain.link(nc.gpsimd.memset(m[:], 0.0))
                nc.gpsimd.affine_select(out=m[:], in_=m[:], compare_op=ALU.not_equal, fill=1.0, base=0,
                                        pattern=[[-1, P]], channel_multiplier=1).then_inc(ident_set, 1)
            chain.link(nc.gpsimd.memset(minus_half[:], -0.5))
            pool.dma_start(lgt[:, 0, :], ret_decay_logit.rearrange("a b h -> a (b h)").broadcast_to([P, 8]))\
                .then_inc(const_in, 16)
            pool.dma_start(r_diff, row_minus_col).then_inc(const_in, 16)
            pool.dma_start(cos_t[:], rope_cos).then_inc(const_in, 16)
            pool.dma_start(sin_t[:], rope_sin).then_inc(const_in, 16)
            load_gain(1)
            pool.dma_start(mask[:], col_mask.bitcast(BF16)).then_inc(const_in, 16)
            pool.dma_start(rw[:, :, :, :].rearrange("p l t e -> p (l t) e"),
                           router_w.rearrange("l (t p) e -> p (l t) e", p=P)).then_inc(const_in, 16)

            def rsqrt(src, scale, dst, t):
                chain.link(nc.gpsimd.tensor_scalar(meansq[:, t:t + 1], src, scale, EPS, ALU.mult, ALU.add))
                return nc.gpsimd.tensor_tensor(dst, meansq[:, t:t + 1], minus_half[:, 0:1], ALU.pow)

            def norm(n, l=None, order=0):
                for t in range(TT):
                    pool.wait_ge(norm_sq[n], t + 1)
                    rsqrt(sumsq[:, t:t + 1], 1.0 / D, rstd[:, t:t + 1], t).then_inc(norm_rs[n], 1)
                if l is not None:
                    rows = grid_rows if order else natural_rows
                    for dram, src, ready, done in ((rows_summed[l], resid, norm_sq[n], resid_saved[l]),
                                                   (rows_normed[l], xn_all, norm_rows[n], rows_out[l])):
                        pool.wait_ge(ready, TT)
                        for d, tiles in rows(dram[0:SEQ_P, :], dram[SEQ_P:TOK, :], src):
                            pool.dma_start(d, tiles).then_inc(done, 16)
                if 1 <= n < 6:
                    load_gain(n + 1)

            def mixture(l, order):
                pool.wait_ge(resid_saved[l], 16 * row_dmas(order))
                pool.wait_ge(rows_out[l], 16 * row_dmas(order))
                drained(pool, f"route{l}", "idx")

                def gather(e):
                    chain.link(nc.gpsimd.tensor_copy(idx_in[:], idx_t[:, bass.ds(e, 1)]))
                    hold(pool)
                    nc.gpsimd.indirect_dma_start(
                        out=m_x, out_offset=None, in_=rows_normed[l],
                        in_offset=bass.IndirectOffsetOnAxis(ap=idx_in[:, :], axis=0)).then_inc(moe_rows[l], 16)

                def scatter(phase, e, n):
                    drained(pool, phase, "y1", e)
                    chain.link(nc.gpsimd.tensor_copy(idx_out[:], idx_t[:, bass.ds(n, 1)]))
                    hold(pool)
                    nc.gpsimd.indirect_dma_start(
                        out=rows_summed[l], out_offset=bass.IndirectOffsetOnAxis(ap=idx_out[:, :], axis=0),
                        in_=m_y, in_offset=None, compute_op=ALU.add).then_inc(moe_added[l], 16)
                    pool.wait_ge(moe_added[l], at(16, 16, n))
                    pool.sem_inc(moe_y_free[l], 1)

                pool.sem_inc(moe_y_free[l], 1)
                gather(0)
                matmuls_done(pool, f"first{l}", "x1")
                gather(1)
                with pool.Fori(0, EXPERTS - 2) as e:
                    chain.enter(e, 2)
                    matmuls_done(pool, f"moe{l}", "x1", e)
                    gather(e + 2)
                    scatter(f"moe{l}", e, e)
                    chain.leave(EXPERTS - 2)
                scatter(f"moe{l}", EXPERTS - 2, EXPERTS - 2)
                scatter(f"last{l}", 0, EXPERTS - 1)

            def after_mixture(l, order):
                rows = grid_rows if order else natural_rows
                src = rows_summed[l]
                for dram, tiles in rows(src[0:SEQ_P, :], src[SEQ_P:TOK, :], resid):
                    pool.dma_start(tiles, dram).then_inc(resid_in[l], 16)
                for dram, tiles in rows(p_prompt[l, 0], p_sample[l, 0], e_p):
                    pool.dma_start(tiles, dram).then_inc(p_in[l], 16)

            def load_bias(q):
                for rows, cols, table, w, lo in ((ROWS_S, COLS_S, bias_s, WIDE_S, 0),
                                                 (ROWS_P, COLS_P, bias_p, WIDE_P, 8 * WIDE_S)):
                    for r in range(rows):
                        a = rows - 1 - r
                        src = table[:, bass.ds(q * QUAD, QUAD), a:a + rows, :].rearrange("c h a w -> c h (a w)")
                        pool.dma_start(bias[r * cols:(r + 1) * cols, :, lo:lo + rows * w], src).then_inc(na_bias, 16)

            norm(0)
            matmuls_done(pool, "norm0", ("t", TT - 1, 1))
            pool.dma_start(r_gn, ret_gn_w.broadcast_to([P, 2 * D])).then_inc(gn_in, 16)
            with pool.Fori(0, RET_HEADS) as h:
                chain.enter(h, TT)
                for t in range(TT):
                    pool.wait_ge(ret_var, at(t + 1, TT, h))
                    hold(pool)
                    rsqrt(mv[:, t % 2, 1:2], 1.0, mvr[:, t % 2:t % 2 + 1], t).then_inc(ret_rstd, 1)
                chain.leave(RET_HEADS)
            norm(1, 0, 0)
            mixture(0, 0)
            after_mixture(0, 1)
            norm(2)
            pool.wait_ge(bias_table, 16 * (COLS_S + COLS_P))
            load_bias(0)
            norm(3)
            with pool.Fori(1, NA_HEADS // QUAD) as q:
                drained(pool, "na", ("s", len(na_units()) - 1), q - 1)
                load_bias(q)
            norm(4, 1, 1)
            mixture(1, 1)
            after_mixture(1, 0)
            norm(5)
            outs = [y_prompt[0, 0:P], y_prompt[0, P:SEQ_P]] + [y_sample[0, t * P:(t + 1) * P] for t in range(4)]
            for t in range(TT):
                pool.wait_ge(norm_sq[6], t + 1)
                rsqrt(sumsq[:, t:t + 1], 1.0 / D, rstd[:, t:t + 1], t).then_inc(norm_rs[6], 1)
                pool.wait_ge(norm_rows[6], t + 1)
                pool.dma_start(outs[t], xn[:, t % 2, :]).then_inc(final_out[t % 2], 16)
            for b in range(2):
                pool.wait_ge(final_out[b], 16 * TT // 2)

        @block.scalar
        def _(act):
            def resid_wait(n, t):
                if n == 0:
                    act.wait_ge(x_in[0 if t < 2 else 1], 16)
                elif n == 1:
                    drained(act, "ret", ("out", 1, 3, 1), RET_HEADS - 1)
                elif n in (2, 5):
                    act.wait_ge(resid_in[n // 3], 16 * (ROWS_P + ROWS_S if n == 2 else 2))
                elif n in (3, 6):
                    act.wait_ge(ple_add[n // 3 - 1], 2 * (t + 1))
                else:
                    drained(act, "naout", ("out", t, 1))

            def norm(n, l=None):
                for t in range(TT + 1):
                    if t < TT:
                        resid_wait(n, t)
                        if t >= 2 and n < 6 and l is None:
                            matmuls_done(act, f"norm{n}", ("t", t - 2, 1))
                        if t >= 2 and n == 6:
                            act.wait_ge(final_out[t % 2], 16 * (t // 2))
                        nc.scalar.activation(normed(n, t), resid[:, t, :], ACT.Square,
                                             accum_out=sumsq[:, t:t + 1]).then_inc(norm_sq[n], 1)
                    if t and n < 6:
                        b, done = filled(act, f"norm{n}", ("t", t - 1, 0))
                        nc.scalar.copy(xt[:, 0:4, (t - 1) * P:t * P],
                                       b[:, :].rearrange("p (f n) -> p f n", f=4)).then_inc(done, 1)

            norm(0)
            act.wait_ge(decay_abs, 1)
            nc.scalar.activation(lgt[:, 2, :], lgt[:, 1, :], ACT.Exp, scale=-1.0).then_inc(decay_exp, 1)

            with act.Fori(0, RET_HEADS) as h:
                act.wait_ge(strip_arg, h + 1)
                nc.scalar.activation(r_strip, r_strip, ACT.Exp).then_inc(strip_set, 1)
                for g, (_, n) in enumerate(GROUPS):
                    nt = n // P
                    for t in range(nt):
                        b, done = filled(act, "ret", ("v", g, t), h)
                        nc.scalar.copy(r_v[:, t, :], b[:, :]).then_inc(done, 1)
                    for t in range(nt + 1):
                        if t < nt:
                            b, done = filled(act, "ret", ("g", g, t), h)
                            nc.scalar.activation(r_silu[:, t % 2, :], b[:, :], ACT.Silu).then_inc(done, 1)
                        if t:
                            b, done = filled(act, "ret", ("tr", g, t - 1), h)
                            nc.scalar.copy(r_ot[:, :, (t - 1) * P:t * P],
                                           b[:, :].rearrange("p (f n) -> p f n", f=4)).then_inc(done, 1)

            def mixture(l):
                drained(act, f"route{l}", "logit")
                nc.scalar.activation(m_ex, m_lg, ACT.Exp).then_inc(moe_exp[l], 1)

                def high(phase, key, i, dst, c):
                    b, _ = filled(act, phase, key, i)
                    nc.scalar.copy(dst[:, 4 * c:4 * c + 4, :],
                                   b[:, 0:4 * CAP].rearrange("p (f n) -> p f n", f=4)).then_inc(moe_th[l], 1)

                def split(c, n, before=None):
                    if c % 2 == 0:
                        s, first, per, _ = slot.get(f"moe{l}", c // 2, n)
                        act.wait_ge(slot_full[s], at(16 * first, 16 * per, n))
                    if before is not None:
                        parts_free(act, l, *before)
                    nc.scalar.copy(w_parts[:, c % 3, 0, :], wt[:, c // 2, c % 2 * 2048:c % 2 * 2048 + 2048])\
                        .then_inc(moe_wh[l], 1)

                def expert(phase, e, n):
                    def silu(f):
                        b, done = filled(act, phase, f"g{f}", e)
                        nc.scalar.activation(m_silu[:, f, :], b[0:CAP, :], ACT.Silu).then_inc(done, 1)

                    def splits(a, z):
                        for c in range(a, z):
                            split(c, n, (c, phase, e) if phase[0] == "m" else (c, phase, EXPERTS - 1))

                    splits(3, 4)
                    silu(0)
                    splits(4, 8)
                    silu(1)
                    splits(8, 10)
                    high(phase, "h0", e, m_hidt[0], 0)
                    if phase[0] == "m":
                        for c in range(2):
                            high(phase, f"x{c}", e, m_xt[0], c)
                    high(phase, "h1", e, m_hidt[0], 1)
                    splits(10, 12)
                    if phase[0] == "m":
                        for c in range(3):
                            split(c, n + 1, (c + 12, phase, e))

                act.wait_ge(moe_aff[l], 1)
                act.wait_ge(resid_saved[l], 16 * row_dmas(l))
                for c in range(3):
                    split(c, 0)
                for c in range(2):
                    high(f"first{l}", f"x{c}", 0, m_xt[0], c)
                with act.Fori(0, EXPERTS - 1) as e:
                    expert(f"moe{l}", e, e)
                expert(f"last{l}", 0, EXPERTS - 1)

            def embedding(l):
                for t in range(TT):
                    b, done = filled(act, f"ple{l}", ("pt", t))
                    nc.scalar.copy(e_pt[:, :, t * P:(t + 1) * P],
                                   b[:, 0:2 * P].rearrange("p (f n) -> p f n", f=2)).then_inc(done, 1)
                for t in range(TT):
                    for f in range(2):
                        if t:
                            drained(act, f"ple{l}", ("u", t - 1, f))
                        b, done = filled(act, f"ple{l}", ("g", t, f))
                        nc.scalar.activation(e_sig[:, f, :], b[:, :], ACT.Sigmoid).then_inc(done, 1)

            norm(1, 0)
            mixture(0)
            norm(2)
            embedding(0)
            norm(3)

            units = na_units()
            with act.Fori(0, NA_HEADS // QUAD) as q:
                for f in range(2):
                    for c, (a, w) in enumerate(((0, 512), (512, 256))):
                        b, done = filled(act, "na", ("qk", f, c), q)
                        nc.scalar.mul(n_qk[:, f, a:a + w], b[:, 0:w], NA_DH ** -0.5).then_inc(done, 1)
                for t in range(0, TT, 2):
                    b, done = filled(act, "na", ("v", t), q)
                    nc.scalar.copy(n_v[:, t, :], b[:, 0:256]).then_inc(done, 1)
                for u in range(len(units) + 2):
                    if u < len(units):
                        t, h = units[u]
                        w = NA_KEYS[t][1] * P
                        act.wait_ge(na_max, at(u + 1, len(units), q))
                        if u >= 2:
                            matmuls_done(act, "na", ("pt", u - 2), q)
                        nc.scalar.activation(n_p[:, u % 2, 0:w], n_s[:, u % 2, 0:w], ACT.Exp, bias=nmx[:, u % 2:u % 2 + 1],
                                             accum_out=den[:, t % 2, h:h + 1]).then_inc(na_exp, 1)
                    if 1 <= u <= len(units) and (u - 1) % 2 == 0:
                        w = NA_KEYS[units[u - 1][0]][1] * P
                        b, done = filled(act, "na", ("pt", u - 1), q)
                        nc.scalar.copy(n_pt[:, 0, 0:w], b[:, 0:w]).then_inc(done, 1)
                    if u >= 2 and units[u - 2][1] == QUAD - 1:
                        t = units[u - 2][0]
                        b, done = filled(act, "na", ("tr", t), q)
                        nc.scalar.copy(n_ot[:, bass.ds(q * 2, 2), t * P:(t + 1) * P],
                                       b[:, 0:2 * P].rearrange("p (f n) -> p f n", f=2)).then_inc(done, 1)
            norm(4, 1)
            mixture(1)
            norm(5)
            embedding(1)
            norm(6)

        @block.tensor
        def _(pe):
            def transposes(phase, key, srcs, i=0, w=P):
                b, full = fill(pe, phase, key, i)
                for c, src in enumerate(srcs):
                    k = src.shape[0]
                    last = nc.tensor.transpose(b[:, c * w:(c + 1) * w], src, ident[0:k, 0:k])
                last.then_inc(full, 1)

            def product(phase, key, lhs, rhs, i=0, m=P):
                b, full = fill(pe, phase, key, i)
                n = rhs[0].shape[-1]
                for c, (x, y) in enumerate(zip(lhs, rhs)):
                    last = nc.tensor.matmul(b[0:m, 0:n], x, y, start=(c == 0), stop=(c == len(lhs) - 1))
                last.then_inc(full, 1)

            def norm(n):
                for t in range(TT):
                    pe.wait_ge(norm_rows[n], t + 1)
                    for c in range(2):
                        transposes(f"norm{n}", ("t", t, c),
                                   [normed(n, t)[:, (4 * c + k) * P:(4 * c + k + 1) * P] for k in range(4)])
                for c in range(2):
                    drained(pe, f"norm{n}", ("t", TT - 1, c))

            def xt_tiles(a, w):
                return [xt[:, k, a:a + w] for k in range(DT)]

            pe.wait_ge(ident_set, 2)
            norm(0)
            with pe.Fori(0, RET_HEADS) as h:
                w_qk, w_v, w_g, w_o = w3(0, DT, 512), w3(1, DT, 512), w3(2, DT, 512), w3(3, 4, D)
                for g, (first, n) in enumerate(GROUPS):
                    nt = n // P
                    if g == 0:
                        loaded(pe, "ret", "k", h)
                    for f in range(4):
                        product("ret", ("qk", g, f), [w_qk[:, k, f * P:(f + 1) * P] for k in range(DT)],
                                xt_tiles(first, n), h)
                    if g == 0:
                        loaded(pe, "ret", "v", h)
                    for t in range(nt):
                        product("ret", ("v", g, t), xt_tiles(first + t * P, P), [w_v[:, k, :] for k in range(DT)], h)
                    pe.wait_ge(ret_rot, at(2 * g + 2, 4, h))
                    for t in range(nt):
                        product("ret", ("s", g, t), [r_qk[:, 2 + k, t * P:(t + 1) * P] for k in range(2)],
                                [r_qk[:, k, 0:n] for k in range(2)], h)
                    if g == 0:
                        loaded(pe, "ret", "g", h)
                    for t in range(nt + 1):
                        if t < nt:
                            product("ret", ("g", g, t), xt_tiles(first + t * P, P),
                                    [w_g[:, k, :] for k in range(DT)], h)
                            if t == 0:
                                for k in range(nt):
                                    drained(pe, "ret", ("v", g, k), h)
                                    drained(pe, "ret", ("s", g, k), h)
                            product("ret", ("o", g, t), [r_s[:, k, t * P:(t + 1) * P] for k in range(nt)],
                                    [r_v[:, k, :] for k in range(nt)], h)
                        if t:
                            pe.wait_ge(ret_og, at(first // P + t, TT, h))
                            transposes("ret", ("tr", g, t - 1),
                                       [r_og[:, (t - 1) % 2, k * P:(k + 1) * P] for k in range(4)], h)
                    if g == 0:
                        loaded(pe, "ret", "o", h)
                    for t in range(nt):
                        drained(pe, "ret", ("tr", g, t), h)
                        for f in range(2):
                            product("ret", ("out", g, t, f), [r_ot[:, k, t * P:(t + 1) * P] for k in range(4)],
                                    [w_o[:, k, f * HALF:(f + 1) * HALF] for k in range(4)], h)

            def mixture(l):
                if l == 0:
                    pe.wait_ge(const_in, 6 * 16)
                b, full = fill(pe, f"route{l}", "logit")
                for t in range(TT):
                    for k in range(DT):
                        last = nc.tensor.matmul(b[:, t * EXPERTS:(t + 1) * EXPERTS], xt[:, k, t * P:(t + 1) * P],
                                                rw[:, l, k, :], start=(k == 0), stop=(k == DT - 1))
                last.then_inc(full, 1)
                pe.wait_ge(moe_aff[l], 1)
                for g, (first, n) in enumerate(GROUPS):
                    b, full = fill(pe, f"route{l}", f"aff{g}")
                    for t in range(n // P):
                        last = nc.tensor.transpose(b[0:EXPERTS, t * P:(t + 1) * P], m_af[:, first // P + t, :], ident[:, :])
                    last.then_inc(full, 1)
                pe.wait_ge(moe_top[l], 1)
                for key, src in (("gate", top_v), ("idx", top_f)):
                    b, full = fill(pe, f"route{l}", key)
                    nc.tensor.transpose(b[0:CAP, 0:EXPERTS], src[:, :], ident[0:EXPERTS, 0:EXPERTS]).then_inc(full, 1)

                def rows(phase, e, n):
                    pe.wait_ge(moe_rows[l], at(16, 16, n))
                    for c in range(2):
                        transposes(phase, f"x{c}", [m_x[:, (4 * c + k) * P:(4 * c + k + 1) * P] for k in range(4)],
                                   e, CAP)

                def product_of_parts(phase, key, lhs, e, n):
                    b, full = fill(pe, phase, key, e)
                    for half in range(2):
                        c = 2 * MOE_USES.index(key) + half
                        pe.wait_ge(moe_wl[l], at(c + 1, 12, n))
                        if key[0] == "y":
                            drained(pe, phase, f"h{half}", e)
                        w = w_parts[:, c % 3, :, :].rearrange("p k (j f) -> p k j f", f=HALF)
                        for j in range(4):
                            for x, k in ((0, 0), (1, 0), (0, 1)):
                                last = nc.tensor.matmul(b[0:CAP, :], lhs[x][:, 4 * half + j, :], w[:, k, j, :],
                                                        start=(c % 2 == 0 and j == 0 and x == k == 0),
                                                        stop=(half == 1 and j == 3 and k == 1))
                        last.then_inc(full if half else moe_wused[l], 1)

                def expert(phase, e, n):
                    for key in MOE_USES[0:4]:
                        product_of_parts(phase, key, m_xt, e, n)
                    for f in range(2):
                        drained(pe, phase, f"u{f}", e)
                        transposes(phase, f"h{f}", [m_hid[:, (4 * f + k) * P:(4 * f + k + 1) * P] for k in range(4)],
                                   e, CAP)
                        if f == 0 and phase[0] == "m":
                            rows(phase, e, n + 1)
                    for key in MOE_USES[4:6]:
                        product_of_parts(phase, key, m_hidt, e, n)

                rows(f"first{l}", 0, 0)
                for c in range(2):
                    drained(pe, f"first{l}", f"x{c}")
                with pe.Fori(0, EXPERTS - 1) as e:
                    expert(f"moe{l}", e, e)
                expert(f"last{l}", 0, EXPERTS - 1)

            def embedding(l):
                pe.wait_ge(p_in[l], 16 * (ROWS_P + ROWS_S if l == 0 else 2))
                for t in range(TT):
                    transposes(f"ple{l}", ("pt", t), [e_p[:, t, k * P:(k + 1) * P] for k in range(2)])
                for key in ("g0", "g1", "u"):
                    loaded(pe, f"ple{l}", key)
                w_g, w_u = [w3(0, DT, HALF), w3(1, DT, HALF)], w3(2, 2, D)
                for t in range(TT):
                    drained(pe, f"ple{l}", ("pt", t))
                    for f in range(2):
                        product(f"ple{l}", ("g", t, f), xt_tiles(t * P, P), [w_g[f][:, k, :] for k in range(DT)])
                        product(f"ple{l}", ("u", t, f), [e_pt[:, k, t * P:(t + 1) * P] for k in range(2)],
                                [w_u[:, k, f * HALF:(f + 1) * HALF] for k in range(2)])

            norm(1)
            mixture(0)
            norm(2)
            embedding(0)
            norm(3)

            units = na_units()
            with pe.Fori(0, NA_HEADS // QUAD) as q:
                w_qk, w_v = w3(0, DT, 512), w3(1, DT, 256)
                loaded(pe, "na", "k", q)
                for f in range(4):
                    for c, (a, w) in enumerate(((0, 512), (512, 256))):
                        product("na", ("qk", f, c), [w_qk[:, k, f * P:(f + 1) * P] for k in range(DT)], xt_tiles(a, w), q)
                loaded(pe, "na", "v", q)
                for t in range(TT):
                    product("na", ("v", t), xt_tiles(t * P, P), [w_v[:, k, :] for k in range(DT)], q)
                for f in range(4):
                    for c in range(2):
                        drained(pe, "na", ("qk", f, c), q)
                for t in range(TT):
                    drained(pe, "na", ("v", t), q)
                for u in range(len(units) + 2):
                    if u < len(units):
                        t, h = units[u]
                        k0, nk, m0 = NA_KEYS[t]
                        b, full = fill(pe, "na", ("s", u), q)
                        a = h % 2 * NA_DH
                        nc.tensor.matmul(b[:, 0:nk * P], ident16[:, :], mask[:, m0:m0 + nk * P], start=True, stop=False)
                        nc.tensor.matmul(b[:, 0:nk * P], n_qk[a:a + NA_DH, h // 2, t * P:(t + 1) * P],
                                         n_qk[a:a + NA_DH, 2 + h // 2, k0 * P:(k0 + nk) * P],
                                         start=False, stop=True).then_inc(full, 1)
                    if 1 <= u <= len(units):
                        v = u - 1
                        nk = NA_KEYS[units[v][0]][1]
                        pe.wait_ge(na_exp, at(v + 1, len(units), q))
                        transposes("na", ("pt", v), [n_p[:, v % 2, k * P:(k + 1) * P] for k in range(nk)], q)
                    if u >= 2:
                        v = u - 2
                        t, h = units[v]
                        k0, nk, _ = NA_KEYS[t]
                        if h == 0:
                            o_bank, o_full = fill(pe, "na", ("o", t), q)
                        drained(pe, "na", ("pt", v), q)
                        for k in range(nk):
                            last = nc.tensor.matmul(o_bank[:, h * NA_DH:(h + 1) * NA_DH], n_pt[:, v % 2, k * P:(k + 1) * P],
                                                    n_v[:, k0 + k, h * NA_DH:(h + 1) * NA_DH],
                                                    start=(k == 0), stop=(k == nk - 1))
                        if h == QUAD - 1:
                            last.then_inc(o_full, 1)
                            drained(pe, "na", ("o", t), q)
                            transposes("na", ("tr", t), [n_o[:, t % 2, k * P:(k + 1) * P] for k in range(2)], q)
            for f in range(2):
                loaded(pe, "naout", f)
            for t in range(TT):
                if t == 0:
                    drained(pe, "na", ("tr", TT - 1), NA_HEADS // QUAD - 1)
                for f in range(2):
                    product("naout", ("out", t, f), [n_ot[:, k, t * P:(t + 1) * P] for k in range(DT)],
                            [w3(4 + f, DT, HALF)[:, k, :] for k in range(DT)])
            norm(4)
            mixture(1)
            norm(5)
            embedding(1)

        @block.vector
        def _(dve):
            chain = Chain(dve, dve_step)
            v = nc.vector

            def norm(n):
                dve.wait_ge(gain_in[n % 2], 16 * (n // 2 + 1))
                for t in range(TT + 1):
                    if t < TT:
                        dve.wait_ge(norm_rs[n], t + 1)
                        v.scalar_tensor_tensor(out=normed(n, t), in0=resid[:, t, :], scalar=rstd[:, t:t + 1],
                                               in1=gain[:, n % 2, :], op0=ALU.mult, op1=ALU.mult)\
                            .then_inc(norm_rows[n], 1)
                    if t and n < 6:
                        b, done = filled(dve, f"norm{n}", ("t", t - 1, 1))
                        v.tensor_copy(xt[:, 4:8, (t - 1) * P:t * P],
                                      b[:, :].rearrange("p (f n) -> p f n", f=4)).then_inc(done, 1)

            dve.wait_ge(const_in, 6 * 16)
            x, ax, y, s, s2, p = (lgt[:, k, :] for k in range(6))
            chain.link(v.tensor_scalar(ax, x, -1.0, None, ALU.mult))
            v.tensor_tensor(ax, ax, x, ALU.max).then_inc(decay_abs, 1)
            norm(0)
            dve.wait_ge(decay_exp, 1)
            chain.link(v.tensor_scalar(s2, y, 2.0, None, ALU.add))
            chain.link(v.reciprocal(p, s2))
            chain.link(v.tensor_tensor(s, p, y, ALU.mult))
            chain.link(v.tensor_tensor(s2, s, s, ALU.mult))
            chain.link(v.tensor_scalar(p, s2, 1.0 / 19, None, ALU.mult))
            for k in range(17, 1, -2):
                chain.link(v.scalar_tensor_tensor(out=p, in0=p, scalar=1.0 / k, in1=s2, op0=ALU.add, op1=ALU.mult))
            chain.link(v.scalar_tensor_tensor(out=p, in0=p, scalar=1.0, in1=s, op0=ALU.add, op1=ALU.mult))
            chain.link(v.tensor_scalar(s, x, 0.0, None, ALU.min))
            chain.link(v.scalar_tensor_tensor(out=lg[:], in0=p, scalar=-2.0, in1=s, op0=ALU.mult, op1=ALU.add))
            dve.wait_ge(gn_in, 16)

            with dve.Fori(0, RET_HEADS) as h:
                chain.enter(h, 2 + 2 * 6 + TT * 2)
                flat = r_tmp.rearrange("p f n -> p (f n)")
                a, b2 = flat[:, 0:STRIP], flat[:, STRIP:2 * STRIP]
                chain.link(v.tensor_scalar(a, r_diff, 0.0, lg[:, bass.ds(h, 1)], ALU.max, ALU.mult))
                chain.link(v.tensor_scalar(b2, r_diff, 0.0, lg[:, bass.ds(h + RET_HEADS, 1)], ALU.min, ALU.mult))
                v.tensor_tensor(r_strip, a, b2, ALU.subtract).then_inc(strip_arg, 1)
                dve.wait_ge(strip_arg, h + 1)
                for g, (first, n) in enumerate(GROUPS):
                    nt = n // P
                    for j in range(2):
                        t0, t1, t2, t3 = (r_tmp[:, k, 0:n] for k in range(4))
                        b, done = filled(dve, "ret", ("qk", g, 2 * j), h)
                        chain.link(v.tensor_tensor(t0, b[:, 0:n], cos_t[:, 0:n], ALU.mult))
                        v.tensor_tensor(t2, b[:, 0:n], sin_t[:, 0:n], ALU.mult).then_inc(done, 1)
                        b, done = filled(dve, "ret", ("qk", g, 2 * j + 1), h)
                        chain.link(v.tensor_tensor(t1, b[:, 0:n], sin_t[:, 0:n], ALU.mult))
                        v.tensor_tensor(t3, b[:, 0:n], cos_t[:, 0:n], ALU.mult).then_inc(done, 1)
                        chain.link(v.tensor_tensor(r_qk[:, 2 * j, 0:n], t0, t1, ALU.subtract))
                        drained(dve, "ret", ("qk", g, 2 * j + 1), h)
                        v.tensor_tensor(r_qk[:, 2 * j + 1, 0:n], t2, t3, ALU.add).then_inc(ret_rot, 1)
                        dve.wait_ge(ret_rot, at(2 * g + j + 1, 4, h))
                    if g == 0:
                        dve.wait_ge(strip_set, h + 1)
                    for t in range(nt):
                        b, done = filled(dve, "ret", ("s", g, t), h)
                        v.scalar_tensor_tensor(out=r_s[:, t, 0:n], in0=b[:, 0:n], scalar=RET_DK ** -0.5,
                                               in1=r_strip[:, STRIP0 - t * P:STRIP0 - t * P + n],
                                               op0=ALU.mult, op1=ALU.mult).then_inc(done, 1)
                    for t in range(nt):
                        k = first // P + t
                        b, done = filled(dve, "ret", ("o", g, t), h)
                        chain.link(v.bn_stats(stats[:], b[:, :]))
                        hold(dve)
                        v.bn_aggr(mv[:, k % 2, :], stats[:]).then_inc(ret_var, 1)
                        drained(dve, "ret", ("g", g, t), h)
                        chain.link(v.tensor_tensor(r_silu[:, t % 2, :], r_silu[:, t % 2, :],
                                                   r_gn[:, bass.ds(h * 512, 512)], ALU.mult))
                        dve.wait_ge(ret_rstd, at(k + 1, TT, h))
                        v.tensor_scalar(r_og[:, t % 2, :], b[:, :], mv[:, k % 2, 0:1], mvr[:, k % 2:k % 2 + 1],
                                        ALU.subtract, ALU.mult).then_inc(done, 1)
                        drained(dve, "ret", ("o", g, t), h)
                        v.tensor_tensor(r_og[:, t % 2, :], r_og[:, t % 2, :], r_silu[:, t % 2, :], ALU.mult)\
                            .then_inc(ret_og, 1)
                    for t in range(nt):
                        for f in range(2):
                            b, done = filled(dve, "ret", ("out", g, t, f), h)
                            k = first // P + t
                            r = resid[:, k, f * HALF:(f + 1) * HALF]
                            v.tensor_tensor(r, r, b[:, :], ALU.add).then_inc(done, 1)
                chain.leave(RET_HEADS)

            def mixture(l, order):
                smax, ssum, srec = rsm[:, 0, 0:TT], rsm[:, 1, 0:TT], rsm[:, 2, 0:TT]

                def wide(x):
                    return x.rearrange("p (t a) -> p t a", a=1).broadcast_to([P, TT, EXPERTS])

                b, done = filled(dve, f"route{l}", "logit")
                logits = b[:, 0:TT * EXPERTS].rearrange("p (t e) -> p t e", t=TT)
                chain.link(v.tensor_reduce(smax, logits, AX_X, ALU.max))
                v.tensor_tensor(m_lg, logits, wide(smax), ALU.subtract).then_inc(done, 1)
                dve.wait_ge(moe_exp[l], 1)
                chain.link(v.tensor_reduce(ssum, m_ex, AX_X, ALU.add))
                chain.link(v.reciprocal(srec, ssum))
                v.tensor_tensor(m_af, m_ex, wide(srec), ALU.mult).then_inc(moe_aff[l], 1)
                for g, (first, n) in enumerate(GROUPS):
                    b, done = filled(dve, f"route{l}", f"aff{g}")
                    dst, src = m_aff[:, first:first + n], b[0:EXPERTS, 0:n]
                    if order:
                        rows, cols = ((ROWS_P, COLS_P), (ROWS_S, COLS_S))[g]
                        dst = dst.rearrange("e (r t c) -> e t r c", r=rows, c=cols)
                        src = src.rearrange("e (t r c) -> e t r c", r=rows, c=cols)
                    for t in range(n // P if order else 1):
                        last = v.tensor_copy(dst[:, t] if order else dst, src[:, t] if order else src)
                    last.then_inc(done, 1)
                drained(dve, f"route{l}", "aff1")
                drained(dve, f"route{l}", "aff0")
                c0 = 0
                for (first, n), cap in zip(GROUPS, (CAP_P, CAP_S)):
                    a = m_aff[:, first:first + n]
                    for c in range(c0, c0 + cap, 8):
                        chain.link(v.max(out=top_v[:, c:c + 8], in_=a))
                        chain.link(v.max_index(out=top_i[:, c:c + 8], in_max=top_v[:, c:c + 8], in_values=a))
                        chain.link(v.match_replace(out=a, in_to_replace=top_v[:, c:c + 8], in_values=a, imm_value=-1.0))
                    c0 += cap
                chain.link(v.tensor_copy(top_f[:], top_i[:]))
                v.tensor_scalar(top_f[:, CAP_P:CAP], top_f[:, CAP_P:CAP], float(SEQ_P), None, ALU.add)\
                    .then_inc(moe_top[l], 1)
                for key, dst in (("gate", gate_t), ("idx", idx_t)):
                    b, done = filled(dve, f"route{l}", key)
                    v.tensor_copy(dst[:, :], b[0:CAP, 0:EXPERTS]).then_inc(done, 1)

                def low(phase, key, i, parts, c, count):
                    b, done = filled(dve, phase, key, i)
                    dve.wait_ge(moe_th[l], count)
                    k = slice(4 * c, 4 * c + 4)
                    v.tensor_tensor(parts[1][:, k, :], b[:, 0:4 * CAP].rearrange("p (f n) -> p f n", f=4),
                                    parts[0][:, k, :].bitcast(F32), ALU.subtract).then_inc(done, 1)

                def splits(a, z, n):
                    for c in range(a, z):
                        dve.wait_ge(moe_wh[l], at(c + 1, 12, n))
                        v.tensor_tensor(w_parts[:, c % 3, 1, :], wt[:, c // 2, c % 2 * 2048:c % 2 * 2048 + 2048],
                                        w_parts[:, c % 3, 0, :].bitcast(F32), ALU.subtract).then_inc(moe_wl[l], 1)

                def expert(phase, e, n):
                    more = phase[0] == "m"

                    def hidden(f):
                        drained(dve, phase, f"g{f}", e)
                        b, done = filled(dve, phase, f"u{f}", e)
                        v.tensor_tensor(m_hid[:, f * HALF:(f + 1) * HALF], m_silu[:, f, :], b[0:CAP, :], ALU.mult)\
                            .then_inc(done, 1)

                    def output(f):
                        b, done = filled(dve, phase, f"y{f}", e)
                        if f == 0:
                            dve.wait_ge(moe_y_free[l], n + 1)
                        v.tensor_scalar(m_y[:, f * HALF:(f + 1) * HALF], b[0:CAP, :], gate_t[:, bass.ds(n, 1)], None,
                                        ALU.mult).then_inc(done, 1)

                    splits(3, 6, n)
                    hidden(0)
                    splits(6, 10, n)
                    hidden(1)
                    low(phase, "h0", e, m_hidt, 0, at(3, 4, n))
                    if more:
                        for c in range(2):
                            low(phase, f"x{c}", e, m_xt, c, at(4 + c, 4, n))
                    low(phase, "h1", e, m_hidt, 1, at(6 if more else 4, 4, n))
                    splits(10, 12, n)
                    if more:
                        splits(0, 1, n + 1)
                    output(0)
                    if more:
                        splits(1, 3, n + 1)
                    output(1)

                splits(0, 3, 0)
                for c in range(2):
                    low(f"first{l}", f"x{c}", 0, m_xt, c, c + 1)
                with dve.Fori(0, EXPERTS - 1) as e:
                    expert(f"moe{l}", e, e)
                expert(f"last{l}", 0, EXPERTS - 1)

            def embedding(l):
                for t in range(TT):
                    for f in range(2):
                        drained(dve, f"ple{l}", ("g", t, f))
                        if t:
                            dve.wait_ge(ple_add[l], 2 * t - 1 + f)
                        b, done = filled(dve, f"ple{l}", ("u", t, f))
                        v.tensor_tensor(e_prod[:, f, :], e_sig[:, f, :], b[:, :], ALU.mult).then_inc(done, 1)
                        drained(dve, f"ple{l}", ("u", t, f))
                        r = resid[:, t, f * HALF:(f + 1) * HALF]
                        v.tensor_tensor(r, r, e_prod[:, f, :], ALU.add).then_inc(ple_add[l], 1)

            norm(1)
            mixture(0, 0)
            norm(2)
            embedding(0)
            norm(3)

            units = na_units()
            with dve.Fori(0, NA_HEADS // QUAD) as q:
                chain.enter(q, len(units) + TT)
                for f in range(2, 4):
                    for c, (a, w) in enumerate(((0, 512), (512, 256))):
                        b, done = filled(dve, "na", ("qk", f, c), q)
                        v.tensor_copy(n_qk[:, f, a:a + w], b[:, 0:w]).then_inc(done, 1)
                for t in range(1, TT, 2):
                    b, done = filled(dve, "na", ("v", t), q)
                    v.tensor_copy(n_v[:, t, :], b[:, 0:256]).then_inc(done, 1)
                dve.wait_ge(na_bias, at(16 * (ROWS_P + ROWS_S), 16 * (ROWS_P + ROWS_S), q))
                for u in range(len(units) + 2):
                    if u < len(units):
                        t, h = units[u]
                        k0, nk, _ = NA_KEYS[t]
                        rows, cols, wide_, lo = ((ROWS_P, COLS_P, WIDE_P, 8 * WIDE_S) if t < 2
                                                 else (ROWS_S, COLS_S, WIDE_S, 0))
                        bb = bias[:, h, lo:lo + rows * wide_].rearrange("p (r k c) -> p k r c", r=rows, c=cols)
                        rel = k0 - t + 1
                        b, done = filled(dve, "na", ("s", u), q)
                        if u >= 2:
                            dve.wait_ge(na_exp, at(u - 1, len(units), q))
                        scored = n_s[:, u % 2, 0:nk * P].rearrange("p (k r c) -> p k r c", k=nk, c=cols)
                        scores = b[:, 0:nk * P].rearrange("p (k r c) -> p k r c", k=nk, c=cols)
                        v.tensor_tensor(scored, scores, bb[:, rel:rel + nk], ALU.add).then_inc(done, 1)
                        drained(dve, "na", ("s", u), q)
                        chain.link(v.tensor_reduce(mx[:, u % 2:u % 2 + 1], n_s[:, u % 2, 0:nk * P], AX_X, ALU.max))
                        v.tensor_scalar(nmx[:, u % 2:u % 2 + 1], mx[:, u % 2:u % 2 + 1], -1.0, None, ALU.mult)\
                            .then_inc(na_max, 1)
                    if 1 <= u <= len(units) and (u - 1) % 2 == 1:
                        w = NA_KEYS[units[u - 1][0]][1] * P
                        b, done = filled(dve, "na", ("pt", u - 1), q)
                        v.tensor_copy(n_pt[:, 1, 0:w], b[:, 0:w]).then_inc(done, 1)
                    if u >= 2 and units[u - 2][1] == QUAD - 1:
                        t = units[u - 2][0]
                        b, done = filled(dve, "na", ("o", t), q)
                        chain.link(v.reciprocal(rden[:], den[:, t % 2, :]))
                        v.tensor_tensor(n_o[:, t % 2, :].rearrange("p (h d) -> p h d", h=QUAD),
                                        b[:, 0:256].rearrange("p (h d) -> p h d", h=QUAD),
                                        rden[:].rearrange("p (h a) -> p h a", a=1).broadcast_to([P, QUAD, NA_DH]),
                                        ALU.mult).then_inc(done, 1)
                chain.leave(NA_HEADS // QUAD)
            for t in range(TT):
                for f in range(2):
                    b, done = filled(dve, "naout", ("out", t, f))
                    r = resid[:, t, f * HALF:(f + 1) * HALF]
                    v.tensor_tensor(r, r, b[:, :], ALU.add).then_inc(done, 1)
            norm(4)
            mixture(1, 1)
            norm(5)
            embedding(1)
            norm(6)


def shape_constants():
    half = RET_DK // 2
    inv = np.float32(10000.0) ** (-np.arange(0, RET_DK, 2, dtype=np.float32) / np.float32(RET_DK))
    ang = inv.astype(np.float32)[:, None] * np.arange(SEQ_S, dtype=np.float32)[None, :]
    diff = np.arange(STRIP, dtype=np.float32)[None, :] - STRIP0 - np.arange(P, dtype=np.float32)[:, None]

    def window(rows, cols, tile, first, n):
        q = tile * cols + np.tile(np.arange(cols), rows)
        k = np.concatenate([(first + j) * cols + np.tile(np.arange(cols), rows) for j in range(n)])
        start = np.clip(q - NA_WIN // 2, 0, GRID_W - NA_WIN)
        ok = (k[None, :] >= start[:, None]) & (k[None, :] < start[:, None] + NA_WIN)
        return np.where(ok, 0.0, MASKED)

    mask = np.concatenate([window(ROWS_P, COLS_P, 0, 0, 2), window(ROWS_P, COLS_P, 1, 0, 2),
                           window(ROWS_S, COLS_S, 0, 0, 2), window(ROWS_S, COLS_S, 1, 0, 3),
                           window(ROWS_S, COLS_S, 3, 2, 2)], axis=1)
    assert mask.shape[1] == MASK_W and half == P
    mask_bits = (np.ascontiguousarray(mask, dtype=np.float32).view(np.uint32) >> 16).astype(np.uint16)
    return {"rope_cos": np.cos(ang).astype(np.float32), "rope_sin": np.sin(ang).astype(np.float32),
            "row_minus_col": diff.astype(np.float32), "col_mask": mask_bits}


_INS = ["x_prompt", "x_sample", "p_prompt", "p_sample", "ret_w_in", "ret_decay_logit", "ret_gn_w", "ret_w_out",
        "na_w_in", "na_rpb", "na_w_out", "mix_norm", "ffn_norm", "ple_norm", "router_w", "exp_w_gate", "exp_w_up",
        "exp_w_down", "ple_w_up", "ple_w_gate", "final_norm"]


def kernel(**inputs):
    import concourse.bacc as bacc
    from concourse.bass_utils import run_bass_kernel_spmd

    nc = bacc.Bacc("TRN2", target_bir_lowering=False, num_devices=1)
    arrays, args = {}, []
    given = {name: np.ascontiguousarray(inputs[name]) for name in _INS}
    given["na_rpb"] = np.pad(given["na_rpb"].reshape(-1), RPB_PAD)
    given.update(shape_constants())
    for name, a in given.items():
        arrays[f"in_{name}"] = a
        args.append(nc.dram_tensor(f"in_{name}", a.shape, mybir.dt.from_np(a.dtype), kind="ExternalInput").ap())
    for name, rows in (("y_prompt", SEQ_P), ("y_sample", SEQ_S)):
        args.append(nc.dram_tensor(name, (1, rows, D), F32, kind="ExternalOutput").ap())
    build(nc, *args)
    r = run_bass_kernel_spmd(nc, [arrays], core_ids=[0])
    return r.results[0]["y_prompt"], r.results[0]["y_sample"]
```

```python
from contextlib import ExitStack

import numpy as np
import concourse.bass as bass
from concourse import mybir

ALU = mybir.AluOpType
ACT = mybir.ActivationFunctionType
AX_X = mybir.AxisListType.X
F32 = mybir.dt.float32
F32R = mybir.dt.float32r
BF16 = mybir.dt.bfloat16
U32 = mybir.dt.uint32

P = 128
D = 1024
DT = D // P
SEQ_P, SEQ_S = 256, 512
TOK = SEQ_P + SEQ_S
TT = TOK // P
GROUPS = [(0, SEQ_P), (SEQ_P, SEQ_S)]
HALF = 512
EPS = 1e-6

RET_HEADS, RET_DK, RET_DV = 4, 256, 512
STRIP = SEQ_S + SEQ_S - P
STRIP0 = SEQ_S - P

GRID_W = 64
NA_HEADS, NA_DH = 16, 64
QUAD = 4
QUADS = NA_HEADS // QUAD
ROWS_P, ROWS_S = SEQ_P // GRID_W, SEQ_S // GRID_W
COLS_P, COLS_S = P // ROWS_P, P // ROWS_S
NA_WIN = 16
RPB_A, RPB_B = 15, 31
RPB_PAD = 64
WIDE_S, WIDE_P = 3 * COLS_S, 3 * COLS_P
A_P = 2 * ROWS_P - 1
A0_P = RPB_A // 2 - (ROWS_P - 1)

EXPERTS = 16
CAP_P, CAP_S = 2 * SEQ_P // EXPERTS, 2 * SEQ_S // EXPERTS
CAP = CAP_P + CAP_S
SAMPLE0 = 32
SPREAD = SAMPLE0 + EXPERTS
PLE = 256
MASKED = -1e30

MOE_USES = ["g0", "u0", "g1", "u1", "y0", "y1"]

NA_KEYS = [(0, 2, 0), (0, 2, 256), (2, 2, 512), (2, 3, 768), (3, 3, 768), (4, 2, 1152)]
MASK_W = 1408


def at(base, per, i):
    return base + i * per if per else base


class Plan:

    def __init__(self, n):
        self.count = [0] * n
        self.where = {}

    def add(self, phase, keys, passes=1):
        places = [place for _, place in keys]
        local = {}
        for key, place in keys:
            local[place] = local.get(place, 0) + 1
            per = places.count(place) if passes > 1 else 0
            self.where[phase, key] = (place, self.count[place] + local[place], per)
        for place, n in local.items():
            self.count[place] += n * passes

    def get(self, phase, key, i):
        place, first, per = self.where[phase, key]
        return place, first, per, at(first, per, i)


class Chain:

    def __init__(self, eng, sem):
        self.eng, self.sem, self.base, self.local, self.i, self.per = eng, sem, 0, 0, 0, 0

    def link(self, ins):
        ins.then_inc(self.sem, 1)
        self.local += 1
        self.eng.wait_ge(self.sem, at(self.base + self.local, self.per, self.i))

    def enter(self, i, per):
        self.base += self.local
        self.local, self.i, self.per = 0, i, per

    def leave(self, passes):
        assert self.local == self.per, (self.local, self.per)
        self.base += self.per * passes
        self.local, self.i, self.per = 0, 0, 0


def psum_keys(keys):
    return [(k, n % 8) for n, k in enumerate(keys)]


def ret_keys():
    keys = []
    for g, (_, n) in enumerate(GROUPS):
        nt = n // P
        keys += [("qk", g, f) for f in range(4)]
        keys += [(k, g, t) for k in "vsg" for t in range(nt)]
        keys += [("o", g, t) for t in range(nt)]
        keys += [("tr", g, t) for t in range(nt - 1)]
        out = [("out", g, t, f) for f in range(2) for t in range(nt)]
        keys += out[0:1] + [("tr", g, nt - 1)] + out[1:]
    return keys


def na_units():
    return [(t, h) for t in range(TT) for h in range(QUAD)]


NA_STEPS = TT * QUAD + 4

NA_DENSE = {2 * f + half: (("qk", f), (half,)) for f in range(4) for half in range(2)}
NA_DENSE.update({8: (("v", 2), (0, 1)), 9: (("v", 3), (0, 1)), 10: (("v", 4), (0,)), 11: (("v", 4), (1,)),
                 12: (("v", 5), (0,)), 13: (("v", 5), (1,))})
NA_NEXT = [("nqk", f) for f in range(4)] + [("nv", t) for t in range(2)]
NA_DENSE.update({15 + 2 * k + half: (key, (half,)) for k, key in enumerate(NA_NEXT) for half in range(2)})
NA_SPLITS = [((0, 1, 2, 3), ("s", 0)), ((4, 5, 6, 6), ("qk", 1)), ((8, 9, 10, 11), ("qk", 3)),
             ((14, 15, 16, 17), ("v", 5)), ((19, 20, 21, 22), ("nqk", 1)), ((23, 24, 25, 26), ("nqk", 3))]


def na_pieces(u, more):
    out = []
    for c, (steps, before) in enumerate(NA_SPLITS):
        for k, step in enumerate(steps):
            if step == u and (more or c < 4):
                phase, chunk = ("na", c) if more else ("nal", c) if c < 2 else ("naout", c - 2)
                out.append((phase, chunk, k, before))
    return out


def na_step(u, more):
    units = na_units()
    n = len(units)
    part = lambda k: units[k] if 0 <= k < n else None
    dense = NA_DENSE.get(u)
    if dense and not more and dense[0][0][0] == "n":
        dense = None
    before = NA_DENSE.get(u - 1)
    ready = before[0] if before and before[1][-1] == 1 and (more or before[0][0][0] != "n") else None
    return part(u), part(u - 2), part(u - 3), part(u - 4), dense, ready


def na_keys(more):
    keys = []
    for u in range(NA_STEPS):
        score, trans, out, close, dense, _ = na_step(u, more)
        if score:
            keys.append(("s", u))
        if trans:
            keys.append(("pt", u - 2))
        if out and out[1] == 0:
            keys.append(("o", out[0]))
        if close and close[1] == QUAD - 1:
            keys.append(("tr", close[0]))
        if dense and dense[1][0] == 0:
            keys.append(dense[0])
    place = {"s": [0, 1], "pt": [2, 3], "o": [4, 5], "tr": [6]}
    seen = {}
    out = []
    for k in keys:
        n = seen.get(k[0], 0)
        seen[k[0]] = n + 1
        banks = place.get(k[0], [7])
        out.append((k, banks[n % len(banks)]))
    return out


def build(nc, x_prompt, x_sample, p_prompt, p_sample, ret_w_in, ret_decay_logit, ret_gn_w, ret_w_out,
          na_w_in, na_rpb_padded, na_w_out, mix_norm, ffn_norm, ple_norm, router_w, exp_w_gate, exp_w_up,
          exp_w_down, ple_w_up, ple_w_gate, final_norm, rope_cos, rope_sin, row_minus_col, col_mask,
          y_prompt, y_sample):
    ctx = ExitStack()
    with ctx:
        def sb(name, shape, dt=F32):
            return ctx.enter_context(nc.sbuf_tensor(name, shape, dt))

        def sem(name):
            return ctx.enter_context(nc.semaphore(name))

        rows_normed = [nc.dram_tensor(f"rows_normed{l}", [TOK, D], F32, kind="Internal").ap() for l in range(2)]
        rows_summed = [nc.dram_tensor(f"rows_summed{l}", [TOK, D], F32, kind="Internal").ap() for l in range(2)]
        bias_s = nc.dram_tensor("bias_s", [COLS_S, NA_HEADS, RPB_A, WIDE_S], F32, kind="Internal").ap()
        bias_p = nc.dram_tensor("bias_p", [COLS_P, NA_HEADS, A_P, WIDE_P], F32, kind="Internal").ap()

        KB = 1024
        arena = nc.sbuf_base + (-nc.sbuf_base) % 64
        sb("arena", [P, (arena - nc.sbuf_base + 200 * KB) // 4])

        def put(name, shape, at_kb, dt=F32):
            return nc.alloc_sbuf_tensor_at(name, shape, dt, offset=arena + int(at_kb * KB))

        wt = put("wt", [P, 6, 4096], 0)
        raw = put("raw", [P, 2, 2048], 0)
        d_parts = put("d_parts", [P, 2, 2, 2048], 16, F32R)
        xt = [put(f"xt{k}", [P, DT, TOK], 96 + 24 * k, F32R) for k in range(2)]
        w_parts = put("w_parts", [P, 3, 2, 2048], 96, F32R)
        resid = put("resid", [P, TT, D], 144)
        xn = put("xn", [P, 2, D], 168)
        xn_all = put("xn_all", [P, TT, D], 168)
        bias = put("bias", [P, QUAD, 8 * WIDE_S + 4 * WIDE_P], 176)
        cos_t = put("cos_t", [P, SEQ_S], 188)
        sin_t = put("sin_t", [P, SEQ_S], 190)
        gain = put("gain", [P, 2, D], 192)
        r_qk = put("r_qk", [P, 4, SEQ_S], 48)
        r_v = put("r_v", [P, 4, RET_DV], 56)
        r_s = put("r_s", [P, 4, SEQ_S], 64)
        r_ot = [put(f"r_ot{k}", [P, 4, SEQ_S], 72 + 8 * k, F32R) for k in range(2)]
        r_diff = put("r_diff", [P, STRIP], 88)
        r_strip = put("r_strip", [P, STRIP], 91.5)
        rw = put("rw", [P, 2, DT, EXPERTS], 95)
        lgt = put("lgt", [P, 8, 8], 184)
        r_tmp = put("r_tmp", [P, 4, 512], 176)
        r_og = [put(f"r_og{t}", [P, 512], kb) for t, kb in enumerate((184, 186, 192, 194))]
        r_gn = put("r_gn", [P, 2 * D], 168)
        m_x = put("m_x", [CAP, D], 144)
        m_silu = put("m_silu", [CAP, 2, HALF], 148)
        m_hid = put("m_hid", [CAP, D], 152)
        m_y = put("m_y", [CAP, D], 156)
        m_xt = [put(f"m_xt{k}", [P, DT, CAP], 176 + 3 * k, F32R) for k in range(2)]
        m_hidt = [put(f"m_hidt{k}", [P, DT, CAP], 182 + 3 * k, F32R) for k in range(2)]
        m_lt = [put(f"m_lt{l}", [EXPERTS, TOK], 192 + 4 * l) for l in range(2)]
        m_lg = [put(f"m_lg{l}", [P, TT, EXPERTS], 195 + 4 * l) for l in range(2)]
        m_at = [put(f"m_at{l}", [SPREAD, SEQ_S], 192 + 4 * l) for l in range(2)]
        m_af = [put(f"m_af{l}", [P, SEQ_S // P, SPREAD], 194 + 4 * l) for l in range(2)]
        e_p = put("e_p", [P, TT, PLE], 48)
        e_pt = [put(f"e_pt{k}", [P, 2, TOK], 54 + 6 * k, F32R) for k in range(2)]
        e_sig = put("e_sig", [P, 2, HALF], 66)
        e_prod = put("e_prod", [P, 2, HALF], 70)
        e_u = put("e_u", [P, 2, 2048], 74, F32R)
        n_qk = put("n_qk", [P, 4, TOK], 48)
        n_v = put("n_v", [P, TT, 256], 60)
        n_ot = put("n_ot", [P, DT, TOK], 66)
        n_s = put("n_s", [P, 2, 3 * P], 90)
        n_p = put("n_p", [P, 2, 3 * P], 168)
        n_pt = put("n_pt", [P, 2, 3 * P], 171)
        n_o = put("n_o", [P, 2, 256], 174)
        ident = sb("ident", [P, P])
        ident16 = sb("ident16", [P, P], BF16)
        mask = sb("mask", [P, MASK_W], BF16)
        rw_parts = [sb(f"rw_parts{k}", [P, 2, DT, EXPERTS], F32R) for k in range(2)]
        sumsq = sb("sumsq", [P, 8])
        meansq = sb("meansq", [P, 8])
        rstd = sb("rstd", [P, 8])
        minus_half = sb("minus_half", [P, 8])
        lg = sb("lg", [P, 2 * RET_HEADS])
        stats = sb("stats", [P, TT, 6])
        mv = sb("mv", [P, TT, 2])
        mvr = sb("mvr", [P, TT])
        top_v = sb("top_v", [SPREAD, CAP])
        top_i = sb("top_i", [SPREAD, CAP], U32)
        top_f = sb("top_f", [SPREAD, CAP])
        gate_t = sb("gate_t", [CAP, EXPERTS])
        idx_t = sb("idx_t", [CAP, EXPERTS], U32)
        idx_in = sb("idx_in", [CAP, 1], U32)
        idx_out = sb("idx_out", [CAP, 1], U32)
        rsm = sb("rsm", [P, 4, 8])
        mx = sb("mx", [P, 2])
        nmx = sb("nmx", [P, 2])
        den = sb("den", [P, 2, QUAD])
        rden = sb("rden", [P, QUAD])

        bank = [ctx.enter_context(nc.psum_tensor(f"bank{b}", [P, HALF], F32)) for b in range(8)]

        psum, slot = Plan(8), Plan(6)
        norm_uses = [(("t", t, c), (2 * t + c) % 8) for t in range(TT) for c in range(2)]
        moe_uses = [("g0", 0), ("u0", 1), ("g1", 2), ("u1", 3), ("x0", 4), ("x1", 5), ("h0", 6), ("h1", 7),
                    ("y0", 4), ("y1", 5)]

        def plan_moe(l):
            psum.add(f"route{l}", [("lt0", 0), ("lt1", 1), ("logit", 2), ("aff", 3), ("gate", 5), ("idx", 6)])
            psum.add(f"first{l}", [("x0", 4), ("x1", 5)])
            psum.add(f"moe{l}", moe_uses, EXPERTS - 1)
            psum.add(f"last{l}", [(k, b) for k, b in moe_uses if k[0] != "x"])

        def plan_ple(l):
            psum.add(f"ple{l}", psum_keys([(k, t, f) for f in range(2) for k in "gu" for t in range(TT)]))

        def plan_inputs(l):
            psum.add(f"inputs{l}", psum_keys([("pt", t) for t in range(TT)]))

        psum.add("norm0", norm_uses)
        psum.add("ret", psum_keys(ret_keys()), RET_HEADS)
        psum.add("norm1", norm_uses)
        plan_moe(0)
        plan_inputs(0)
        psum.add("norm2", norm_uses)
        plan_ple(0)
        psum.add("norm3", norm_uses)
        psum.add("na0", [(k, 7) for k in NA_NEXT])
        psum.add("na", na_keys(True), QUADS - 1)
        psum.add("nal", na_keys(False))
        psum.add("naout", psum_keys([("out", t, f) for f in range(2) for t in range(TT)]))
        psum.add("norm4", norm_uses)
        plan_moe(1)
        plan_inputs(1)
        psum.add("norm5", norm_uses)
        plan_ple(1)

        for l in range(2):
            slot.add(f"moe{l}", [(s, s) for s in range(6)], EXPERTS)

        chunks = {"ret": [], "ple": [], "na": [], "naout": []}
        for g, (_, n) in enumerate(GROUPS):
            nt = n // P
            chunks["ret"] += [(2, None), (2, ("qk", g, 3)), (1, None), (1, ("v", g, nt - 1)),
                              (1, None), (1, ("g", g, nt - 1)), (1, ("out", g, nt - 1, 0)), (1, ("out", g, nt - 1, 1))]
        chunks["ple"] = [(1, ("u", TT - 1, 1)), (1, None), (1, ("g", TT - 1, 0)), (1, None), (1, ("g", TT - 1, 1))]
        chunks["na0"] = [(1, ("nqk", 1)), (1, ("nqk", 3)), (1, ("nv", 1)), (1, None)]
        chunks["na"] = [(1, None)] * 6
        chunks["nal"] = [(1, None)] * 2
        chunks["naout"] = [(1, None), (1, ("out", TT - 1, 0)), (1, None), (1, ("out", TT - 1, 1))]
        raw_loads, splits_n, goes_on = Plan(2), Plan(1), Plan(1)

        def buffer_of(phase, c):
            return (c + (phase[0] == "n")) % 2

        def pieces_of(phase):
            return 4 if phase[0] == "n" else 1

        def plan_chunks(phase, kind, passes=1):
            raw_loads.add(phase, [((c, k), buffer_of(phase, c)) for c, (n, _) in enumerate(chunks[kind]) for k in range(n)],
                          passes)
            splits_n.add(phase, [((c, k), 0) for c in range(len(chunks[kind])) for k in range(pieces_of(phase))], passes)
            if phase[0] != "n" or phase == "naout":
                goes_on.add(phase, [(c, 0) for c, (_, end) in enumerate(chunks[kind]) if end is None], passes)

        plan_chunks("ret", "ret", RET_HEADS)
        plan_chunks("ple0", "ple")
        plan_chunks("na0", "na0")
        plan_chunks("na", "na", QUADS - 1)
        plan_chunks("nal", "nal")
        plan_chunks("naout", "naout")
        plan_chunks("ple1", "ple")

        bank_full = [sem(f"bank_full{b}") for b in range(8)]
        bank_free = [sem(f"bank_free{b}") for b in range(8)]
        slot_full = [sem(f"slot_full{s}") for s in range(6)]
        raw_full = [sem(f"raw_full{b}") for b in range(2)]
        part_h, part_l = sem("part_h"), sem("part_l")
        part_used = sem("part_used")
        norm_hi = [sem(f"norm_hi{n}") for n in range(6)]
        rw_h, rw_l = sem("rw_h"), sem("rw_l")
        ret_th, ple_th, na_th = sem("ret_th"), [sem(f"ple_th{l}") for l in range(2)], sem("na_th")
        na_tl = sem("na_tl")
        dve_step, pool_step = sem("dve_step"), sem("pool_step")
        held = sem("held")
        x_in = [sem(f"x_in{g}") for g in range(2)]
        decay_in, first_gain_in = sem("decay_in"), sem("first_gain_in")
        const_in, bias_table, gn_in, ident_set = sem("const_in"), sem("bias_table"), sem("gn_in"), sem("ident_set")
        gain_in = [sem(f"gain_in{b}") for b in range(2)]
        norm_sq = [sem(f"norm_sq{n}") for n in range(7)]
        norm_rs = [sem(f"norm_rs{n}") for n in range(7)]
        norm_rows = [sem(f"norm_rows{n}") for n in range(7)]
        rows_out = [sem(f"rows_out{l}") for l in range(2)]
        final_out = [sem(f"final_out{b}") for b in range(2)]
        decay_abs, decay_exp = sem("decay_abs"), sem("decay_exp")
        strip_arg, strip_set = sem("strip_arg"), sem("strip_set")
        ret_rot = sem("ret_rot")
        ret_var, ret_rstd, ret_og = sem("ret_var"), sem("ret_rstd"), sem("ret_og")
        moe_exp = [sem(f"moe_exp{l}") for l in range(2)]
        moe_aff = [sem(f"moe_aff{l}") for l in range(2)]
        moe_top = [sem(f"moe_top{l}") for l in range(2)]
        moe_rows = [sem(f"moe_rows{l}") for l in range(2)]
        moe_wh = [sem(f"moe_wh{l}") for l in range(2)]
        moe_wl = [sem(f"moe_wl{l}") for l in range(2)]
        moe_wused = [sem(f"moe_wused{l}") for l in range(2)]
        moe_th = [sem(f"moe_th{l}") for l in range(2)]
        moe_added = [sem(f"moe_added{l}") for l in range(2)]
        moe_y_free = [sem(f"moe_y_free{l}") for l in range(2)]
        resid_saved = [sem(f"resid_saved{l}") for l in range(2)]
        resid_in = [[sem(f"resid_in{l}_{g}") for g in range(2)] for l in range(2)]
        p_in = [sem(f"p_in{l}") for l in range(2)]
        ple_add = [sem(f"ple_add{l}") for l in range(2)]
        na_bias, na_max, na_exp = [sem(f"na_bias{g}") for g in range(2)], sem("na_max"), sem("na_exp")

        def fill(pe, phase, key, i=0):
            b, first, per, _ = psum.get(phase, key, i)
            if first > 1 or per:
                pe.wait_ge(bank_free[b], at(first - 1, per, i))
            return bank[b], bank_full[b]

        def filled(eng, phase, key, i=0):
            b, _, _, n = psum.get(phase, key, i)
            eng.wait_ge(bank_full[b], n)
            return bank[b], bank_free[b]

        def matmuls_done(eng, phase, key, i=0):
            b, _, _, n = psum.get(phase, key, i)
            eng.wait_ge(bank_full[b], n)

        def drained(eng, phase, key, i=0):
            b, _, _, n = psum.get(phase, key, i)
            eng.wait_ge(bank_free[b], n)

        def split_done(eng, l, s, e):
            eng.wait_ge(moe_wl[l], at(2 * s + 2, 12, e))

        def parts_free(eng, l, c, phase, e):
            c = c - 3
            if c % 2 == 0:
                eng.wait_ge(moe_wused[l], at(c // 2 + 1, 6, e))
            else:
                matmuls_done(eng, phase, MOE_USES[c // 2], e if phase[0] == "m" else 0)

        def hold(eng):
            eng.sem_inc(held, 1)

        def prompt_ready(eng, key, q):
            per = psum.get("na", key, 0)[2]
            b, first, _, _ = psum.get("na0", key, 0)
            eng.wait_ge(bank_free[b], at(first, per, q))

        def raw_free(eng, phase, c, i=0):
            _, _, _, n = splits_n.get(phase, (c, pieces_of(phase) - 1), i)
            eng.wait_ge(part_l, n)

        def part_free(eng, phase, end_phase, c, i=0, kind=None, before=0):
            end = chunks[kind or phase][c][1]
            if end is None:
                _, first, per, _ = goes_on.get(phase, c, 0)
                eng.wait_ge(part_used, at(first - before * per, per, i))
            else:
                b, first, per, _ = psum.get(end_phase, end, 0)
                eng.wait_ge(bank_full[b], at(first - before * per, per, i))

        def piece(phase, k, n=2048):
            w = n // pieces_of(phase)
            return slice(k * w, (k + 1) * w)

        def high_of_chunk(act, phase, c, i=0, dst=None, pieces=None):
            n_dmas = chunks[phase.rstrip("01") if phase[0] in "pr" else phase][c][0]
            b, first, per, _ = raw_loads.get(phase, (c, n_dmas - 1), 0)
            for k in pieces or range(pieces_of(phase)):
                if k == 0:
                    act.wait_ge(raw_full[b], at(16 * first, 16 * per, i))
                cols = piece(phase, k)
                nc.scalar.copy((d_parts[:, b, 0, :] if dst is None else dst)[:, cols], raw[:, b, cols]).then_inc(part_h, 1)

        def low_of_chunk(dve, phase, c, i=0, dst=None, pieces=None):
            b = buffer_of(phase, c)
            high, low = (d_parts[:, b, 0, :], d_parts[:, b, 1, :]) if dst is None else dst
            for k in pieces or range(pieces_of(phase)):
                cols = piece(phase, k)
                dve.wait_ge(part_h, splits_n.get(phase, (c, k), i)[3])
                nc.vector.tensor_tensor(low[:, cols], raw[:, b, cols], high[:, cols].bitcast(F32), ALU.subtract)\
                    .then_inc(part_l, 1)

        def natural_rows(src_p, src_s, tiles):
            return [(src_p.rearrange("(t p) d -> p t d", p=P), tiles[:, 0:2, :]),
                    (src_s.rearrange("(t p) d -> p t d", p=P), tiles[:, 2:TT, :])]

        def grid_rows(src_p, src_s, tiles):
            out = []
            for r in range(ROWS_P):
                out.append((src_p[r * GRID_W:(r + 1) * GRID_W, :].rearrange("(t c) d -> c t d", c=COLS_P),
                            tiles[r * COLS_P:(r + 1) * COLS_P, 0:2, :]))
            for r in range(ROWS_S):
                out.append((src_s[r * GRID_W:(r + 1) * GRID_W, :].rearrange("(t c) d -> c t d", c=COLS_S),
                            tiles[r * COLS_S:(r + 1) * COLS_S, 2:TT, :]))
            return out

        def normed(n, t):
            return xn_all[:, t, :] if n in (1, 4) else xn[:, t % 2, :]

        def row_pairs(pairs):
            n = 1 if len(pairs) == 2 else ROWS_P
            return [(int(k >= n), pair) for k, pair in enumerate(pairs)]

        def row_dmas(order):
            return ROWS_P + ROWS_S if order else 2

        block = ctx.enter_context(nc.Block())

        @block.sync
        def _(sp):
            sp.dma_start(lgt[:, 0, :], ret_decay_logit.rearrange("a b h -> a (b h)").broadcast_to([P, 8]))\
                .then_inc(decay_in, 16)
            sp.dma_start(resid[:, 0:2, :], x_prompt[0].rearrange("(t p) d -> p t d", p=P)).then_inc(x_in[0], 16)
            sp.dma_start(gain[:, 0, :], mix_norm[0:1, :].broadcast_to([P, D])).then_inc(first_gain_in, 16)
            sp.dma_start(resid[:, 2:TT, :], x_sample[0].rearrange("(t p) d -> p t d", p=P)).then_inc(x_in[1], 16)

            def block_of(w, t0, nt, first, n):
                return w.rearrange("(t p) f -> p t f", p=P)[:, bass.ds(t0, nt), bass.ds(first, n)]

            def chunk(phase, c, *srcs):
                b = buffer_of(phase, c)
                nt, n = srcs[0].shape[1], srcs[0].shape[2]
                dst = raw[:, b, 0:nt * n * len(srcs)].rearrange("p (t f) -> p t f", t=nt)
                for k, src in enumerate(srcs):
                    sp.dma_start(dst[:, :, k * n:(k + 1) * n], src).then_inc(raw_full[b], 16)

            def ret_chunk(c, h):
                w = ret_w_in[0]
                k, half = c % 8 // 2, c % 2
                if k == 0:
                    return [block_of(w, 4 * half, 4, h * 256 + j * D, 256) for j in range(2)]
                if k < 3:
                    return [block_of(w, 4 * half, 4, h * 512 + 2 * k * D, 512)]
                return [block_of(ret_w_out[0], h * 4, 4, half * HALF, HALF)]

            for c in range(len(chunks["ret"])):
                if c == 2:
                    sp.dma_start(r_diff[:, :], row_minus_col).then_inc(const_in, 16)
                    sp.dma_start(cos_t[:], rope_cos).then_inc(const_in, 16)
                    sp.dma_start(sin_t[:], rope_sin).then_inc(const_in, 16)
                    sp.dma_start(mask[:], col_mask.bitcast(BF16)).then_inc(const_in, 16)
                    sp.dma_start(rw[:, :, :, :].rearrange("p l t e -> p (l t) e"),
                                 router_w.rearrange("l (t p) e -> p (l t) e", p=P)).then_inc(const_in, 16)
                if c >= 2:
                    raw_free(sp, "ret", c - 2, 0)
                chunk("ret", c, *ret_chunk(c, 0))
            with sp.Fori(1, RET_HEADS) as h:
                for c in range(len(chunks["ret"])):
                    raw_free(sp, "ret", (c - 2) % 16, h if c >= 2 else h - 1)
                    chunk("ret", c, *ret_chunk(c, h))

            def shifted(first, n_a, wide):
                v = na_rpb_padded[bass.ds(first, 64)]
                return bass.AP(tensor=v.tensor, offset=v.offset,
                               ap=[[RPB_A * RPB_B, NA_HEADS], [RPB_B, n_a], [1, wide]])

            with sp.Fori(0, COLS_S) as c:
                sp.dma_start(bias_s[c], shifted(RPB_PAD + NA_WIN - 1 - COLS_S - c, RPB_A, WIDE_S))\
                    .then_inc(bias_table, 16)
            with sp.Fori(0, COLS_P) as c:
                sp.dma_start(bias_p[c], shifted(RPB_PAD + A0_P * RPB_B + NA_WIN - 1 - COLS_P - c, A_P, WIDE_P))\
                    .then_inc(bias_table, 16)

            def slot_view(s):
                return wt[:, s, :].rearrange("p (t f) -> p t f", t=DT)

            def moe_loads(l, *before):
                order = [(2 * f + k, w, f) for f in range(2) for k, w in enumerate((exp_w_gate, exp_w_up))]
                order += [(4 + f, exp_w_down, f) for f in range(2)]
                matmuls_done(sp, *before)
                for s, w, f in order:
                    if s == 5:
                        sp.wait_ge(moe_rows[l], 16)
                    sp.dma_start(slot_view(s), block_of(w[l, 0], 0, DT, f * HALF, HALF)).then_inc(slot_full[s], 16)
                with sp.Fori(1, EXPERTS) as e:
                    for s, w, f in order:
                        split_done(sp, l, s, e - 1)
                        sp.dma_start(slot_view(s), block_of(w[l, e], 0, DT, f * HALF, HALF)).then_inc(slot_full[s], 16)

            def ple_loads(l, order):
                w = ple_w_gate[l]
                srcs = [block_of(ple_w_up[l], 0, 2, 0, D)] + [block_of(w, 4 * k, 4, f * HALF, HALF)
                                                              for f in range(2) for k in range(2)]
                split_done(sp, l, 0, EXPERTS - 1)
                for c in range(2):
                    chunk(f"ple{l}", c, srcs[c])
                rows = grid_rows if order else natural_rows
                split_done(sp, l, 5, EXPERTS - 1)
                for g, (dram, tiles) in row_pairs(rows(p_prompt[l, 0], p_sample[l, 0], e_p)):
                    sp.dma_start(tiles, dram).then_inc(p_in[l], 16)
                raw_free(sp, f"ple{l}", 0)
                chunk(f"ple{l}", 2, srcs[2])
                sp.wait_ge(moe_added[l], 16 * EXPERTS)
                src = rows_summed[l]
                for g, (dram, tiles) in row_pairs(rows(src[0:SEQ_P, :], src[SEQ_P:TOK, :], resid)):
                    sp.dma_start(tiles, dram).then_inc(resid_in[l][g], 16)
                for c in range(3, 5):
                    raw_free(sp, f"ple{l}", c - 2)
                    chunk(f"ple{l}", c, srcs[c])

            sp.wait_ge(rw_l, 1)
            moe_loads(0, "ret", ("out", 1, 3, 1), RET_HEADS - 1)
            ple_loads(0, 1)

            def qkv(which, q):
                return block_of(na_w_in[0], 0, DT, q * 256 + "qkv".index(which) * D, 256)

            for c, which in enumerate("qkvq"):
                if c < 2:
                    raw_free(sp, "ple0", 3 + c)
                else:
                    raw_free(sp, "na0", c - 2)
                chunk("na0", c, qkv(which, 0))

            def na_chunks(q, phase, i, prior):
                srcs = [qkv("k", q), qkv("v", q)]
                if phase == "na":
                    srcs += [qkv(which, q + 1) for which in "qkvq"]
                for c, src in enumerate(srcs):
                    if c < 2:
                        prior(c)
                    else:
                        raw_free(sp, phase, c - 2, i)
                    chunk(phase, c, src)

            na_chunks(0, "na", 0, lambda c: raw_free(sp, "na0", 2 + c))
            with sp.Fori(1, QUADS - 1) as q:
                na_chunks(q, "na", q, lambda c: raw_free(sp, "na", 4 + c, q - 1))
            na_chunks(QUADS - 1, "nal", 0, lambda c: raw_free(sp, "na", 4 + c, QUADS - 2))
            for c in range(4):
                if c < 2:
                    raw_free(sp, "nal", c)
                else:
                    raw_free(sp, "naout", c - 2)
                chunk("naout", c, block_of(na_w_out[0], 4 * (c % 2), 4, c // 2 * HALF, HALF))
            moe_loads(1, "naout", ("out", TT - 1, 1), 0)
            ple_loads(1, 0)

        @block.gpsimd
        def _(pool):
            chain = Chain(pool, pool_step)
            gains = [mix_norm[0], ffn_norm[0], ple_norm[0], mix_norm[1], ffn_norm[1], ple_norm[1], final_norm]

            def load_gain(n):
                pool.dma_start(gain[:, n % 2, :], gains[n].rearrange("(a d) -> a d", a=1).broadcast_to([P, D]))\
                    .then_inc(gain_in[n % 2], 16)

            for m in (ident, ident16):
                chain.link(nc.gpsimd.memset(m[:], 0.0))
                nc.gpsimd.affine_select(out=m[:], in_=m[:], compare_op=ALU.not_equal, fill=1.0, base=0,
                                        pattern=[[-1, P]], channel_multiplier=1).then_inc(ident_set, 1)
            chain.link(nc.gpsimd.memset(minus_half[:], -0.5))
            def rsqrt(src, scale, dst, t):
                chain.link(nc.gpsimd.tensor_scalar(meansq[:, t:t + 1], src, scale, EPS, ALU.mult, ALU.add))
                return nc.gpsimd.tensor_tensor(dst, meansq[:, t:t + 1], minus_half[:, 0:1], ALU.pow)

            def norm(n, l=None, order=0):
                for t in range(TT):
                    pool.wait_ge(norm_sq[n], t + 1)
                    rsqrt(sumsq[:, t:t + 1], 1.0 / D, rstd[:, t:t + 1], t).then_inc(norm_rs[n], 1)
                if l is not None:
                    rows = grid_rows if order else natural_rows
                    for dram, src, ready, done in ((rows_summed[l], resid, norm_sq[n], resid_saved[l]),
                                                   (rows_normed[l], xn_all, norm_rows[n], rows_out[l])):
                        pool.wait_ge(ready, TT)
                        for d, tiles in rows(dram[0:SEQ_P, :], dram[SEQ_P:TOK, :], src):
                            pool.dma_start(d, tiles).then_inc(done, 16)
                if 1 <= n < 6 and l is None:
                    load_gain(n + 1)

            def mixture(l, order):
                pool.wait_ge(resid_saved[l], 16 * row_dmas(order))
                pool.wait_ge(rows_out[l], 16 * row_dmas(order))
                drained(pool, f"route{l}", "idx")

                def gather(e):
                    chain.link(nc.gpsimd.tensor_copy(idx_in[:], idx_t[:, bass.ds(e, 1)]))
                    hold(pool)
                    nc.gpsimd.indirect_dma_start(
                        out=m_x[:, :], out_offset=None, in_=rows_normed[l],
                        in_offset=bass.IndirectOffsetOnAxis(ap=idx_in[:, :], axis=0)).then_inc(moe_rows[l], 16)

                def scatter(phase, e, n):
                    drained(pool, phase, "y1", e)
                    chain.link(nc.gpsimd.tensor_copy(idx_out[:], idx_t[:, bass.ds(n, 1)]))
                    hold(pool)
                    nc.gpsimd.indirect_dma_start(
                        out=rows_summed[l], out_offset=bass.IndirectOffsetOnAxis(ap=idx_out[:, :], axis=0),
                        in_=m_y[:, :], in_offset=None, compute_op=ALU.add).then_inc(moe_added[l], 16)
                    pool.wait_ge(moe_added[l], at(16, 16, n))
                    pool.sem_inc(moe_y_free[l], 1)

                pool.sem_inc(moe_y_free[l], 1)
                gather(0)
                load_gain(3 * l + 2)
                matmuls_done(pool, f"first{l}", "x1")
                gather(1)
                with pool.Fori(0, EXPERTS - 2) as e:
                    chain.enter(e, 2)
                    matmuls_done(pool, f"moe{l}", "x1", e)
                    gather(e + 2)
                    scatter(f"moe{l}", e, e)
                    chain.leave(EXPERTS - 2)
                scatter(f"moe{l}", EXPERTS - 2, EXPERTS - 2)
                scatter(f"last{l}", 0, EXPERTS - 1)

            def load_bias(q, g):
                rows, cols, table, w, lo = ((ROWS_P, COLS_P, bias_p, WIDE_P, 8 * WIDE_S),
                                            (ROWS_S, COLS_S, bias_s, WIDE_S, 0))[g]
                for r in range(rows):
                    a = rows - 1 - r
                    src = table[:, bass.ds(q * QUAD, QUAD), a:a + rows, :].rearrange("c h a w -> c h (a w)")
                    pool.dma_start(bias[r * cols:(r + 1) * cols, :, lo:lo + rows * w], src).then_inc(na_bias[g], 16)

            norm(0)
            load_gain(1)
            matmuls_done(pool, "norm0", ("t", TT - 1, 1))
            pool.dma_start(r_gn[:, :], ret_gn_w.broadcast_to([P, 2 * D])).then_inc(gn_in, 16)
            with pool.Fori(0, RET_HEADS) as h:
                chain.enter(h, TT)
                for t in range(TT):
                    pool.wait_ge(ret_var, at(t + 1, TT, h))
                    hold(pool)
                    rsqrt(mv[:, t, 1:2], 1.0, mvr[:, t:t + 1], t).then_inc(ret_rstd, 1)
                chain.leave(RET_HEADS)
            norm(1, 0, 0)
            mixture(0, 0)
            norm(2)
            pool.wait_ge(bias_table, 16 * (COLS_S + COLS_P))
            for g in range(2):
                load_bias(0, g)
            norm(3)
            with pool.Fori(0, QUADS - 1) as q:
                for g, last_unit in enumerate((2 * QUAD - 1, TT * QUAD - 1)):
                    drained(pool, "na", ("s", last_unit), q)
                    load_bias(q + 1, g)
            norm(4, 1, 1)
            mixture(1, 1)
            norm(5)
            outs = [y_prompt[0, 0:P], y_prompt[0, P:SEQ_P]] + [y_sample[0, t * P:(t + 1) * P] for t in range(4)]
            for t in range(TT):
                pool.wait_ge(norm_sq[6], t + 1)
                rsqrt(sumsq[:, t:t + 1], 1.0 / D, rstd[:, t:t + 1], t).then_inc(norm_rs[6], 1)
                pool.wait_ge(norm_rows[6], t + 1)
                pool.dma_start(outs[t], xn[:, t % 2, :]).then_inc(final_out[t % 2], 16)
            for b in range(2):
                pool.wait_ge(final_out[b], 16 * TT // 2)

        @block.scalar
        def _(act):
            def resid_wait(n, t):
                if n == 0:
                    act.wait_ge(x_in[0 if t < 2 else 1], 16)
                elif n == 1:
                    drained(act, "ret", ("out", 1, 3, 1), RET_HEADS - 1)
                elif n in (2, 5):
                    g = int(t >= 2)
                    act.wait_ge(resid_in[n // 3][g], 16 * ((ROWS_P, ROWS_S)[g] if n == 2 else 1))
                elif n in (3, 6):
                    act.wait_ge(ple_add[n // 3 - 1], TT + t + 1)
                else:
                    drained(act, "naout", ("out", t, 1))

            def squares(n, t):
                resid_wait(n, t)
                if t >= 2 and n in (0, 2, 3, 5):
                    matmuls_done(act, f"norm{n}", ("t", t - 2, 1))
                if t >= 2 and n == 6:
                    act.wait_ge(final_out[t % 2], 16 * (t // 2))
                nc.scalar.activation(normed(n, t), resid[:, t, :], ACT.Square,
                                     accum_out=sumsq[:, t:t + 1]).then_inc(norm_sq[n], 1)

            def norm(n):
                for t in range(TT + 1):
                    if t < TT:
                        squares(n, t)
                    for c in range(2 if t else 0):
                        b, _ = filled(act, f"norm{n}", ("t", t - 1, c))
                        nc.scalar.copy(xt[0][:, 4 * c:4 * c + 4, (t - 1) * P:t * P],
                                       b[:, :].rearrange("p (f n) -> p f n", f=4)).then_inc(norm_hi[n], 1)

            act.wait_ge(decay_abs, 1)
            nc.scalar.activation(lgt[:, 2, :], lgt[:, 1, :], ACT.Exp, scale=-1.0).then_inc(decay_exp, 1)
            norm(0)

            with act.Fori(0, RET_HEADS) as h:
                for g, (_, n) in enumerate(GROUPS):
                    nt = n // P

                    def split(k):
                        c = 8 * g + k
                        if c >= 2:
                            part_free(act, "ret", "ret", c - 2, h)
                        else:
                            part_free(act, "ret", "ret", c + 14, h, before=1)
                        high_of_chunk(act, "ret", c, h)

                    for k in range(5):
                        split(k)
                    if g == 0:
                        act.wait_ge(strip_arg, h + 1)
                        nc.scalar.activation(r_strip[:, :], r_strip[:, :], ACT.Exp).then_inc(strip_set, 1)
                    for t in range(nt):
                        b, done = filled(act, "ret", ("v", g, t), h)
                        nc.scalar.copy(r_v[:, t, :], b[:, :]).then_inc(done, 1)
                    split(5)
                    split(6)

                    def transposed(t):
                        b, _ = filled(act, "ret", ("tr", g, t), h)
                        nc.scalar.copy(r_ot[0][:, :, t * P:(t + 1) * P],
                                       b[:, :].rearrange("p (f n) -> p f n", f=4)).then_inc(ret_th, 1)

                    for t in range(nt):
                        b, done = filled(act, "ret", ("g", g, t), h)
                        nc.scalar.activation(r_tmp[:, t, :], b[:, :], ACT.Silu).then_inc(done, 1)
                        if t:
                            transposed(t - 1)
                    transposed(nt - 1)
                    split(7)

            act.wait_ge(const_in, 5 * 16)
            nc.scalar.copy(rw_parts[0][:], rw[:]).then_inc(rw_h, 1)

            def mixture(l):
                for k, (a, w) in enumerate(((0, 512), (512, 256))):
                    b, done = filled(act, f"route{l}", f"lt{k}")
                    nc.scalar.copy(m_lt[l][:, a:a + w], b[0:EXPERTS, 0:w]).then_inc(done, 1)
                drained(act, f"route{l}", "logit")
                nc.scalar.activation(m_lg[l][:], m_lg[l][:], ACT.Exp).then_inc(moe_exp[l], 1)

                def high(phase, key, i, dst, c):
                    b, _ = filled(act, phase, key, i)
                    nc.scalar.copy(dst[:, 4 * c:4 * c + 4, :],
                                   b[:, 0:4 * CAP].rearrange("p (f n) -> p f n", f=4)).then_inc(moe_th[l], 1)

                def split(c, n, before=None):
                    if c % 2 == 0:
                        s, first, per, _ = slot.get(f"moe{l}", c // 2, n)
                        act.wait_ge(slot_full[s], at(16 * first, 16 * per, n))
                    if before is not None:
                        parts_free(act, l, *before)
                    nc.scalar.copy(w_parts[:, c % 3, 0, :], wt[:, c // 2, c % 2 * 2048:c % 2 * 2048 + 2048])\
                        .then_inc(moe_wh[l], 1)

                def expert(phase, e, n):
                    def silu(f):
                        b, done = filled(act, phase, f"g{f}", e)
                        nc.scalar.activation(m_silu[:, f, :], b[0:CAP, :], ACT.Silu).then_inc(done, 1)

                    def splits(a, z):
                        for c in range(a, z):
                            split(c, n, (c, phase, e) if phase[0] == "m" else (c, phase, EXPERTS - 1))

                    splits(3, 4)
                    silu(0)
                    splits(4, 8)
                    silu(1)
                    splits(8, 10)
                    high(phase, "h0", e, m_hidt[0], 0)
                    if phase[0] == "m":
                        for c in range(2):
                            high(phase, f"x{c}", e, m_xt[0], c)
                    high(phase, "h1", e, m_hidt[0], 1)
                    splits(10, 12)
                    if phase[0] == "m":
                        for c in range(3):
                            split(c, n + 1, (c + 12, phase, e))

                act.wait_ge(moe_aff[l], 1)
                for c in range(3):
                    split(c, 0)
                for c in range(2):
                    high(f"first{l}", f"x{c}", 0, m_xt[0], c)
                with act.Fori(0, EXPERTS - 1) as e:
                    expert(f"moe{l}", e, e)
                expert(f"last{l}", 0, EXPERTS - 1)

            def embedding_weights(l):
                split_done(act, l, 5, EXPERTS - 1)
                high_of_chunk(act, f"ple{l}", 0, dst=e_u[:, 0, :])
                high_of_chunk(act, f"ple{l}", 1)
                for t in range(TT):
                    b, _ = filled(act, f"inputs{l}", ("pt", t))
                    nc.scalar.copy(e_pt[0][:, :, t * P:(t + 1) * P],
                                   b[:, 0:2 * P].rearrange("p (f n) -> p f n", f=2)).then_inc(ple_th[l], 1)

            def embedding(l):
                high_of_chunk(act, f"ple{l}", 2)
                for f in range(2):
                    if f == 0:
                        part_free(act, f"ple{l}", f"ple{l}", 1, kind="ple")
                        high_of_chunk(act, f"ple{l}", 3)
                    for t in range(TT):
                        if f or t >= 2:
                            u = TT * f + t - 2
                            drained(act, f"ple{l}", ("u", u % TT, u // TT))
                        b, done = filled(act, f"ple{l}", ("g", t, f))
                        nc.scalar.activation(e_sig[:, t % 2, :], b[:, :], ACT.Sigmoid).then_inc(done, 1)
                        if l == f == 1 and t:
                            squares(6, t - 1)
                    if f == 0:
                        part_free(act, f"ple{l}", f"ple{l}", 2, kind="ple")
                        high_of_chunk(act, f"ple{l}", 4)

            norm(1)
            mixture(0)
            embedding_weights(0)
            norm(2)
            embedding(0)
            for c in range(2):
                part_free(act, "ple0", "ple0", 3 + c, kind="ple")
                high_of_chunk(act, "na0", c)
            norm(3)

            def product_out(phase, key, q, i=0):
                kind, k = key
                a, w = (0, SEQ_P) if kind[0] == "n" else (SEQ_P, SEQ_S)
                if kind[-1] == "k" and k < 2:
                    b, done = filled(act, phase, key, i)
                    nc.scalar.mul(n_qk[:, k, a:a + w], b[:, 0:w], NA_DH ** -0.5).then_inc(done, 1)
                elif kind[-1] == "v" and k % 2 == 0:
                    b, done = filled(act, phase, key, i)
                    nc.scalar.copy(n_v[:, k, :], b[:, 0:256]).then_inc(done, 1)

            for f in range(2):
                product_out("na0", ("nqk", f), 0)
            high_of_chunk(act, "na0", 2)
            matmuls_done(act, "na0", ("nqk", 3))
            high_of_chunk(act, "na0", 3)
            product_out("na0", ("nv", 0), 0)

            def attention(phase, q, i):
                n = len(na_units())
                for u in range(NA_STEPS):
                    score, trans, _, close, _, ready = na_step(u, phase == "na")
                    if ready:
                        product_out(phase, ready, q, i)
                    if trans and u % 2 == 0:
                        w = NA_KEYS[trans[0]][1] * P
                        b, done = filled(act, phase, ("pt", u - 2), i)
                        nc.scalar.copy(n_pt[:, 0, 0:w], b[:, 0:w]).then_inc(done, 1)
                    if score:
                        t, h = score
                        w = NA_KEYS[t][1] * P
                        act.wait_ge(na_max, at(u + 1, n, q))
                        if u >= 2:
                            matmuls_done(act, phase, ("pt", u - 2), i)
                        nc.scalar.activation(n_p[:, u % 2, 0:w], n_s[:, u % 2, 0:w], ACT.Exp, bias=nmx[:, u % 2:u % 2 + 1],
                                             accum_out=den[:, t % 2, h:h + 1]).then_inc(na_exp, 1)
                    for ph, c, k, before in na_pieces(u, phase == "na"):
                        if k == 0:
                            matmuls_done(act, phase, before, i)
                        high_of_chunk(act, ph, c, i, pieces=[k])
                    if close and close[1] == QUAD - 1:
                        t = close[0]
                        b, done = filled(act, phase, ("tr", t), i)
                        nc.scalar.copy(n_ot[:, bass.ds(q * 2, 2), t * P:(t + 1) * P],
                                       b[:, 0:2 * P].rearrange("p (f n) -> p f n", f=2)).then_inc(done, 1)

            with act.Fori(0, QUADS - 1) as q:
                attention("na", q, q)
            attention("nal", QUADS - 1, 0)
            for t in range(TT):
                drained(act, "nal", ("tr", t))
                nc.scalar.copy(xt[0][:, :, t * P:(t + 1) * P], n_ot[:, :, t * P:(t + 1) * P]).then_inc(na_th, 1)
            for c in range(2, 4):
                part_free(act, "naout", "naout", c - 2)
                high_of_chunk(act, "naout", c)
            norm(4)
            mixture(1)
            embedding_weights(1)
            norm(5)
            embedding(1)
            squares(6, TT - 1)

        @block.tensor
        def _(pe):
            def transposes(phase, key, srcs, i=0, w=P):
                b, full = fill(pe, phase, key, i)
                for c, src in enumerate(srcs):
                    k = src.shape[0]
                    last = nc.tensor.transpose(b[:, c * w:(c + 1) * w], src, ident[0:k, 0:k])
                last.then_inc(full, 1)

            def product(phase, key, lhs, rhs, i=0, m=P):
                b, full = fill(pe, phase, key, i)
                n = rhs[0].shape[-1]
                for c, (x, y) in enumerate(zip(lhs, rhs)):
                    last = nc.tensor.matmul(b[0:m, 0:n], x, y, start=(c == 0), stop=(c == len(lhs) - 1))
                last.then_inc(full, 1)

            def norm(n):
                for t in range(TT):
                    pe.wait_ge(norm_rows[n], t + 1)
                    for c in range(2):
                        transposes(f"norm{n}", ("t", t, c),
                                   [normed(n, t)[:, (4 * c + k) * P:(4 * c + k + 1) * P] for k in range(4)])
                for c in range(2):
                    drained(pe, f"norm{n}", ("t", TT - 1, c))

            def part_products(parts, x, phase, keys, tiles, weights_stay, first, last, i=0, done=None, m=P):
                for n, key in enumerate(keys):
                    if first:
                        b, full = fill(pe, phase, key, i)
                    else:
                        b, full = bank[psum.get(phase, key, i)[0]], bank_full[psum.get(phase, key, i)[0]]
                    for j in range(tiles):
                        for wk, xk in ((0, 0), (1, 0), (0, 1)):
                            w = parts[wk][:, j, :]
                            y = x(xk, n, j)
                            lhs, rhs = (parts[wk][:, j, weights_stay(n)], y) if weights_stay else (y, w)
                            ins = nc.tensor.matmul(b[0:m, 0:rhs.shape[-1]], lhs, rhs,
                                                   start=(first and j == 0 and wk == xk == 0),
                                                   stop=(last and j == tiles - 1 and xk == 1))
                    if last:
                        ins.then_inc(full, 1)
                if not last and done is not None:
                    ins.then_inc(done, 1)

            def chunk_parts(phase, c, i=0, tiles=4, wide=HALF):
                pe.wait_ge(part_l, splits_n.get(phase, (c, pieces_of(phase) - 1), i)[3])
                both = d_parts[:, buffer_of(phase, c), :, 0:tiles * wide]
                return [both[:, k, :].rearrange("p (t f) -> p t f", t=tiles) for k in range(2)]

            pe.wait_ge(ident_set, 2)
            norm(0)
            with pe.Fori(0, RET_HEADS) as h:
                for g, (first, n) in enumerate(GROUPS):
                    nt = n // P

                    def two_chunks(c, keys, x, weights_stay=None):
                        for half in range(2):
                            part_products(chunk_parts("ret", 8 * g + c + half, h), lambda k, a, j: x(k, a, 4 * half + j),
                                          "ret", keys, 4, weights_stay, half == 0, half == 1, h, part_used)

                    two_chunks(0, [("qk", g, f) for f in range(4)], lambda k, a, j: xt[k][:, j, first:first + n],
                               lambda f: slice(f * P, (f + 1) * P))
                    two_chunks(2, [("v", g, t) for t in range(nt)],
                               lambda k, t, j: xt[k][:, j, first + t * P:first + (t + 1) * P])
                    pe.wait_ge(ret_rot, at(2 * g + 2, 4, h))
                    for t in range(nt):
                        product("ret", ("s", g, t), [r_qk[:, 2 + k, t * P:(t + 1) * P] for k in range(2)],
                                [r_qk[:, k, 0:n] for k in range(2)], h)
                    gates = [("g", g, t) for t in range(nt)]
                    part_products(chunk_parts("ret", 8 * g + 4, h),
                                  lambda k, t, j: xt[k][:, j, first + t * P:first + (t + 1) * P],
                                  "ret", gates, 4, None, True, False, h, part_used)
                    for t in range(nt):
                        drained(pe, "ret", ("v", g, t), h)
                        drained(pe, "ret", ("s", g, t), h)
                    for t in range(nt):
                        product("ret", ("o", g, t), [r_s[:, k, t * P:(t + 1) * P] for k in range(nt)],
                                [r_v[:, k, :] for k in range(nt)], h)

                    def gated(t):
                        pe.wait_ge(ret_og, at(first // P + t + 1, TT, h))
                        transposes("ret", ("tr", g, t), [r_og[t][:, k * P:(k + 1) * P] for k in range(4)], h)

                    parts = chunk_parts("ret", 8 * g + 5, h)
                    for t in range(nt):
                        part_products(parts, lambda k, n, j: xt[k][:, 4 + j, first + t * P:first + (t + 1) * P],
                                      "ret", gates[t:t + 1], 4, None, False, True, h)
                        if t:
                            gated(t - 1)
                    for f in range(2):
                        parts = chunk_parts("ret", 8 * g + 6 + f, h)
                        for t in range(nt):
                            if f == 0:
                                drained(pe, "ret", ("tr", g, t), h)
                            part_products(parts, lambda k, a, j: r_ot[k][:, j, t * P:(t + 1) * P], "ret",
                                          [("out", g, t, f)], 4, None, True, True, h)
                            if f == t == 0:
                                gated(nt - 1)

            def mixture(l):
                pe.wait_ge(rw_l, 1)
                for c, (a, w) in enumerate(((0, 512), (512, 256))):
                    part_products([rw_parts[k][:, l, :, :] for k in range(2)], lambda k, n, j: xt[k][:, j, a:a + w],
                                  f"route{l}", [f"lt{c}"], DT, lambda n: slice(0, EXPERTS), True, True, m=EXPERTS)
                for c in range(2):
                    drained(pe, f"route{l}", f"lt{c}")
                b, full = fill(pe, f"route{l}", "logit")
                for t in range(TT):
                    last = nc.tensor.transpose(b[:, t * EXPERTS:(t + 1) * EXPERTS], m_lt[l][:, t * P:(t + 1) * P],
                                               ident[0:EXPERTS, 0:EXPERTS])
                last.then_inc(full, 1)
                pe.wait_ge(moe_aff[l], 1)
                b, full = fill(pe, f"route{l}", "aff")
                for t in range(SEQ_S // P):
                    last = nc.tensor.transpose(b[0:SPREAD, t * P:(t + 1) * P], m_af[l][:, t, :], ident[:, :])
                last.then_inc(full, 1)
                pe.wait_ge(moe_top[l], 1)
                for key, src in (("gate", top_v), ("idx", top_f)):
                    b, full = fill(pe, f"route{l}", key)
                    nc.tensor.transpose(b[0:CAP, 0:SPREAD], src[:, :], ident[0:SPREAD, 0:SPREAD]).then_inc(full, 1)

                def rows(phase, e, n):
                    pe.wait_ge(moe_rows[l], at(16, 16, n))
                    for c in range(2):
                        transposes(phase, f"x{c}", [m_x[:, (4 * c + k) * P:(4 * c + k + 1) * P] for k in range(4)],
                                   e, CAP)

                def product_of_parts(phase, key, lhs, e, n):
                    b, full = fill(pe, phase, key, e)
                    for half in range(2):
                        c = 2 * MOE_USES.index(key) + half
                        pe.wait_ge(moe_wl[l], at(c + 1, 12, n))
                        if key[0] == "y":
                            drained(pe, phase, f"h{half}", e)
                        w = w_parts[:, c % 3, :, :].rearrange("p k (j f) -> p k j f", f=HALF)
                        for j in range(4):
                            for x, k in ((0, 0), (1, 0), (0, 1)):
                                last = nc.tensor.matmul(b[0:CAP, :], lhs[x][:, 4 * half + j, :], w[:, k, j, :],
                                                        start=(c % 2 == 0 and j == 0 and x == k == 0),
                                                        stop=(half == 1 and j == 3 and k == 1))
                        last.then_inc(full if half else moe_wused[l], 1)

                def expert(phase, e, n):
                    for key in MOE_USES[0:4]:
                        product_of_parts(phase, key, m_xt, e, n)
                    for f in range(2):
                        drained(pe, phase, f"u{f}", e)
                        transposes(phase, f"h{f}", [m_hid[:, (4 * f + k) * P:(4 * f + k + 1) * P] for k in range(4)],
                                   e, CAP)
                        if f == 0 and phase[0] == "m":
                            rows(phase, e, n + 1)
                    for key in MOE_USES[4:6]:
                        product_of_parts(phase, key, m_hidt, e, n)

                rows(f"first{l}", 0, 0)
                for c in range(2):
                    drained(pe, f"first{l}", f"x{c}")
                with pe.Fori(0, EXPERTS - 1) as e:
                    expert(f"moe{l}", e, e)
                expert(f"last{l}", 0, EXPERTS - 1)

            def embedding_inputs(l):
                pe.wait_ge(p_in[l], 16 * (ROWS_P + ROWS_S if l == 0 else 2))
                for t in range(TT):
                    transposes(f"inputs{l}", ("pt", t), [e_p[:, t, k * P:(k + 1) * P] for k in range(2)])

            def embedding(l):
                u_parts = [e_u[:, k, :].rearrange("p (t f) -> p t f", t=2) for k in range(2)]
                for f in range(2):
                    keys = [("g", t, f) for t in range(TT)]
                    part_products(chunk_parts(f"ple{l}", 1 + 2 * f), lambda k, t, j: xt[k][:, j, t * P:(t + 1) * P],
                                  f"ple{l}", keys, 4, None, True, False, done=part_used)
                    parts = chunk_parts(f"ple{l}", 2 + 2 * f)
                    for t in range(TT):
                        part_products(parts, lambda k, n, j: xt[k][:, 4 + j, t * P:(t + 1) * P],
                                      f"ple{l}", keys[t:t + 1], 4, None, False, True)
                        if f == 0:
                            drained(pe, f"inputs{l}", ("pt", t))
                        part_products([u[:, :, f * HALF:(f + 1) * HALF] for u in u_parts],
                                      lambda k, n, j: e_pt[k][:, j, t * P:(t + 1) * P],
                                      f"ple{l}", [("u", t, f)], 2, None, True, True)

            norm(1)
            mixture(0)
            embedding_inputs(0)
            norm(2)
            embedding(0)
            norm(3)

            units = na_units()

            def dense(key, halves, phase, parts, i=0):
                kind, n = key
                first, w = (0, SEQ_P) if kind[0] == "n" else (SEQ_P, SEQ_S)
                for half in halves:
                    half_parts = [x[:, 4 * half:4 * half + 4, :] for x in parts]
                    if kind[-1] == "k":
                        part_products(half_parts, lambda k, m, j: xt[k][:, 4 * half + j, first:first + w], phase, [key], 4,
                                      lambda m: slice(n % 2 * P, (n % 2 + 1) * P), half == 0, half == 1, i)
                    else:
                        part_products(half_parts, lambda k, m, j: xt[k][:, 4 * half + j, n * P:(n + 1) * P], phase, [key], 4,
                                      None, half == 0, half == 1, i)

            def chunk_of(key, phase, q, i):
                kind, n = key
                if kind == "qk" and n < 2:
                    pe.wait_ge(part_l, at(splits_n.get("na0", (3, 3), 0)[1], splits_n.get("na", (5, 3), 0)[2], q))
                    return [d_parts[:, buffer_of("na0", 3), k, :].rearrange("p (t f) -> p t f", t=DT) for k in range(2)]
                c = {"qk": 0, "v": 1, "nqk": 2 + n // 2, "nv": 4}[kind]
                return chunk_parts(phase, c, i, DT, 256)

            for k, key in enumerate(NA_NEXT):
                dense(key, (0, 1), "na0", chunk_parts("na0", k // 2, 0, DT, 256))

            def attention(phase, q, i):
                for u in range(NA_STEPS):
                    score, trans, out, close, product_now, _ = na_step(u, phase == "na")
                    if u == 0:
                        prompt_ready(pe, ("nqk", 3), q)
                    if u == 3:
                        prompt_ready(pe, ("nv", 1), q)
                    if u == 2 * QUAD:
                        dense(*product_now, phase, chunk_of(product_now[0], phase, q, i), i)
                        drained(pe, phase, ("qk", 3), i)
                    if score:
                        t, h = score
                        k0, nk, m0 = NA_KEYS[t]
                        b, full = fill(pe, phase, ("s", u), i)
                        a = h % 2 * NA_DH
                        nc.tensor.matmul(b[:, 0:nk * P], ident16[:, :], mask[:, m0:m0 + nk * P], start=True, stop=False)
                        nc.tensor.matmul(b[:, 0:nk * P], n_qk[a:a + NA_DH, h // 2, t * P:(t + 1) * P],
                                         n_qk[a:a + NA_DH, 2 + h // 2, k0 * P:(k0 + nk) * P],
                                         start=False, stop=True).then_inc(full, 1)
                    if trans:
                        v = u - 2
                        pe.wait_ge(na_exp, at(v + 1, len(units), q))
                        transposes(phase, ("pt", v),
                                   [n_p[:, v % 2, k * P:(k + 1) * P] for k in range(NA_KEYS[trans[0]][1])], i)
                    if out:
                        v = u - 3
                        t, h = out
                        k0, nk, _ = NA_KEYS[t]
                        if h == 0:
                            o_bank, o_full = fill(pe, phase, ("o", t), i)
                            if t >= 2:
                                drained(pe, phase, ("v", k0 + nk - 1), i)
                        drained(pe, phase, ("pt", v), i)
                        for k in range(nk):
                            last = nc.tensor.matmul(o_bank[:, h * NA_DH:(h + 1) * NA_DH], n_pt[:, v % 2, k * P:(k + 1) * P],
                                                    n_v[:, k0 + k, h * NA_DH:(h + 1) * NA_DH],
                                                    start=(k == 0), stop=(k == nk - 1))
                        if h == QUAD - 1:
                            last.then_inc(o_full, 1)
                    if close and close[1] == QUAD - 1:
                        t = close[0]
                        drained(pe, phase, ("o", t), i)
                        transposes(phase, ("tr", t), [n_o[:, t % 2, k * P:(k + 1) * P] for k in range(2)], i)
                    if product_now and u != 2 * QUAD:
                        dense(*product_now, phase, chunk_of(product_now[0], phase, q, i), i)

            with pe.Fori(0, QUADS - 1) as q:
                attention("na", q, q)
            attention("nal", QUADS - 1, 0)
            for c in range(4):
                f, half = c // 2, c % 2
                parts = chunk_parts("naout", c)
                for t in range(TT):
                    if c == 0:
                        pe.wait_ge(na_tl, t + 1)
                    part_products(parts, lambda k, n, j: xt[k][:, 4 * half + j, t * P:(t + 1) * P], "naout",
                                  [("out", t, f)], 4, None, half == 0, half == 1,
                                  done=part_used if t == TT - 1 else None)
            norm(4)
            mixture(1)
            embedding_inputs(1)
            norm(5)
            embedding(1)

        @block.vector
        def _(dve):
            chain = Chain(dve, dve_step)
            v = nc.vector

            def scaled(n, t):
                if t == 0 and n == 0:
                    dve.wait_ge(first_gain_in, 16)
                elif t == 0:
                    dve.wait_ge(gain_in[n % 2], 16 * ((n + 1) // 2))
                dve.wait_ge(norm_rs[n], t + 1)
                v.scalar_tensor_tensor(out=normed(n, t), in0=resid[:, t, :], scalar=rstd[:, t:t + 1],
                                       in1=gain[:, n % 2, :], op0=ALU.mult, op1=ALU.mult)\
                    .then_inc(norm_rows[n], 1)

            def norm(n):
                for t in range(TT + 1):
                    if t < TT:
                        scaled(n, t)
                    for c in range(2 if t else 0):
                        b, done = filled(dve, f"norm{n}", ("t", t - 1, c))
                        dve.wait_ge(norm_hi[n], 2 * (t - 1) + c + 1)
                        at_tile = (slice(None), slice(4 * c, 4 * c + 4), slice((t - 1) * P, t * P))
                        v.tensor_tensor(xt[1][at_tile], b[:, :].rearrange("p (f n) -> p f n", f=4),
                                        xt[0][at_tile].bitcast(F32), ALU.subtract).then_inc(done, 1)

            dve.wait_ge(decay_in, 16)
            x, ax, y, s, s2, p = (lgt[:, k, :] for k in range(6))
            chain.link(v.tensor_scalar(ax, x, -1.0, None, ALU.mult))
            v.tensor_tensor(ax, ax, x, ALU.max).then_inc(decay_abs, 1)
            dve.wait_ge(decay_exp, 1)
            chain.link(v.tensor_scalar(s2, y, 2.0, None, ALU.add))
            chain.link(v.reciprocal(p, s2))
            chain.link(v.tensor_tensor(s, p, y, ALU.mult))
            chain.link(v.tensor_tensor(s2, s, s, ALU.mult))
            chain.link(v.tensor_scalar(p, s2, 1.0 / 19, None, ALU.mult))
            for k in range(17, 1, -2):
                chain.link(v.scalar_tensor_tensor(out=p, in0=p, scalar=1.0 / k, in1=s2, op0=ALU.add, op1=ALU.mult))
            chain.link(v.scalar_tensor_tensor(out=p, in0=p, scalar=1.0, in1=s, op0=ALU.add, op1=ALU.mult))
            chain.link(v.tensor_scalar(s, x, 0.0, None, ALU.min))
            chain.link(v.scalar_tensor_tensor(out=lg[:], in0=p, scalar=-2.0, in1=s, op0=ALU.mult, op1=ALU.add))
            norm(0)
            with dve.Fori(0, RET_HEADS) as h:
                chain.enter(h, 2 + 2 * 6 + TT)
                for g, (first, n) in enumerate(GROUPS):
                    nt = n // P

                    def splits(a, z):
                        for c in range(a, z):
                            low_of_chunk(dve, "ret", 8 * g + c, h)

                    splits(0 if g == 0 else 1, 4)
                    if g == 0:
                        dve.wait_ge(const_in, 5 * 16)
                        flat = r_tmp[:, :, :].rearrange("p f n -> p (f n)")
                        a, b2 = flat[:, 0:STRIP], flat[:, STRIP:2 * STRIP]
                        chain.link(v.tensor_scalar(a, r_diff[:, :], 0.0, lg[:, bass.ds(h, 1)], ALU.max, ALU.mult))
                        chain.link(v.tensor_scalar(b2, r_diff[:, :], 0.0, lg[:, bass.ds(h + RET_HEADS, 1)],
                                                   ALU.min, ALU.mult))
                        v.tensor_tensor(r_strip[:, :], a, b2, ALU.subtract).then_inc(strip_arg, 1)
                        dve.wait_ge(strip_arg, h + 1)
                    for j in range(2):
                        t0, t1, t2, t3 = (r_tmp[:, k, 0:n] for k in range(4))
                        b, done = filled(dve, "ret", ("qk", g, 2 * j), h)
                        chain.link(v.tensor_tensor(t0, b[:, 0:n], cos_t[:, 0:n], ALU.mult))
                        v.tensor_tensor(t2, b[:, 0:n], sin_t[:, 0:n], ALU.mult).then_inc(done, 1)
                        b, done = filled(dve, "ret", ("qk", g, 2 * j + 1), h)
                        chain.link(v.tensor_tensor(t1, b[:, 0:n], sin_t[:, 0:n], ALU.mult))
                        v.tensor_tensor(t3, b[:, 0:n], cos_t[:, 0:n], ALU.mult).then_inc(done, 1)
                        chain.link(v.tensor_tensor(r_qk[:, 2 * j, 0:n], t0, t1, ALU.subtract))
                        drained(dve, "ret", ("qk", g, 2 * j + 1), h)
                        v.tensor_tensor(r_qk[:, 2 * j + 1, 0:n], t2, t3, ALU.add).then_inc(ret_rot, 1)
                        dve.wait_ge(ret_rot, at(2 * g + j + 1, 4, h))
                    splits(4, 6)
                    if g == 0:
                        dve.wait_ge(strip_set, h + 1)
                    for t in range(nt):
                        b, done = filled(dve, "ret", ("s", g, t), h)
                        v.scalar_tensor_tensor(out=r_s[:, t, 0:n], in0=b[:, 0:n], scalar=RET_DK ** -0.5,
                                               in1=r_strip[:, STRIP0 - t * P:STRIP0 - t * P + n],
                                               op0=ALU.mult, op1=ALU.mult).then_inc(done, 1)
                    dve.wait_ge(gn_in, 16)
                    for t in range(nt):
                        k = first // P + t
                        b, done = filled(dve, "ret", ("o", g, t), h)
                        chain.link(v.bn_stats(stats[:, k, :], b[:, :]))
                        hold(dve)
                        v.bn_aggr(mv[:, k, :], stats[:, k, :]).then_inc(ret_var, 1)
                        dve.wait_ge(ret_var, at(k + 1, TT, h))
                        v.scalar_tensor_tensor(out=r_og[t][:, :], in0=b[:, :], scalar=mv[:, k, 0:1],
                                               in1=r_gn[:, bass.ds(h * 512, 512)], op0=ALU.subtract, op1=ALU.mult)\
                            .then_inc(done, 1)
                        if t == 0:
                            splits(6, 7)

                    def transposed(t):
                        b, done = filled(dve, "ret", ("tr", g, t), h)
                        dve.wait_ge(ret_th, at(first // P + t + 1, TT, h))
                        s_t = slice(t * P, (t + 1) * P)
                        v.tensor_tensor(r_ot[1][:, :, s_t], b[:, :].rearrange("p (f n) -> p f n", f=4),
                                        r_ot[0][:, :, s_t].bitcast(F32), ALU.subtract).then_inc(done, 1)

                    for t in range(nt):
                        k = first // P + t
                        drained(dve, "ret", ("o", g, t), h)
                        drained(dve, "ret", ("g", g, t), h)
                        dve.wait_ge(ret_rstd, at(k + 1, TT, h))
                        v.scalar_tensor_tensor(out=r_og[t][:, :], in0=r_og[t][:, :], scalar=mvr[:, k:k + 1],
                                               in1=r_tmp[:, t, :], op0=ALU.mult, op1=ALU.mult).then_inc(ret_og, 1)
                        if t:
                            transposed(t - 1)
                    transposed(nt - 1)
                    splits(7, 8)
                    for f in range(2):
                        for t in range(nt):
                            b, done = filled(dve, "ret", ("out", g, t, f), h)
                            r = resid[:, first // P + t, f * HALF:(f + 1) * HALF]
                            v.tensor_tensor(r, r, b[:, :], ALU.add).then_inc(done, 1)
                        if g == f == 0:
                            splits(8, 9)
                chain.leave(RET_HEADS)
            dve.wait_ge(rw_h, 1)
            v.tensor_tensor(rw_parts[1][:].rearrange("p l t e -> p (l t e)"), rw[:].rearrange("p l t e -> p (l t e)"),
                            rw_parts[0][:].rearrange("p l t e -> p (l t e)").bitcast(F32), ALU.subtract).then_inc(rw_l, 1)

            def mixture(l, order):
                smax, ssum, srec = rsm[:, 0, 0:TT], rsm[:, 1, 0:TT], rsm[:, 2, 0:TT]

                def wide(x):
                    return x.rearrange("p (t a) -> p t a", a=1).broadcast_to([P, x.shape[1], EXPERTS])

                b, done = filled(dve, f"route{l}", "logit")
                logits = b[:, 0:TT * EXPERTS].rearrange("p (t e) -> p t e", t=TT)
                chain.link(v.tensor_reduce(smax, logits, AX_X, ALU.max))
                v.tensor_tensor(m_lg[l][:], logits, wide(smax), ALU.subtract).then_inc(done, 1)
                dve.wait_ge(moe_exp[l], 1)
                chain.link(v.tensor_reduce(ssum, m_lg[l][:], AX_X, ALU.add))
                chain.link(v.reciprocal(srec, ssum))
                chain.link(v.memset(m_af[l][:], -1.0))
                chain.link(v.tensor_tensor(m_af[l][:, 0:2, 0:EXPERTS], m_lg[l][:, 0:2, :], wide(srec[:, 0:2]), ALU.mult))
                v.tensor_tensor(m_af[l][:, :, SAMPLE0:SPREAD], m_lg[l][:, 2:TT, :], wide(srec[:, 2:TT]), ALU.mult)\
                    .then_inc(moe_aff[l], 1)
                b, done = filled(dve, f"route{l}", "aff")
                if order:
                    chain.link(v.tensor_copy(m_at[l][:, :], b[0:SPREAD, :]))
                    for g, (e0, n) in enumerate(((0, SEQ_P), (SAMPLE0, SEQ_S))):
                        rows, cols = ((ROWS_P, COLS_P), (ROWS_S, COLS_S))[g]
                        dst = m_at[l][e0:e0 + EXPERTS, 0:n].rearrange("e (r t c) -> e t r c", r=rows, c=cols)
                        src = b[e0:e0 + EXPERTS, 0:n].rearrange("e (t r c) -> e t r c", r=rows, c=cols)
                        for t in range(n // P):
                            last = v.tensor_copy(dst[:, t], src[:, t])
                else:
                    last = v.tensor_copy(m_at[l][:, :], b[0:SPREAD, :])
                last.then_inc(done, 1)
                drained(dve, f"route{l}", "aff")
                a = m_at[l][:, :]
                for c in range(0, CAP_S, 8):
                    chain.link(v.max(out=top_v[:, c:c + 8], in_=a))
                    chain.link(v.max_index(out=top_i[:, c:c + 8], in_max=top_v[:, c:c + 8], in_values=a))
                    if c + 8 < CAP_S:
                        chain.link(v.match_replace(out=a, in_to_replace=top_v[:, c:c + 8], in_values=a, imm_value=-1.0))
                v.tensor_copy(top_v[:, CAP_S:CAP], top_v[:, 0:CAP_P])
                chain.link(v.tensor_copy(top_f[:, 0:CAP_S], top_i[:, 0:CAP_S]))
                chain.link(v.tensor_copy(top_f[:, CAP_S:CAP], top_f[:, 0:CAP_P]))
                v.tensor_scalar(top_f[SAMPLE0:SPREAD, 0:CAP_S], top_f[SAMPLE0:SPREAD, 0:CAP_S], float(SEQ_P), None, ALU.add)\
                    .then_inc(moe_top[l], 1)
                for key, dst in (("gate", gate_t), ("idx", idx_t)):
                    b, done = filled(dve, f"route{l}", key)
                    v.tensor_copy(dst[0:CAP_S, :], b[0:CAP_S, SAMPLE0:SPREAD])
                    v.tensor_copy(dst[CAP_S:CAP, :], b[CAP_S:CAP, 0:EXPERTS]).then_inc(done, 1)

                def low(phase, key, i, parts, c, count):
                    b, done = filled(dve, phase, key, i)
                    dve.wait_ge(moe_th[l], count)
                    k = slice(4 * c, 4 * c + 4)
                    v.tensor_tensor(parts[1][:, k, :], b[:, 0:4 * CAP].rearrange("p (f n) -> p f n", f=4),
                                    parts[0][:, k, :].bitcast(F32), ALU.subtract).then_inc(done, 1)

                def splits(a, z, n):
                    for c in range(a, z):
                        dve.wait_ge(moe_wh[l], at(c + 1, 12, n))
                        v.tensor_tensor(w_parts[:, c % 3, 1, :], wt[:, c // 2, c % 2 * 2048:c % 2 * 2048 + 2048],
                                        w_parts[:, c % 3, 0, :].bitcast(F32), ALU.subtract).then_inc(moe_wl[l], 1)

                def expert(phase, e, n):
                    more = phase[0] == "m"

                    def hidden(f):
                        drained(dve, phase, f"g{f}", e)
                        b, done = filled(dve, phase, f"u{f}", e)
                        v.tensor_tensor(m_hid[:, f * HALF:(f + 1) * HALF], m_silu[:, f, :], b[0:CAP, :], ALU.mult)\
                            .then_inc(done, 1)

                    def output(f):
                        b, done = filled(dve, phase, f"y{f}", e)
                        if f == 0:
                            dve.wait_ge(moe_y_free[l], n + 1)
                        v.tensor_scalar(m_y[:, f * HALF:(f + 1) * HALF], b[0:CAP, :], gate_t[:, bass.ds(n, 1)], None,
                                        ALU.mult).then_inc(done, 1)

                    splits(3, 6, n)
                    hidden(0)
                    splits(6, 10, n)
                    hidden(1)
                    low(phase, "h0", e, m_hidt, 0, at(3, 4, n))
                    if more:
                        for c in range(2):
                            low(phase, f"x{c}", e, m_xt, c, at(4 + c, 4, n))
                    low(phase, "h1", e, m_hidt, 1, at(6 if more else 4, 4, n))
                    splits(10, 12, n)
                    if more:
                        splits(0, 1, n + 1)
                    output(0)
                    if more:
                        splits(1, 3, n + 1)
                    output(1)

                splits(0, 3, 0)
                for c in range(2):
                    low(f"first{l}", f"x{c}", 0, m_xt, c, c + 1)
                with dve.Fori(0, EXPERTS - 1) as e:
                    expert(f"moe{l}", e, e)
                expert(f"last{l}", 0, EXPERTS - 1)

            def embedding_weights(l):
                low_of_chunk(dve, f"ple{l}", 0, dst=(e_u[:, 0, :], e_u[:, 1, :]))
                low_of_chunk(dve, f"ple{l}", 1)
                for t in range(TT):
                    b, done = filled(dve, f"inputs{l}", ("pt", t))
                    dve.wait_ge(ple_th[l], t + 1)
                    s_t = slice(t * P, (t + 1) * P)
                    v.tensor_tensor(e_pt[1][:, :, s_t], b[:, 0:2 * P].rearrange("p (f n) -> p f n", f=2),
                                    e_pt[0][:, :, s_t].bitcast(F32), ALU.subtract).then_inc(done, 1)

            def embedding(l):
                low_of_chunk(dve, f"ple{l}", 2)
                for f in range(2):
                    low_of_chunk(dve, f"ple{l}", 3 + f)
                    for t in range(TT):
                        u = TT * f + t
                        drained(dve, f"ple{l}", ("g", t, f))
                        if u >= 2:
                            dve.wait_ge(ple_add[l], u - 1)
                        b, done = filled(dve, f"ple{l}", ("u", t, f))
                        v.tensor_tensor(e_prod[:, t % 2, :], e_sig[:, t % 2, :], b[:, :], ALU.mult).then_inc(done, 1)
                        drained(dve, f"ple{l}", ("u", t, f))
                        r = resid[:, t, f * HALF:(f + 1) * HALF]
                        v.tensor_tensor(r, r, e_prod[:, t % 2, :], ALU.add).then_inc(ple_add[l], 1)
                        if l == f == 1 and t:
                            scaled(6, t - 1)

            norm(1)
            mixture(0, 0)
            embedding_weights(0)
            norm(2)
            embedding(0)
            for c in range(2):
                low_of_chunk(dve, "na0", c)
            norm(3)

            units = na_units()

            def product_out(phase, key, i=0):
                kind, k = key
                a, w = (0, SEQ_P) if kind[0] == "n" else (SEQ_P, SEQ_S)
                if kind[-1] == "k" and k >= 2:
                    b, done = filled(dve, phase, key, i)
                    v.tensor_copy(n_qk[:, k, a:a + w], b[:, 0:w]).then_inc(done, 1)
                elif kind[-1] == "v" and k % 2 == 1:
                    b, done = filled(dve, phase, key, i)
                    v.tensor_copy(n_v[:, k, :], b[:, 0:256]).then_inc(done, 1)

            low_of_chunk(dve, "na0", 2)
            for f in range(2, 4):
                product_out("na0", ("nqk", f))
            low_of_chunk(dve, "na0", 3)
            product_out("na0", ("nv", 1))

            def attention(phase, q, i):
                for u in range(NA_STEPS):
                    score, trans, _, close, _, ready = na_step(u, phase == "na")
                    if ready:
                        product_out(phase, ready, i)
                    if close and close[1] == QUAD - 1:
                        t = close[0]
                        b, done = filled(dve, phase, ("o", t), i)
                        chain.link(v.reciprocal(rden[:], den[:, t % 2, :]))
                        v.tensor_tensor(n_o[:, t % 2, :].rearrange("p (h d) -> p h d", h=QUAD),
                                        b[:, 0:256].rearrange("p (h d) -> p h d", h=QUAD),
                                        rden[:].rearrange("p (h a) -> p h a", a=1).broadcast_to([P, QUAD, NA_DH]),
                                        ALU.mult).then_inc(done, 1)
                    for ph, c, k, _ in na_pieces(u - 1, phase == "na"):
                        low_of_chunk(dve, ph, c, i, pieces=[k])
                    if score:
                        t, h = score
                        g = int(t >= 2)
                        if h == 0 and t in (0, 2):
                            n_dmas = (ROWS_P, ROWS_S)[g]
                            dve.wait_ge(na_bias[g], at(16 * n_dmas, 16 * n_dmas, q))
                        k0, nk, _ = NA_KEYS[t]
                        rows, cols, wide_, lo = ((ROWS_P, COLS_P, WIDE_P, 8 * WIDE_S),
                                                 (ROWS_S, COLS_S, WIDE_S, 0))[g]
                        bb = bias[:, h, lo:lo + rows * wide_].rearrange("p (r k c) -> p k r c", r=rows, c=cols)
                        rel = k0 - t + 1
                        b, done = filled(dve, phase, ("s", u), i)
                        if u >= 2:
                            dve.wait_ge(na_exp, at(u - 1, len(units), q))
                        scored = n_s[:, u % 2, 0:nk * P].rearrange("p (k r c) -> p k r c", k=nk, c=cols)
                        scores = b[:, 0:nk * P].rearrange("p (k r c) -> p k r c", k=nk, c=cols)
                        v.tensor_tensor(scored, scores, bb[:, rel:rel + nk], ALU.add).then_inc(done, 1)
                        drained(dve, phase, ("s", u), i)
                        chain.link(v.tensor_reduce(mx[:, u % 2:u % 2 + 1], n_s[:, u % 2, 0:nk * P], AX_X, ALU.max))
                        v.tensor_scalar(nmx[:, u % 2:u % 2 + 1], mx[:, u % 2:u % 2 + 1], -1.0, None, ALU.mult)\
                            .then_inc(na_max, 1)
                    if trans and u % 2 == 1:
                        w = NA_KEYS[trans[0]][1] * P
                        b, done = filled(dve, phase, ("pt", u - 2), i)
                        v.tensor_copy(n_pt[:, 1, 0:w], b[:, 0:w]).then_inc(done, 1)

            with dve.Fori(0, QUADS - 1) as q:
                chain.enter(q, len(units) + TT)
                attention("na", q, q)
                chain.leave(QUADS - 1)
            attention("nal", QUADS - 1, 0)
            for t in range(TT):
                dve.wait_ge(na_th, t + 1)
                s_t = slice(t * P, (t + 1) * P)
                v.tensor_tensor(xt[1][:, :, s_t], n_ot[:, :, s_t], xt[0][:, :, s_t].bitcast(F32), ALU.subtract)\
                    .then_inc(na_tl, 1)
            for f in range(2):
                if f == 0:
                    for c in range(2, 4):
                        low_of_chunk(dve, "naout", c)
                for t in range(TT):
                    b, done = filled(dve, "naout", ("out", t, f))
                    r = resid[:, t, f * HALF:(f + 1) * HALF]
                    v.tensor_tensor(r, r, b[:, :], ALU.add).then_inc(done, 1)
            norm(4)
            mixture(1, 1)
            embedding_weights(1)
            norm(5)
            embedding(1)
            scaled(6, TT - 1)


def shape_constants():
    half = RET_DK // 2
    inv = np.float32(10000.0) ** (-np.arange(0, RET_DK, 2, dtype=np.float32) / np.float32(RET_DK))
    ang = inv.astype(np.float32)[:, None] * np.arange(SEQ_S, dtype=np.float32)[None, :]
    diff = np.arange(STRIP, dtype=np.float32)[None, :] - STRIP0 - np.arange(P, dtype=np.float32)[:, None]

    def window(rows, cols, tile, first, n):
        q = tile * cols + np.tile(np.arange(cols), rows)
        k = np.concatenate([(first + j) * cols + np.tile(np.arange(cols), rows) for j in range(n)])
        start = np.clip(q - NA_WIN // 2, 0, GRID_W - NA_WIN)
        ok = (k[None, :] >= start[:, None]) & (k[None, :] < start[:, None] + NA_WIN)
        return np.where(ok, 0.0, MASKED)

    mask = np.concatenate([window(ROWS_P, COLS_P, 0, 0, 2), window(ROWS_P, COLS_P, 1, 0, 2),
                           window(ROWS_S, COLS_S, 0, 0, 2), window(ROWS_S, COLS_S, 1, 0, 3),
                           window(ROWS_S, COLS_S, 3, 2, 2)], axis=1)
    assert mask.shape[1] == MASK_W and half == P
    mask_bits = (np.ascontiguousarray(mask, dtype=np.float32).view(np.uint32) >> 16).astype(np.uint16)
    return {"rope_cos": np.cos(ang).astype(np.float32), "rope_sin": np.sin(ang).astype(np.float32),
            "row_minus_col": diff.astype(np.float32), "col_mask": mask_bits}


_INS = ["x_prompt", "x_sample", "p_prompt", "p_sample", "ret_w_in", "ret_decay_logit", "ret_gn_w", "ret_w_out",
        "na_w_in", "na_rpb", "na_w_out", "mix_norm", "ffn_norm", "ple_norm", "router_w", "exp_w_gate", "exp_w_up",
        "exp_w_down", "ple_w_up", "ple_w_gate", "final_norm"]


def kernel(**inputs):
    import concourse.bacc as bacc
    from concourse.bass_utils import run_bass_kernel_spmd

    nc = bacc.Bacc("TRN2", target_bir_lowering=False, num_devices=1)
    arrays, args = {}, []
    given = {name: np.ascontiguousarray(inputs[name]) for name in _INS}
    given["na_rpb"] = np.pad(given["na_rpb"].reshape(-1), RPB_PAD)
    given.update(shape_constants())
    for name, a in given.items():
        arrays[f"in_{name}"] = a
        args.append(nc.dram_tensor(f"in_{name}", a.shape, mybir.dt.from_np(a.dtype), kind="ExternalInput").ap())
    for name, rows in (("y_prompt", SEQ_P), ("y_sample", SEQ_S)):
        args.append(nc.dram_tensor(name, (1, rows, D), F32, kind="ExternalOutput").ap())
    build(nc, *args)
    r = run_bass_kernel_spmd(nc, [arrays], core_ids=[0])
    return r.results[0]["y_prompt"], r.results[0]["y_sample"]
```
